# Optimizing a Trainium2 kernel written in Bass

```python
import math
import jax, jax.numpy as jnp
from jax import lax
import numpy as np

D_MODEL = 1024
BATCH = 1
SEQ = 512
DEPTH = 2

N_META = 16
D_MIX = D_MODEL
ATTN_WIDTH = D_MIX // 2
CONV_CH = D_MIX - ATTN_WIDTH
N_ATTN_HEADS = 4
V_HEAD_DIM = ATTN_WIDTH // N_ATTN_HEADS
HEAD_DIM = V_HEAD_DIM // 2
QK_WIDTH = N_ATTN_HEADS * 2 * HEAD_DIM
IN_WIDTH = 2 * QK_WIDTH + ATTN_WIDTH + 2 * CONV_CH
CONV_WIDTH = 31
D_FF = -(-8 * D_MODEL // (3 * 256)) * 256
ROPE_THETA = 10000.0
Q_BLOCK = 128
NORM_EPS = 1e-5


def rmsnorm(x, g):
    x32 = x.astype(jnp.float32)
    y = x32 * lax.rsqrt(jnp.mean(x32 * x32, axis=-1, keepdims=True) + NORM_EPS)
    return (y * g.astype(jnp.float32)).astype(x.dtype)

def layer_norm(x, g, b):
    x32 = x.astype(jnp.float32)
    mu = jnp.mean(x32, axis=-1, keepdims=True)
    xc = x32 - mu
    y = xc * lax.rsqrt(jnp.mean(xc * xc, axis=-1, keepdims=True) + NORM_EPS)
    return (y * g.astype(jnp.float32) + b.astype(jnp.float32)).astype(x.dtype)

def rope_tables(length, dtype):
    pos = jnp.arange(length, dtype=jnp.float32)
    inv = ROPE_THETA ** (-jnp.arange(0, HEAD_DIM, 2, dtype=jnp.float32) / HEAD_DIM)
    ang = pos[:, None] * inv[None, :]
    ang = jnp.concatenate([ang, ang], axis=-1)
    return jnp.cos(ang).astype(dtype), jnp.sin(ang).astype(dtype)

def apply_rope(t, cos, sin):
    c = cos[None, :, None, None, :]
    s = sin[None, :, None, None, :]
    t1, t2 = jnp.split(t, 2, axis=-1)
    return t * c + jnp.concatenate([-t2, t1], axis=-1) * s

def diff_attention(q, k, v, lam, sub_g, lam_init):
    B, L = q.shape[0], q.shape[1]
    n_blk = -(-L // Q_BLOCK)
    L_pad = n_blk * Q_BLOCK
    pad = L_pad - L
    q = jnp.pad(q, ((0, 0), (0, pad), (0, 0), (0, 0), (0, 0)))
    k = jnp.pad(k, ((0, 0), (0, pad), (0, 0), (0, 0), (0, 0)))
    v = jnp.pad(v, ((0, 0), (0, pad), (0, 0), (0, 0)))
    qb = q.reshape(B, n_blk, Q_BLOCK, N_ATTN_HEADS, 2, HEAD_DIM).transpose(1, 0, 2, 3, 4, 5)
    k_pos = jnp.arange(L_pad)
    scale = HEAD_DIM ** -0.5

    def one_block(args):
        q_blk, start = args
        s = jnp.einsum('bqhcd,bkhcd->bhcqk', q_blk, k).astype(jnp.float32) * scale
        q_pos = start + jnp.arange(Q_BLOCK)
        mask = k_pos[None, :] <= q_pos[:, None]
        s = jnp.where(mask, s, -jnp.inf)
        p = jax.nn.softmax(s, axis=-1)
        a = p[:, :, 0] - lam * p[:, :, 1]
        return jnp.einsum('bhqk,bkhe->bqhe', a.astype(v.dtype), v)

    starts = jnp.arange(n_blk) * Q_BLOCK
    o = lax.map(one_block, (qb, starts))
    o = o.transpose(1, 0, 2, 3, 4).reshape(B, L_pad, N_ATTN_HEADS, V_HEAD_DIM)[:, :L]
    o = rmsnorm(o, sub_g) * (1.0 - lam_init)
    return o.reshape(B, L, ATTN_WIDTH)

def conformer_conv(u, conv_w, conv_b, ln_g, ln_b):
    a, gate = jnp.split(u, 2, axis=-1)
    z = a * jax.nn.sigmoid(gate)
    z = lax.conv_general_dilated(
        z, conv_w[:, None, :], window_strides=(1,), padding=((CONV_WIDTH - 1, 0),),
        dimension_numbers=('NWC', 'WIO', 'NWC'), feature_group_count=CONV_CH)
    z = z + conv_b
    z = layer_norm(z, ln_g, ln_b)
    return jax.nn.silu(z)

def first_inputs(seed: int = 0) -> dict:
    key = jax.random.key(seed)
    ks = jax.random.split(key, 20)
    f = jnp.float32
    nrm = lambda k, shape, s: jax.random.normal(k, shape, f) * s
    return {
        "x": nrm(ks[0], (BATCH, SEQ, D_MODEL), 1.0),
        "meta_tokens": nrm(ks[1], (N_META, D_MODEL), 1.0),
        "norm1_g": 1.0 + nrm(ks[2], (DEPTH, D_MODEL), 0.02),
        "w_in": nrm(ks[3], (DEPTH, D_MODEL, IN_WIDTH), D_MODEL ** -0.5),
        "b_glu": nrm(ks[4], (DEPTH, 2 * CONV_CH), 0.02),
        "conv_w": nrm(ks[5], (DEPTH, CONV_WIDTH, CONV_CH), CONV_WIDTH ** -0.5),
        "conv_b": nrm(ks[6], (DEPTH, CONV_CH), 0.02),
        "conv_ln_g": 1.0 + nrm(ks[7], (DEPTH, CONV_CH), 0.02),
        "conv_ln_b": nrm(ks[8], (DEPTH, CONV_CH), 0.02),
        "lam_q1": nrm(ks[9], (DEPTH, HEAD_DIM), 0.1),
        "lam_k1": nrm(ks[10], (DEPTH, HEAD_DIM), 0.1),
        "lam_q2": nrm(ks[11], (DEPTH, HEAD_DIM), 0.1),
        "lam_k2": nrm(ks[12], (DEPTH, HEAD_DIM), 0.1),
        "subln_g": 1.0 + nrm(ks[13], (DEPTH, V_HEAD_DIM), 0.02),
        "w_out": nrm(ks[14], (DEPTH, D_MIX, D_MODEL), D_MIX ** -0.5),
        "norm2_g": 1.0 + nrm(ks[15], (DEPTH, D_MODEL), 0.02),
        "w_gate_up": nrm(ks[16], (DEPTH, D_MODEL, 2 * D_FF), D_MODEL ** -0.5),
        "w_down": nrm(ks[17], (DEPTH, D_FF, D_MODEL), D_FF ** -0.5),
        "final_g": 1.0 + nrm(ks[18], (D_MODEL,), 0.02),
    }

def first_block(x, meta_tokens, norm1_g, w_in, b_glu, conv_w, conv_b, conv_ln_g, conv_ln_b,
              lam_q1, lam_k1, lam_q2, lam_k2, subln_g, w_out, norm2_g, w_gate_up, w_down,
              final_g):
    B, S, D = x.shape
    meta = jnp.broadcast_to(meta_tokens[None].astype(x.dtype), (B, N_META, D))
    h = jnp.concatenate([meta, x], axis=1)
    L = S + N_META
    cos, sin = rope_tables(L, x.dtype)
    for l in range(DEPTH):
        lam_init = 0.8 - 0.6 * math.exp(-0.3 * l)
        hn = rmsnorm(h, norm1_g[l])
        proj = hn @ w_in[l]
        q, k, v, u = jnp.split(proj, [QK_WIDTH, 2 * QK_WIDTH, 2 * QK_WIDTH + ATTN_WIDTH], axis=-1)
        q = apply_rope(q.reshape(B, L, N_ATTN_HEADS, 2, HEAD_DIM), cos, sin)
        k = apply_rope(k.reshape(B, L, N_ATTN_HEADS, 2, HEAD_DIM), cos, sin)
        v = v.reshape(B, L, N_ATTN_HEADS, V_HEAD_DIM)
        lam = (jnp.exp(jnp.sum(lam_q1[l].astype(jnp.float32) * lam_k1[l].astype(jnp.float32)))
               - jnp.exp(jnp.sum(lam_q2[l].astype(jnp.float32) * lam_k2[l].astype(jnp.float32)))
               + lam_init)
        attn_out = diff_attention(q, k, v, lam, subln_g[l], lam_init)
        conv_out = conformer_conv(u + b_glu[l], conv_w[l], conv_b[l],
                                  conv_ln_g[l], conv_ln_b[l])
        h = h + jnp.concatenate([attn_out, conv_out], axis=-1) @ w_out[l]
        hn = rmsnorm(h, norm2_g[l])
        gate, up = jnp.split(hn @ w_gate_up[l], 2, axis=-1)
        h = h + (jax.nn.silu(gate) * up) @ w_down[l]
    h = rmsnorm(h, final_g)
    return h[:, N_META:]


DEPTH_2 = 1

DN_HEADS = 8
DN_HEAD_DIM = 128
DN_W = DN_HEADS * DN_HEAD_DIM
DN_CONV = 4
DN_CHUNK = 64
NSA_HEADS = 16
NSA_GROUPS = 4
NSA_REP = NSA_HEADS // NSA_GROUPS
NSA_HEAD_DIM = 64
NSA_W = NSA_HEADS * NSA_HEAD_DIM
NSA_KV_W = NSA_GROUPS * NSA_HEAD_DIM
CMP_LEN = 32
CMP_STRIDE = 16
CMP_HIDDEN = 2 * NSA_HEAD_DIM
SLC_LEN = 64
SLC_TOPK = 8
WINDOW = 256
ATT_QBLK = 128
SLC_QBLK = 64
D_FF_2 = 4 * D_MODEL
IN_WIDTH_2 = 4 * DN_W + 2 * DN_HEADS + NSA_W + 6 * NSA_KV_W + 3 * NSA_HEADS + 2 * D_MODEL
EPS = 1e-6
NEG = -1e30
FORCE = 1e9


def _in_split_points():
    sizes = [3 * DN_W, DN_W, DN_HEADS, DN_HEADS,
             NSA_W, NSA_KV_W, NSA_KV_W, NSA_KV_W, NSA_KV_W, NSA_KV_W, NSA_KV_W, 3 * NSA_HEADS,
             D_MODEL, D_MODEL]
    return [int(v) for v in np.cumsum(sizes)[:-1]]

def rmsnorm_2(x, gain):
    xf = x.astype(jnp.float32)
    y = xf * lax.rsqrt(jnp.mean(xf * xf, axis=-1, keepdims=True) + EPS)
    return (y * gain.astype(jnp.float32)).astype(x.dtype)

def l2norm(x):
    xf = x.astype(jnp.float32)
    return (xf * lax.rsqrt(jnp.sum(xf * xf, axis=-1, keepdims=True) + EPS)).astype(x.dtype)

def alibi_slopes(n_heads):
    return jnp.asarray(2.0 ** (-8.0 * np.arange(1, n_heads + 1) / n_heads), jnp.float32)

def causal_depthwise_conv(x, w):
    k, c = w.shape
    return lax.conv_general_dilated(x, w[:, None, :].astype(x.dtype), window_strides=(1,),
                                    padding=[(k - 1, 0)], dimension_numbers=('NWC', 'WIO', 'NWC'),
                                    feature_group_count=c)

def chunk_gated_delta_rule(q, k, v, g, beta):
    B, S, H, dk = q.shape
    dv = v.shape[-1]
    C = DN_CHUNK
    N = S // C
    f32 = jnp.float32

    def chunks(t):
        t = t.astype(f32).reshape((B, N, C, H) + t.shape[3:])
        return jnp.moveaxis(t, (1, 3), (0, 2))

    q = chunks(q) * (dk ** -0.5)
    k = chunks(k)
    v = chunks(v)
    beta = chunks(beta)
    gc = jnp.cumsum(chunks(g), axis=-1)
    kb = k * beta[..., None]
    vb = v * beta[..., None]
    causal = jnp.tril(jnp.ones((C, C), bool))
    strict = jnp.tril(jnp.ones((C, C), bool), -1)
    decay = jnp.exp(jnp.where(causal, gc[..., :, None] - gc[..., None, :], -jnp.inf))
    a = jnp.where(strict, jnp.einsum('nbhid,nbhjd->nbhij', kb, k) * decay, 0.0)
    t_mat = a + jnp.eye(C, dtype=f32)
    u = lax.linalg.triangular_solve(t_mat, vb, left_side=True, lower=True)
    w = lax.linalg.triangular_solve(t_mat, kb * jnp.exp(gc)[..., None], left_side=True, lower=True)
    qk = jnp.einsum('nbhid,nbhjd->nbhij', q, k) * decay
    q_dec = q * jnp.exp(gc)[..., None]
    k_end = k * jnp.exp(gc[..., -1:] - gc)[..., None]
    g_last = jnp.exp(gc[..., -1])

    def step(state, inp):
        qd, ke, u_c, w_c, qk_c, gl = inp
        v_new = u_c - jnp.einsum('bhcd,bhde->bhce', w_c, state)
        o = jnp.einsum('bhcd,bhde->bhce', qd, state) + jnp.einsum('bhij,bhje->bhie', qk_c, v_new)
        state = state * gl[..., None, None] + jnp.einsum('bhcd,bhce->bhde', ke, v_new)
        return state, o

    s0 = jnp.zeros((B, H, dk, dv), f32)
    _, o = lax.scan(step, s0, (q_dec, k_end, u, w, qk, g_last))
    return jnp.moveaxis(o, (0, 2), (1, 3)).reshape(B, S, H, dv)

def gated_deltanet(qkv, z, b_logit, a_logit, conv_w, a_log, dt_bias, out_norm):
    B, S, _ = qkv.shape
    f32 = jnp.float32
    qkv = jax.nn.silu(causal_depthwise_conv(qkv, conv_w))
    q, k, v = jnp.split(qkv, 3, axis=-1)
    q = l2norm(q.reshape(B, S, DN_HEADS, DN_HEAD_DIM))
    k = l2norm(k.reshape(B, S, DN_HEADS, DN_HEAD_DIM))
    v = v.reshape(B, S, DN_HEADS, DN_HEAD_DIM)
    beta = jax.nn.sigmoid(b_logit.astype(f32))
    g = -jnp.exp(a_log.astype(f32)) * jax.nn.softplus(a_logit.astype(f32) + dt_bias.astype(f32))
    o = chunk_gated_delta_rule(q, k, v, g, beta)
    o = rmsnorm_2(o, out_norm) * jax.nn.silu(z.reshape(B, S, DN_HEADS, DN_HEAD_DIM).astype(f32))
    return o.reshape(B, S, DN_W).astype(qkv.dtype)

def cmp_to_slc_overlap(n_cmp, n_sel):
    c0 = np.arange(n_cmp)[:, None] * CMP_STRIDE
    j0 = np.arange(n_sel)[None, :] * SLC_LEN
    ov = np.clip(np.minimum(c0 + CMP_LEN, j0 + SLC_LEN) - np.maximum(c0, j0), 0, None) / CMP_LEN
    return jnp.asarray(ov, jnp.float32)

def compress_blocks(t, pos_emb, w1, w2, idx):
    B, _, G, d = t.shape
    n_cmp = idx.shape[0]
    blk = t[:, idx] + pos_emb[:, None, :].astype(t.dtype)
    blk = jnp.moveaxis(blk, 3, 2).reshape(B, n_cmp, G, CMP_LEN * d)
    return jax.nn.gelu(blk @ w1) @ w2

def window_branch(q, k, v, slopes):
    B, S, G, R, _ = q.shape
    span = WINDOW + ATT_QBLK
    kp = jnp.pad(k, ((0, 0), (WINDOW, 0), (0, 0), (0, 0)))
    vp = jnp.pad(v, ((0, 0), (WINDOW, 0), (0, 0), (0, 0)))

    def block(i):
        t0 = i * ATT_QBLK
        qb = lax.dynamic_slice_in_dim(q, t0, ATT_QBLK, axis=1)
        kb = lax.dynamic_slice_in_dim(kp, t0, span, axis=1)
        vb = lax.dynamic_slice_in_dim(vp, t0, span, axis=1)
        qpos = t0 + jnp.arange(ATT_QBLK)
        kpos = t0 - WINDOW + jnp.arange(span)
        dist = qpos[:, None] - kpos[None, :]
        mask = (dist >= 0) & (dist < WINDOW) & (kpos[None, :] >= 0)
        s = jnp.einsum('bqgrd,bkgd->bgrqk', qb, kb).astype(jnp.float32) - slopes[:, :, None, None] * dist
        p = jax.nn.softmax(jnp.where(mask, s, NEG), axis=-1).astype(vb.dtype)
        return jnp.einsum('bgrqk,bkge->bqgre', p, vb)

    o = lax.map(block, jnp.arange(S // ATT_QBLK))
    return jnp.moveaxis(o, 0, 1).reshape(B, S, G, R, -1)

def selection_branch(q, k, v, sel_idx, slopes):
    B, S, G, R, dk = q.shape
    dv = v.shape[-1]
    n_sel = S // SLC_LEN
    K = sel_idx.shape[-1]
    kblk = jnp.moveaxis(k.reshape(B, n_sel, SLC_LEN, G, dk), 3, 1).reshape(B, G, n_sel, SLC_LEN * dk)
    vblk = jnp.moveaxis(v.reshape(B, n_sel, SLC_LEN, G, dv), 3, 1).reshape(B, G, n_sel, SLC_LEN * dv)
    gather = jax.vmap(jax.vmap(lambda tab, ix: tab[ix]))

    def block(i):
        t0 = i * SLC_QBLK
        qb = lax.dynamic_slice_in_dim(q, t0, SLC_QBLK, axis=1)
        ib = lax.dynamic_slice_in_dim(sel_idx, t0, SLC_QBLK, axis=2)
        flat = ib.reshape(B, G, SLC_QBLK * K)
        kg = gather(kblk, flat).reshape(B, G, SLC_QBLK, K * SLC_LEN, dk)
        vg = gather(vblk, flat).reshape(B, G, SLC_QBLK, K * SLC_LEN, dv)
        kpos = (ib[..., None] * SLC_LEN + jnp.arange(SLC_LEN)).reshape(B, G, SLC_QBLK, K * SLC_LEN)
        qpos = t0 + jnp.arange(SLC_QBLK)
        dist = (qpos[:, None] - kpos)[:, :, None]
        s = jnp.einsum('bqgrd,bgqkd->bgrqk', qb, kg).astype(jnp.float32) - slopes[None, :, :, None, None] * dist
        p = jax.nn.softmax(jnp.where(dist >= 0, s, NEG), axis=-1).astype(vg.dtype)
        return jnp.einsum('bgrqk,bgqke->bqgre', p, vg)

    o = lax.map(block, jnp.arange(S // SLC_QBLK))
    return jnp.moveaxis(o, 0, 1).reshape(B, S, G, R, dv)

def nsa_mixer(q, k_c, v_c, k_s, v_s, k_w, v_w, gate_logits, q_norm, kn_cmp, kn_slc, kn_win,
              cmp_pos_k, cmp_w1_k, cmp_w2_k, cmp_pos_v, cmp_w1_v, cmp_w2_v):
    B, S, _ = q.shape
    G, R, d = NSA_GROUPS, NSA_REP, NSA_HEAD_DIM
    f32 = jnp.float32
    slopes = alibi_slopes(NSA_HEADS).reshape(G, R)
    pos = jnp.arange(S)
    q = (rmsnorm_2(q.reshape(B, S, NSA_HEADS, d), q_norm) * (d ** -0.5)).reshape(B, S, G, R, d)
    kv = lambda t: t.reshape(B, S, G, d)

    n_cmp = (S - CMP_LEN) // CMP_STRIDE + 1
    idx = np.arange(n_cmp)[:, None] * CMP_STRIDE + np.arange(CMP_LEN)[None, :]
    kc = rmsnorm_2(compress_blocks(kv(k_c), cmp_pos_k, cmp_w1_k, cmp_w2_k, idx), kn_cmp)
    vc = compress_blocks(kv(v_c), cmp_pos_v, cmp_w1_v, cmp_w2_v, idx)
    cmp_end = jnp.asarray(idx[:, -1])
    dist_c = pos[:, None] - cmp_end[None, :]
    s_c = jnp.einsum('bsgrd,bcgd->bgrsc', q, kc).astype(f32) - slopes[:, :, None, None] * dist_c
    any_valid = (pos >= CMP_LEN - 1).astype(f32)[:, None]
    p_c = jax.nn.softmax(jnp.where(dist_c >= 0, s_c, NEG), axis=-1) * any_valid
    o_cmp = jnp.einsum('bgrsc,bcgd->bsgrd', p_c.astype(vc.dtype), vc)

    n_sel = S // SLC_LEN
    imp = jnp.einsum('bgrsc,cj->bgsj', p_c, cmp_to_slc_overlap(n_cmp, n_sel))
    j = jnp.arange(n_sel)[None, :]
    blk_t = (pos // SLC_LEN)[:, None]
    imp = jnp.where(j <= blk_t, imp, NEG)
    imp = jnp.where((j == blk_t) | (j == 0), FORCE, imp)
    _, sel_idx = lax.top_k(imp, min(SLC_TOPK, n_sel))
    o_slc = selection_branch(q, rmsnorm_2(kv(k_s), kn_slc), kv(v_s), sel_idx, slopes)

    o_win = window_branch(q, rmsnorm_2(kv(k_w), kn_win), kv(v_w), slopes)

    gates = jax.nn.sigmoid(gate_logits.astype(f32)).reshape(B, S, G, R, 3)
    o = gates[..., 0:1] * o_cmp + gates[..., 1:2] * o_slc + gates[..., 2:3] * o_win
    return o.reshape(B, S, NSA_W).astype(q.dtype)

def second_inputs(seed: int = 0) -> dict:
    key = jax.random.key(seed)
    ks = jax.random.split(key, 24)
    f32 = jnp.float32
    L = DEPTH_2

    def nrm(k, shape, scale):
        return jax.random.normal(k, shape, f32) * scale

    def gain(k, n):
        return 1.0 + 0.02 * jax.random.normal(k, (L, n), f32)

    dt = jnp.exp(jax.random.uniform(ks[4], (L, DN_HEADS), f32, math.log(1e-3), math.log(1e-1)))
    flat = CMP_LEN * NSA_HEAD_DIM
    return {
        "x": nrm(ks[0], (BATCH, SEQ, D_MODEL), 1.0),
        "norm_mix": gain(ks[1], D_MODEL),
        "w_in": nrm(ks[2], (L, D_MODEL, IN_WIDTH_2), D_MODEL ** -0.5),
        "dn_conv": nrm(ks[3], (L, DN_CONV, 3 * DN_W), DN_CONV ** -0.5),
        "dn_a_log": jnp.log(jax.random.uniform(ks[5], (L, DN_HEADS), f32, 1.0, 16.0)),
        "dn_dt_bias": dt + jnp.log(-jnp.expm1(-dt)),
        "dn_out_norm": gain(ks[6], DN_HEAD_DIM),
        "nsa_q_norm": gain(ks[7], NSA_HEAD_DIM),
        "nsa_k_norm_cmp": gain(ks[8], NSA_HEAD_DIM),
        "nsa_k_norm_slc": gain(ks[9], NSA_HEAD_DIM),
        "nsa_k_norm_win": gain(ks[10], NSA_HEAD_DIM),
        "cmp_pos_k": nrm(ks[11], (L, CMP_LEN, NSA_HEAD_DIM), 0.1),
        "cmp_w1_k": nrm(ks[12], (L, flat, CMP_HIDDEN), flat ** -0.5),
        "cmp_w2_k": nrm(ks[13], (L, CMP_HIDDEN, NSA_HEAD_DIM), CMP_HIDDEN ** -0.5),
        "cmp_pos_v": nrm(ks[14], (L, CMP_LEN, NSA_HEAD_DIM), 0.1),
        "cmp_w1_v": nrm(ks[15], (L, flat, CMP_HIDDEN), flat ** -0.5),
        "cmp_w2_v": nrm(ks[16], (L, CMP_HIDDEN, NSA_HEAD_DIM), CMP_HIDDEN ** -0.5),
        "w_proj_dn": nrm(ks[17], (L, DN_W, D_MODEL), DN_W ** -0.5),
        "w_proj_nsa": nrm(ks[18], (L, NSA_W, D_MODEL), NSA_W ** -0.5),
        "w_out": nrm(ks[19], (L, D_MODEL, D_MODEL), D_MODEL ** -0.5),
        "norm_mlp": gain(ks[20], D_MODEL),
        "w_up": nrm(ks[21], (L, D_MODEL, D_FF_2), D_MODEL ** -0.5),
        "w_down": nrm(ks[22], (L, D_FF_2, D_MODEL), D_FF_2 ** -0.5),
    }

def second_block(x, norm_mix, w_in, dn_conv, dn_a_log, dn_dt_bias, dn_out_norm,
              nsa_q_norm, nsa_k_norm_cmp, nsa_k_norm_slc, nsa_k_norm_win,
              cmp_pos_k, cmp_w1_k, cmp_w2_k, cmp_pos_v, cmp_w1_v, cmp_w2_v,
              w_proj_dn, w_proj_nsa, w_out, norm_mlp, w_up, w_down):
    splits = _in_split_points()
    for l in range(DEPTH_2):
        h = rmsnorm_2(x, norm_mix[l])
        (dn_qkv, dn_z, dn_b, dn_a, ns_q, ns_kc, ns_vc, ns_ks, ns_vs, ns_kw, ns_vw, ns_gate,
         gate_dn, gate_nsa) = jnp.split(h @ w_in[l], splits, axis=-1)
        o_dn = gated_deltanet(dn_qkv, dn_z, dn_b, dn_a, dn_conv[l], dn_a_log[l], dn_dt_bias[l], dn_out_norm[l])
        o_ns = nsa_mixer(ns_q, ns_kc, ns_vc, ns_ks, ns_vs, ns_kw, ns_vw, ns_gate,
                         nsa_q_norm[l], nsa_k_norm_cmp[l], nsa_k_norm_slc[l], nsa_k_norm_win[l],
                         cmp_pos_k[l], cmp_w1_k[l], cmp_w2_k[l], cmp_pos_v[l], cmp_w1_v[l], cmp_w2_v[l])
        mix = jax.nn.sigmoid(gate_dn) * (o_dn @ w_proj_dn[l]) + jax.nn.sigmoid(gate_nsa) * (o_ns @ w_proj_nsa[l])
        x = x + mix @ w_out[l]
        h2 = rmsnorm_2(x, norm_mlp[l])
        x = x + jnp.square(jax.nn.relu(h2 @ w_up[l])) @ w_down[l]
    return x


def setup_inputs(seed=0):
    out = dict(first_inputs(seed))
    for name, value in second_inputs(seed + 1).items():
        if name != "x":
            out[name + "_2"] = value
    return out


def reference(
    x, meta_tokens, norm1_g, w_in, b_glu, conv_w, conv_b, conv_ln_g, conv_ln_b, lam_q1, lam_k1,
    lam_q2, lam_k2, subln_g, w_out, norm2_g, w_gate_up, w_down, final_g, norm_mix_2, w_in_2,
    dn_conv_2, dn_a_log_2, dn_dt_bias_2, dn_out_norm_2, nsa_q_norm_2, nsa_k_norm_cmp_2,
    nsa_k_norm_slc_2, nsa_k_norm_win_2, cmp_pos_k_2, cmp_w1_k_2, cmp_w2_k_2, cmp_pos_v_2,
    cmp_w1_v_2, cmp_w2_v_2, w_proj_dn_2, w_proj_nsa_2, w_out_2, norm_mlp_2, w_up_2, w_down_2,
):
    x = first_block(
        x, meta_tokens, norm1_g, w_in, b_glu, conv_w, conv_b, conv_ln_g, conv_ln_b, lam_q1,
        lam_k1, lam_q2, lam_k2, subln_g, w_out, norm2_g, w_gate_up, w_down, final_g,
    )
    return second_block(
        x, norm_mix_2, w_in_2, dn_conv_2, dn_a_log_2, dn_dt_bias_2, dn_out_norm_2, nsa_q_norm_2,
        nsa_k_norm_cmp_2, nsa_k_norm_slc_2, nsa_k_norm_win_2, cmp_pos_k_2, cmp_w1_k_2,
        cmp_w2_k_2, cmp_pos_v_2, cmp_w1_v_2, cmp_w2_v_2, w_proj_dn_2, w_proj_nsa_2, w_out_2,
        norm_mlp_2, w_up_2, w_down_2,
    )


_drawn_inputs = setup_inputs


def setup_inputs(seed=0):
    import zlib

    import numpy as np

    out = dict(_drawn_inputs(seed))
    spreads = {}
    factors = {'b_glu': 3.426,
     'conv_ln_g': 3.503,
     'conv_ln_b': 3.98,
     'lam_q1': 3.204,
     'subln_g': 3.186,
     'norm_mix_2': 4.225,
     'dn_out_norm_2': 8.0,
     'nsa_q_norm_2': 26.397,
     'nsa_k_norm_cmp_2': 64.0,
     'nsa_k_norm_slc_2': 41.985,
     'nsa_k_norm_win_2': 43.698,
     'cmp_pos_k_2': 8.0,
     'cmp_pos_v_2': 28.416,
     'norm_mlp_2': 12.164,
     'norm2_g': 2.799}
    for name, (base, spread) in spreads.items():
        noise = np.random.default_rng([zlib.crc32(name.encode()), seed]).standard_normal(out[name].shape)
        drawn = base * np.exp(spread * noise) if base else spread * noise
        out[name] = __import__('jax').numpy.asarray(drawn.astype(out[name].dtype))
    for name, factor in factors.items():
        out[name] = (out[name] * factor).astype(out[name].dtype)
    return out
```

```python
import math
from contextlib import ExitStack

import numpy as np

import concourse.bass as bass
from concourse import mybir

F32 = mybir.dt.float32
F32R = mybir.dt.float32r
ALU = mybir.AluOpType
ACT = mybir.ActivationFunctionType
AX = mybir.AxisListType
ds = bass.ds

P = 128
D = 1024
KD = D // P
SEQ = 512
N_META = 16
T1 = SEQ + N_META
HALF = T1 // 2
NT1 = 5
LAST = T1 - 4 * P
PADT = NT1 * P
DEPTH = 2
HEADS1 = 4
TAPS = 31
FF1 = 2816
FC = (12, 10)
PW = 256
PANEL = KD * PW
PANELS_L = 4 + 2 + 4 + 4 + 12 + 8 + 10 + 8
MASKED = -1e30

EV_GLU, EV_V, EV_QK, EV_OUT = 0, 16, 26, 42
EV_FF = (58, 126)
EV_DOWN = (106, 166)
EVENTS = 186
PANELS_L = 52
GLUS = 52
FFS = 44
ADDS = 48


def first_constants():
    pos = np.arange(T1, dtype=np.float32)
    inv = np.float32(10000.0) ** (-np.arange(0, 64, 2, dtype=np.float32) / np.float32(64))
    ang = (pos[None, :] * inv[np.arange(P) % 32][:, None]).astype(np.float32)
    rot = np.zeros((P, P), np.float32)
    for m in range(P):
        low = m % 64 < 32
        rot[m + 32 if low else m - 32, m] = -1.0 if low else 1.0
    q, k = np.arange(P)[:, None], np.arange(P)[None, :]
    lam = [0.8 - 0.6 * math.exp(-0.3 * l) for l in range(DEPTH)]
    return {
        "ident": np.eye(P, dtype=np.float32),
        "rot": rot,
        "cos": np.cos(ang, dtype=np.float32),
        "sin": np.sin(ang, dtype=np.float32),
        "causal": np.where(k <= q, 0.0, MASKED).astype(np.float32),
        "eps5": np.full((P, 1), 1e-5, np.float32),
        "eps6": np.full((P, 1), 1e-6, np.float32),
        "lam_init": np.tile(np.float32(lam), (P, 1)),
        "lam_rest": np.tile(np.float32([1.0 - v for v in lam]), (P, 1)),
    }


def packed(tables):
    return np.ascontiguousarray(np.concatenate(list(tables.values()), axis=1), np.float32)


def columns(tables):
    at, out = 0, {}
    for name, a in tables.items():
        out[name] = (at, a.shape[1])
        at += a.shape[1]
    return out, at

(EV_QKV, EV_Z, EV_NQ, EV_KC, EV_KS, EV_KW, EV_VS, EV_VW, EV_VC, EV_MDN, EV_MNS, EV_WO) = (
    0, 24, 32, 40, 42, 44, 46, 50, 54, 56, 72, 88)
EV_UP = (96, 120)
EV_DN = (112, 136)
(PN_QKV, PN_Z, PN_NQ, PN_KC, PN_KS, PN_KW, PN_VS, PN_VW, PN_VC, PN_MDN, PN_MNS, PN_WO) = (
    0, 12, 16, 20, 21, 22, 23, 24, 25, 26, 34, 42)
PN_UP = (46, 62)
PN_DN = (54, 70)
PANELS_2 = 78
NT2 = 4
DN_HEADS = 8
HG = 4
CHUNK = 64
LEVELS = 6
KINDS = 6
NSA_HEADS, GROUPS, REP, HD = 16, 4, 4, 64
N_CMP = (SEQ - 32) // 16 + 1
WINDOW = 256
FAR = 1e32
C_Z = 3072
C_BA = 4096
C_NQ = 4112
C_KC, C_VC, C_KS, C_VS, C_KW, C_VW = (C_NQ + 1024 + 256 * i for i in range(6))
C_GATE = C_VW + 256
C_MDN = C_GATE + 48
C_MNS = C_MDN + 1024


def second_constants():
    i, j = np.arange(P)[:, None], np.arange(P)[None, :]
    same = i // CHUNK == j // CHUNK
    out = {
        "tri": (same & (i <= j)).astype(np.float32),
        "blk": same.astype(np.float32),
        "decay_mask": np.where(same & (j >= i), 0.0, MASKED).astype(np.float32),
    }
    levels = []
    for n in range(LEVELS):
        s = 1 << n
        levels.append((i // (2 * s) == j // (2 * s)) & (i // s % 2 == 1) & (j // s % 2 == 0))
    out["levels"] = np.concatenate(levels, axis=1).astype(np.float32)
    d = i - np.arange(SEQ)[None, :] + (SEQ - P)
    out["dist"] = np.where(d >= 0, d, FAR).astype(np.float32)
    w = d[:, SEQ - P - WINDOW:]
    out["dist_win"] = np.where((w >= 0) & (w < WINDOW), w, FAR).astype(np.float32)
    c = [P * t + i - (16 * np.arange(N_CMP)[None, :] + 31) for t in range(NT2)]
    out["dist_cmp"] = np.concatenate([np.where(x >= 0, x, FAR) for x in c], axis=1).astype(np.float32)
    out["valid"] = np.concatenate([(P * t + i >= 31) for t in range(NT2)], axis=1).astype(np.float32)
    out["halves"] = (i // 64 == np.arange(2)[None, :]).astype(np.float32)
    out["neg_slope"] = np.tile(-(2.0 ** (-8.0 * np.arange(1, NSA_HEADS + 1) / NSA_HEADS)), (P, 1)).astype(np.float32)
    return out


def hybrid_blocks(nc, A, table1, table2, out):
    tab1, n1 = columns(first_constants())
    tab2, n2 = columns(second_constants())
    flat = "p a b -> p (a b)"

    with ExitStack() as ctx:
        base = -(-nc.sbuf_base // 64) * 64

        def put(name, shape, offset, dtype=F32):
            return nc.alloc_sbuf_tensor_at(name, shape, dtype, offset=offset)[:]

        def room(n):
            nonlocal base
            at, base = base, base + -(-n // 32) * 32
            return at

        def keep(name, shape, dtype=F32):
            return put(name, shape, room(4 * int(np.prod(shape[1:]))), dtype)

        const1_at = room(4 * n1)
        const1 = put("const1", [P, n1], const1_at)
        ident, rot, cos, sin, causal, eps5, eps6, lam_init, lam_rest = (
            const1[:, a:a + n] for a, n in tab1.values())
        ones = keep("ones", [P, 2])
        vec_cols = keep("vec_cols", [P, 103])
        conv_cols_at = room(4 * DEPTH * TAPS * 4)
        conv_cols = put("conv_cols", [P, DEPTH * TAPS * 4], conv_cols_at)
        dn_cols = keep("dn_cols", [P, 128])
        lay = keep("lay", [P, 37])
        lay_conv = keep("lay_conv", [P, TAPS * 4])
        sub_gain = keep("sub_gain", [P, 1])
        lam_dot = keep("lam_dot", [P, 2 * DEPTH])
        lam_exp = keep("lam_exp", [P, 2 * DEPTH])
        neg_lam = keep("neg_lam", [P, DEPTH])
        lay_neg_lam = keep("lay_neg_lam", [P, 1])
        rms = keep("rms", [P, 32])
        rstd = keep("rstd", [P, 32])
        top, neg_top, mass, weight = (keep(n, [P, 2, 2]) for n in ("top", "neg_top", "mass", "weight"))
        weight2 = keep("weight2", [P, 2])
        sq_at = room(4 * 2 * PADT)
        sq = put("sq", [P, 2, PADT], sq_at)
        wraw_at = room(4 * 2 * PANEL)
        wraw = put("wraw", [P, 2, PANEL], wraw_at)
        whi = keep("whi", [P, 2, PANEL], F32R)
        wlo = keep("wlo", [P, 2, PANEL], F32R)
        hn_hi = keep("hn_hi", [P, KD * T1 + PADT - T1], F32R)
        hn_lo = keep("hn_lo", [P, KD * T1 + PADT - T1], F32R)
        h_at = room(4 * KD * T1)
        h = put("h", [P, KD, T1], h_at)
        work = room(2 * 4 * FC[0] * T1)
        ff_hi = put("ff_hi", [P, FC[0], T1], work, F32R)
        ff_lo = put("ff_lo", [P, FC[0], T1], work + 4 * FC[0] * T1, F32R)
        x_tok = put("x_tok", [P, 4, D], work)
        meta_tok = put("meta_tok", [N_META, D], work + 16 * D)
        rows_vec = put("rows_vec", [103, P], work + 20 * D)
        rows_conv = put("rows_conv", [TAPS * 4, DEPTH, P], work + 20 * D + 512)
        rows_dn = put("rows_dn", [P, P], work + 20 * D + 1536)
        lam_rows = put("lam_rows", [P, 4, DEPTH * 64], work + 20 * D + 2048)
        lam_prod = put("lam_prod", [P, 2 * DEPTH, 64], work + 20 * D + 4096)
        qk_raw = put("qk_raw", [P, KD, T1], work)
        o_raw = qk_raw
        v_at = work + 4 * KD * T1
        v_tok = put("v_tok", [P, NT1, 512], v_at)
        z = put("z", [P, 4, TAPS - 1 + T1], v_at + 4 * NT1 * 512)
        conv_at = v_at + 4 * NT1 * 512 + 16 * (TAPS - 1 + T1)
        conv = put("conv", [P, 4 * T1 + PADT - T1], conv_at)
        scratch = room(32 * 1024)
        t_chunk = put("t_chunk", [P, 2, T1], scratch)
        glu_gate = put("glu_gate", [P, 4, HALF], scratch + 8 * T1)
        glu_val = put("glu_val", [P, 4, HALF], scratch + 16 * T1)
        s_at = scratch
        q_head = put("q_head", [P, PADT], s_at)
        k_head = put("k_head", [P, T1], s_at + 4 * PADT)
        s_at += 4 * PADT + 4 * T1
        rope_a = put("rope_a", [P, 2, T1], s_at)
        v_head = put("v_head", [P, NT1, P], s_at + 8 * T1)
        s_at += 8 * T1 + 4 * PADT
        rope_b = put("rope_b", [P, 2, T1], s_at)
        probs4 = put("probs", [P, 2, 2, T1], s_at)
        diff = put("diff", [P, 2, PADT], s_at + 16 * T1)
        diff_t = put("diff_t", [P, 2, PADT], s_at + 16 * T1 + 8 * PADT)
        s_at += 16 * T1 + 16 * PADT
        assert s_at <= scratch + 32 * 1024
        const2 = keep("const2", [P, n2])
        (tri, blk, decay_mask, levels, dist, dist_win, dist_cmp, valid, halves, neg_slope) = (
            const2[:, a:a + n] for a, n in tab2.values())
        small_at = room(4 * KD * 64)
        w_small = put("w_small", [P, KD, 64], small_at)
        v_grp = put("v_grp", [P, 2, NT2, HD], small_at)
        head_rows = keep("head_rows", [P, 2, DN_HEADS])
        w2k = keep("w2k", [P, 2 * HD])
        w2v = keep("w2v", [P, HD])
        gates = keep("gates", [P, NT2, 48])
        col_tab = keep("col_tab", [P, 2 * NT2, KINDS, HG])
        cur = keep("cur", [P, KINDS, HG])
        tap_w = keep("tap_w", [P, 4, 4])
        n_rms = put("n_rms", [P, 97], conv_cols_at)
        n_rstd = put("n_rstd", [P, 97], conv_cols_at + 416)
        q_gain = keep("q_gain", [P, 1])
        pos_sum = keep("pos_sum", [P, 1])
        slope4 = keep("slope4", [P, REP])
        s_top, s_neg, s_mass, s_weight = (keep(n, [P, 3, REP]) for n in ("s_top", "s_neg", "s_mass", "s_weight"))
        assert base <= nc.sbuf_usable_end, base

        x2 = put("x2", [P, KD, SEQ], scratch)
        tmp = scratch + 4 * KD * SEQ
        t2 = put("t2", [P, 2, SEQ], tmp)
        qkv = put("qkv", [P, 24, SEQ], work)
        taps = put("taps", [P, 2, SEQ + 3], tmp)
        taps_sum = put("taps_sum", [P, 2, SEQ], tmp + 4160)
        ws_hi = put("ws_hi", [P, KD * 64], tmp + 8256, F32R)
        ws_lo = put("ws_lo", [P, KD * 64], tmp + 10304, F32R)
        (beta, a_dt, a_abs, a_ln, a_sp, g_log, g_cum, g_rest, g_exp, ke_exp, a_exp) = (
            put(n, [P, NT2, DN_HEADS], tmp + 12352 + 128 * i) for i, n in enumerate(
                ("beta", "a_dt", "a_abs", "a_ln", "a_sp", "g_log", "g_cum", "g_rest", "g_exp", "ke_exp", "a_exp")))
        l2_rms = put("l2_rms", [P, 16, NT2], tmp + 13760)
        l2_inv = put("l2_inv", [P, 16, NT2], tmp + 14016)
        dk_t, dkb_t, dq_t, dqd_t, dkbg, dke, dvb, da_t = (
            put(n, [P, HG, P], h_at + 2048 * i) for i, n in enumerate(
                ("dk_t", "dkb_t", "dq_t", "dqd_t", "dkbg", "dke", "dvb", "da_t")))
        dqk_t, decay, g_rows, dx, dx_t, dp, dw_t, dvn = (
            put(n, [P, HG, P], tmp + 2048 * i) for i, n in enumerate(
                ("dqk_t", "decay", "g_rows", "dx", "dx_t", "dp", "dw_t", "dvn")))
        rope_at = const1_at + 4 * 2 * P
        dv_t = put("dv_t", [P, HG, P], rope_at)
        state = put("state", [P, HG, P], rope_at + 2048)
        z_act = put("z_act", [P, 2, SEQ], tmp)
        nq = put("nq", [P, KD, SEQ], work)
        kcmp = put("kcmp", [P, GROUPS, SEQ], work + 16384)
        w1 = put("w1", [P, 16, P], work + 8192 + 16384)
        ks2 = put("ks2", [P, GROUPS, SEQ], h_at)
        kw2 = put("kw2", [P, GROUPS, SEQ], h_at + 8192)
        k_grp = put("k_grp", [P, 2, SEQ], rope_at)
        kc_grp = put("kc_grp", [P, N_CMP], rope_at + 4096)
        vs = put("vs", [P, NT2, GROUPS * HD], tmp)
        vw = put("vw", [P, NT2, GROUPS * HD], tmp + 4096)
        k_raw = put("k_raw", [P, 4, SEQ], tmp + 8192)
        p_t = put("p_t", [P, 2, REP * P], tmp + 8192)
        vc = put("vc", [P, GROUPS, HD], tmp + 12288)
        vc_grp = put("vc_grp", [P, HD], tmp + 13312)
        kc2 = put("kc2", [P, P], tmp + 13568)
        kc_raw = put("kc_raw", [P, P], tmp + 14080)
        pc_t = put("pc_t", [P, REP * P], tmp + 14080)
        c_gelu = put("c_gelu", [P, P], tmp + 14592)
        probs_at = (work + 16384, wraw_at)
        p_slc = [put(f"p_slc{i}", [P, REP, SEQ], at) for i, at in enumerate(probs_at)]
        p_win = [put(f"p_win{i}", [P, REP, SEQ - P], at + 8192) for i, at in enumerate(probs_at)]
        p_cmp = [put(f"p_cmp{i}", [P, REP, 32], at + 14336) for i, at in enumerate(probs_at)]
        q_grp = put("q_grp", [P, 2, SEQ], sq_at)
        o_hi = put("o_hi", [P, KD, SEQ], h_at, F32R)
        o_lo = put("o_lo", [P, KD, SEQ], tmp, F32R)
        merged = put("merged", [P, KD, SEQ], work + 16384)
        sig = put("sig", [P, 2, SEQ], sq_at)
        f_hi = put("f_hi", [P, 16, SEQ], h_at, F32R)
        f_lo = put("f_lo", [P, 16, SEQ], h_at + 32768, F32R)
        relu = put("relu", [P, 2, SEQ], sq_at)
        relu_sq = put("relu_sq", [P, 2, SEQ], rope_at)
        y_tok = put("y_tok", [P, NT2, D], tmp)

        ps = ctx.enter_context(nc.psum_tensor("ps", [P, 8, 512], F32))
        line = ps[:, :, :].rearrange(flat)

        def sem(name):
            return ctx.enter_context(nc.semaphore(name))

        setup_in = sem("setup_in")
        raw_in = [sem("raw_in0"), sem("raw_in1")]
        w_hi = sem("w_hi")
        w_split = sem("w_split")
        products_done = sem("products_done")
        x_turned = sem("x_turned")
        h_copied = sem("h_copied")
        cols_turned = sem("cols_turned")
        lam_dots = sem("lam_dots")
        lam_exps = sem("lam_exps")
        h_ready = sem("h_ready")
        sq_ready = sem("sq_ready")
        sq_used = sem("sq_used")
        rms_ready = sem("rms_ready")
        rstd_ready = sem("rstd_ready")
        rows_ready = sem("rows_ready")
        t_ready = sem("t_ready")
        hi_ready = sem("hi_ready")
        hn_ready = sem("hn_ready")
        gate_act = sem("gate_act")
        glu_used = sem("glu_used")
        ffv_hi = sem("ffv_hi")
        ff_ready = sem("ff_ready")
        qkv_copied = sem("qkv_copied")
        conv_done = sem("conv_done")
        h_added = sem("h_added")
        vh_ready = sem("vh_ready")
        rope_a_ready = sem("rope_a_ready")
        rot_done = sem("rot_done")
        rope_done = sem("rope_done")
        scored = sem("scored")
        max_ready = sem("max_ready")
        exp_done = sem("exp_done")
        diff_ready = sem("diff_ready")
        diff_turned = sem("diff_turned")
        diff_t_ready = sem("diff_t_ready")
        pv_done = sem("pv_done")
        o_copied = sem("o_copied")
        sub_sq = sem("sub_sq")
        sub_stat = sem("sub_stat")
        sub_rms = sem("sub_rms")
        sub_rstd = sem("sub_rstd")
        sub_rows = sem("sub_rows")
        sub_t = sem("sub_t")
        sub_hi = sem("sub_hi")
        ln_sum = sem("ln_sum")
        ln_mean = sem("ln_mean")
        ln_mean_rows = sem("ln_mean_rows")
        ln_centred = sem("ln_centred")
        ln_sq = sem("ln_sq")
        ln_stat = sem("ln_stat")
        ln_rms = sem("ln_rms")
        ln_rstd = sem("ln_rstd")
        ln_rows = sem("ln_rows")
        ln_t = sem("ln_t")
        ln_silu = sem("ln_silu")
        mix_hi = sem("mix_hi")
        mix_ready = sem("mix_ready")
        stored = sem("stored")

        x2_ready = sem("x2_ready")
        ws_hi_ready = sem("ws_hi_ready")
        ws_ready = sem("ws_ready")
        small_done = sem("small_done")
        small_act = sem("small_act")
        a_abs_ready = sem("a_abs_ready")
        a_ln_ready = sem("a_ln_ready")
        g_ready = sem("g_ready")
        gc_done = sem("gc_done")
        gc_copied = sem("gc_copied")
        g_rest_ready = sem("g_rest_ready")
        decays_ready = sem("decays_ready")
        dconv_done = sem("dconv_done")
        silu_done = sem("silu_done")
        l2_sq = sem("l2_sq")
        l2_stat = sem("l2_stat")
        l2_rms_ready = sem("l2_rms_ready")
        cur_ready = sem("cur_ready")
        drows_done = sem("drows_done")
        dk_ready = sem("dk_ready")
        dv_ready = sem("dv_ready")
        dec_ready = sem("dec_ready")
        dexp_done = sem("dexp_done")
        dqd_ready = sem("dqd_ready")
        dturned = sem("dturned")
        dkk_done = sem("dkk_done")
        da_ready = sem("da_ready")
        p1_done = sem("p1_done")
        dp_ready = sem("dp_ready")
        delta_done = sem("delta_done")
        dx_ready = sem("dx_ready")
        dw_done = sem("dw_done")
        dw_ready = sem("dw_ready")
        vn_done = sem("vn_done")
        vn_ready = sem("vn_ready")
        s_done = sem("s_done")
        state_ready = sem("state_ready")
        do_copied = sem("do_copied")
        odn_sq = sem("odn_sq")
        odn_stat = sem("odn_stat")
        odn_rms = sem("odn_rms")
        odn_rstd = sem("odn_rstd")
        odn_rows = sem("odn_rows")
        odn_normed = sem("odn_normed")
        z_copied = sem("z_copied")
        odn_ready = sem("odn_ready")
        nsa_copied = sem("nsa_copied")
        n_sq = sem("n_sq")
        n_stat = sem("n_stat")
        n_rms_ready = sem("n_rms_ready")
        n_rstd_ready = sem("n_rstd_ready")
        n_rows = sem("n_rows")
        n_scaled = sem("n_scaled")
        w1_in = sem("w1_in")
        hidden_done = sem("hidden_done")
        pos_ready = sem("pos_ready")
        gelu_ready = sem("gelu_ready")
        kc_done = sem("kc_done")
        kc_sq = sem("kc_sq")
        kc_stat = sem("kc_stat")
        kc_rms = sem("kc_rms")
        kc_rstd = sem("kc_rstd")
        kc_rows = sem("kc_rows")
        kc_ready = sem("kc_ready")
        vc_done = sem("vc_done")
        vc_ready = sem("vc_ready")
        q_ready = sem("q_ready")
        kg_ready = sem("kg_ready")
        vg_ready = sem("vg_ready")
        c_pad_ready = sem("c_pad_ready")
        slc_scored = sem("slc_scored")
        slc_read = sem("slc_read")
        win_scored = sem("win_scored")
        win_read = sem("win_read")
        tops_ready = sem("tops_ready")
        exps_done = sem("exps_done")
        p_ready = sem("p_ready")
        p_turned = sem("p_turned")
        p_t_ready = sem("p_t_ready")
        pv2_done = sem("pv2_done")
        att_copied = sem("att_copied")
        o_hi_ready = sem("o_hi_ready")
        o_ready = sem("o_ready")
        sig_ready = sem("sig_ready")
        merged_part = sem("merged_part")
        merged_hi = sem("merged_hi")
        merged_ready = sem("merged_ready")
        x2_added = sem("x2_added")
        relu_ready = sem("relu_ready")
        relu_sq_ready = sem("relu_sq_ready")
        f_hi_ready = sem("f_hi_ready")
        f_ready = sem("f_ready")
        y_turned = sem("y_turned")
        y_copied = sem("y_copied")
        E0, N0 = DEPTH * EVENTS, DEPTH * PANELS_L
        Q0, M0, X0 = DEPTH * 26, 2 * DEPTH, DEPTH + 1

        def hx(x, k, start, n):
            return x[:, k * SEQ + start:k * SEQ + start + n]

        def tile(t):
            return slice(P * t, P * (t + 1))

        def by_head(bank):
            return ps[:, bank, :].rearrange("p (h n) -> p h n", h=HG)

        def col(name):
            return vec_cols[:, name:name + 1]

        BLOCKS = [(t + 1) + min(t + 1, 3) + 1 for t in range(NT2)]
        BLOCKS_G = sum(BLOCKS)

        def first_key(t):
            return P * max(0, t - 2)

        def wide(x, shape, axis):
            return x.unsqueeze(axis).to_broadcast(shape)
        block = ctx.enter_context(nc.Block())

        n_setup = [0]

        def tok_tile(t):
            return P * t, (P if t < 4 else LAST)

        def hn(x, k, start, n):
            return x[:, k * T1 + start:k * T1 + start + n]

        def scores_of(t):
            n, keys = tok_tile(t)[1], min(P * (t + 1), T1)
            if t < 4:
                return ps[0:n, 2 * (t % 2):2 * (t % 2) + 2, 0:keys]
            return ps[0:n, 0:4, :].rearrange("p (c b) w -> p c (b w)", c=2)[:, :, 0:keys]

        def key_blocks(t):
            return [(P * b, min(P, T1 - P * b)) for b in range(t + 1)]

        mean_rows = line[:, 2048:2048 + T1]
        conv_acc = line[:, 3072:3072 + T1]

        VEC = {"norm1": 0, "norm2": 8, "a_bias": 16, "gate_bias": 20, "conv_b": 24, "ln_g": 28,
               "ln_b": 32, "sub": 36}
        FINAL, NORM_MIX, NORM_MLP, DN_OUT, QN, KC_N, KS_N, KW_N = 74, 82, 90, 98, 99, 100, 101, 102

        @block.sync
        def _(sp):
            loads = [(const1, table1)]
            for t in range(4):
                loads.append((x_tok[:, t, :], A["x"][0, P * t:P * (t + 1), :]))
            loads.append((meta_tok, A["meta_tokens"]))

            def rows(a):
                return a.rearrange("(r w) -> r w", w=P)

            for l in range(DEPTH):
                for name, at in (("norm1_g", 0), ("norm2_g", 8), ("b_glu", 16), ("conv_b", 24),
                                 ("conv_ln_g", 28), ("conv_ln_b", 32), ("subln_g", 36)):
                    src = rows(A[name][l])
                    loads.append((rows_vec[37 * l + at:37 * l + at + src.shape[0], :], src))
                loads.append((rows_conv[:, l, :], A["conv_w"][l].rearrange("j (c w) -> (j c) w", w=P)))
            for name, at in (("final_g", FINAL), ("norm_mix_2", NORM_MIX), ("norm_mlp_2", NORM_MLP),
                             ("dn_out_norm_2", DN_OUT)):
                src = rows(A[name] if name == "final_g" else A[name][0])
                loads.append((rows_vec[at:at + src.shape[0], :], src))
            for name, at in (("nsa_q_norm_2", QN), ("nsa_k_norm_cmp_2", KC_N),
                             ("nsa_k_norm_slc_2", KS_N), ("nsa_k_norm_win_2", KW_N)):
                for half in range(2):
                    loads.append((rows_vec[at:at + 1, 64 * half:64 * half + 64], A[name]))
            loads.append((rows_dn[0:96, :], A["dn_conv_2"][0].rearrange("j (c w) -> (j c) w", w=P)))
            loads.append((rows_dn[96:112, :], A["cmp_pos_k_2"][0].rearrange("(m a) w -> m (a w)", a=2)))
            loads.append((rows_dn[112:128, :], A["cmp_pos_v_2"][0].rearrange("(m a) w -> m (a w)", a=2)))
            for i, name in enumerate(("lam_q1", "lam_k1", "lam_q2", "lam_k2")):
                loads.append((lam_rows[:, i, :], A[name].rearrange("a b -> (a b)").partition_broadcast(P)))
            w_in_2 = A["w_in_2"][0].rearrange("(k p) n -> p k n", p=P)
            loads += [(const2, table2), (w_small[:, :, 0:16], w_in_2[:, :, C_BA:C_BA + 16]),
                      (w_small[:, :, 16:64], w_in_2[:, :, C_GATE:C_GATE + 48])]
            for i, name in enumerate(("dn_a_log_2", "dn_dt_bias_2")):
                loads.append((head_rows[:, i, :], A[name][0].partition_broadcast(P)))
            for half in range(2):
                loads.append((w2k[:, HD * half:HD * (half + 1)], A["cmp_w2_k_2"][0]))
            loads.append((w2v, A["cmp_w2_v_2"][0]))
            n_setup[0] = 16 * len(loads)
            for dst, src in loads:
                sp.dma_start(dst, src).then_inc(setup_in, 16)

            def panel(n, slot, src):
                sp.wait_ge(w_split, n + 1)
                nk, w = src.shape[1], src.shape[2]
                dst = wraw[:, slot, 0:nk * w].rearrange("p (k n) -> p k n", k=nk)
                sp.dma_start(dst, src).then_inc(raw_in[slot], 16)

            w_in, w_out, w_gu, w_dn = (A[n].rearrange("d (k p) n -> d p k n", p=P)
                                       for n in ("w_in", "w_out", "w_gate_up", "w_down"))
            with sp.Fori(0, DEPTH) as l:
                first = l * PANELS_L
                cols = []
                for p in range(2):
                    cols += [2048 + PW * p, 1536 + PW * p]
                cols += [1024, 1024 + PW]
                for j, c in enumerate(cols):
                    panel(first + j, j % 2, w_in[l, :, :, c:c + PW])
                with sp.Fori(0, 2) as i:
                    for s in range(2):
                        panel(first + i * 2 + (6 + s), s, w_in[l, :, :, ds(i * (2 * PW) + s * PW, PW)])
                for j in range(4):
                    panel(first + 10 + j, j % 2, w_out[l, :, :, PW * j:PW * (j + 1)])
                at, k0 = 14, 0
                for n in FC:
                    with sp.Fori(0, n // 2) as i:
                        panel(first + at + i * 2, 0, w_gu[l, :, :, ds(i * PW + k0 * P, PW)])
                        panel(first + at + i * 2 + 1, 1,
                              w_gu[l, :, :, ds(i * PW + (k0 * P + FF1), PW)])
                    at += n
                    with sp.Fori(0, 4) as b:
                        for s in range(2):
                            ks = k0 + s * n // 2
                            panel(first + at + b * 2 + s, s,
                                  w_dn[l, :, ks:ks + n // 2, ds(b * PW, PW)])
                    at += 8
                    k0 += n
            def cols_of(name, c):
                return A[name][0].rearrange("(k p) n -> p k n", p=P)[:, :, c:c + PW]

            with sp.Fori(0, PN_Z // 2) as i:
                for s in range(2):
                    panel(i * 2 + (N0 + s), s, w_in_2[:, :, ds(i * (2 * PW) + s * PW, PW)])
            for j in range(4):
                panel(N0 + PN_Z + j, j % 2, w_in_2[:, :, C_Z + PW * j:C_Z + PW * (j + 1)])
            for j in range(4):
                panel(N0 + PN_NQ + j, j % 2, w_in_2[:, :, C_NQ + PW * j:C_NQ + PW * (j + 1)])
            sp.wait_ge(do_copied, 2 * NT2)
            sp.dma_start(w1, A["cmp_w1_k_2"][0].rearrange("(m p) n -> p m n", p=P)).then_inc(w1_in, 16)
            for j, c in enumerate((C_KC, C_KS, C_KW, C_VS, C_VW, C_VC)):
                n = PN_KC + j
                panel(N0 + n, n % 2, w_in_2[:, :, c:c + PW])
            sp.wait_ge(hidden_done, 1)
            sp.dma_start(w1, A["cmp_w1_v_2"][0].rearrange("(m p) n -> p m n", p=P)).then_inc(w1_in, 16)
            for pn, c, name in ((PN_MDN, C_MDN, "w_proj_dn_2"), (PN_MNS, C_MNS, "w_proj_nsa_2")):
                for j in range(4):
                    if pn == PN_MDN and j == 1:
                        sp.wait_ge(att_copied, GROUPS * NT2)
                    panel(N0 + pn + 2 * j, 0, w_in_2[:, :, c + PW * j:c + PW * (j + 1)])
                    panel(N0 + pn + 2 * j + 1, 1, cols_of(name, PW * j))
            for j in range(4):
                panel(N0 + PN_WO + j, j % 2, cols_of("w_out_2", PW * j))
            w_up = A["w_up_2"][0].rearrange("(k p) n -> p k n", p=P)
            w_down = A["w_down_2"][0].rearrange("(k p) n -> p k n", p=P)
            for part in range(2):
                with sp.Fori(0, 4) as i:
                    for s in range(2):
                        panel(i * 2 + (N0 + PN_UP[part] + s), s,
                              w_up[:, :, ds(i * (2 * PW) + (2048 * part + s * PW), PW)])
                with sp.Fori(0, 4) as i:
                    for s in range(2):
                        panel(i * 2 + (N0 + PN_DN[part] + s), s,
                              w_down[:, ds(i * 4 + (16 * part + 2 * s), 2), :])
            for half in range(2):
                sp.wait_ge(y_copied, 4 * half + 4)
                columns_of = slice(512 * half, 512 * (half + 1))
                sp.dma_start(out[0].rearrange("(t p) d -> p t d", p=P)[:, :, columns_of], y_tok[:, :, columns_of]
                             ).then_inc(stored, 16)
            sp.wait_ge(stored, 32)

        @block.tensor
        def _(pe):
            def product(dst, slot, k, oc, rhs_hi, rhs_lo, start, stop):
                c = k * PW + oc * P
                nc.tensor.matmul(dst, whi[:, slot, c:c + P], rhs_hi, start=start, stop=False)
                nc.tensor.matmul(dst, whi[:, slot, c:c + P], rhs_lo, start=False, stop=False)
                return nc.tensor.matmul(dst, wlo[:, slot, c:c + P], rhs_hi, start=False, stop=stop)

            def norm(idx):
                for c in range(KD):
                    pe.wait_ge(sq_ready, idx * KD + (c + 1))
                    for t in range(NT1):
                        last = nc.tensor.matmul(ps[:, 6, t:t + 1], sq[:, c % 2, P * t:P * t + P], ones[:, 0:1],
                                                start=(c == 0 and t == 0), stop=(c == KD - 1),
                                                skip_group_check=True)
                    last.then_inc(sq_used, 1)
                pe.wait_ge(rstd_ready, idx + 1)
                spread(rstd, 0, mean_rows).then_inc(rows_ready, 1)

            def spread(col, at, rows):
                for t in range(NT1):
                    p0, n = tok_tile(t)
                    last = nc.tensor.matmul(rows[:, p0:p0 + n], col[:, at + t:at + t + 1].to_broadcast([P, P]),
                                            ident[:, 0:n], start=True, stop=True)
                return last

            pe.wait_ge(setup_in, n_setup[0])
            for c in range(KD):
                if c >= 4:
                    pe.wait_ge(h_copied, c - 3)
                for t in range(4):
                    last = nc.tensor.transpose(ps[:, c % 4, P * t:P * t + P], x_tok[:, t, P * c:P * c + P], ident)
                last.then_inc(x_turned, 1)
            for c in range(KD):
                last = nc.tensor.transpose(ps[:, 4, N_META * c:N_META * (c + 1)],
                                           meta_tok[:, P * c:P * c + P], ident[0:N_META, 0:N_META])
            last.then_inc(x_turned, 1)
            nc.tensor.transpose(ps[:, 5, 0:103], rows_vec[:, :], ident[0:103, 0:103])
            for l in range(DEPTH):
                nc.tensor.transpose(ps[:, 6, 124 * l:124 * l + 124], rows_conv[:, l, :], ident[0:124, 0:124])
            nc.tensor.transpose(ps[:, 7, 0:P], rows_dn, ident).then_inc(cols_turned, 1)

            with pe.Fori(0, DEPTH) as l:
                first = l * PANELS_L

                def glu_pair(n, glu_at, hn_at):
                    for s in range(2):
                        pe.wait_ge(w_split, n + (s + 3))
                        for j in range(4):
                            oc, half = j // 2, j % 2
                            if glu_at is not None and s == 0:
                                pe.wait_ge(glu_used, glu_at + (j + 1))
                            for k in range(KD):
                                if hn_at is not None and s == 0 and j == 0:
                                    pe.wait_ge(hn_ready, hn_at + (k + 1))
                                last = product(ps[:, 4 * s + j, 0:HALF], s, k, oc,
                                               hn(hn_hi, k, HALF * half, HALF),
                                               hn(hn_lo, k, HALF * half, HALF), k == 0, k == KD - 1)
                            last.then_inc(products_done, 1)

                norm(l * 2)
                glu_pair(first, None, l * 2 * KD)
                glu_pair(first + 2, l * GLUS, None)
                pe.wait_ge(glu_used, l * GLUS + 8)
                f = 0
                for j in range(2):
                    pe.wait_ge(w_split, first + (4 + j + 3))
                    for t in range(NT1):
                        if f >= 6:
                            pe.wait_ge(qkv_copied, l * 26 + (f - 5))
                        for k in range(KD):
                            a = k * T1 + P * t
                            for i, (x, w) in enumerate(((hn_hi, whi), (hn_lo, whi), (hn_hi, wlo))):
                                last = nc.tensor.matmul(ps[:, f % 6, 0:PW], x[:, a:a + P],
                                                        w[:, j % 2, k * PW:(k + 1) * PW],
                                                        start=(k == 0 and i == 0), stop=(k == KD - 1 and i == 2))
                        last.then_inc(products_done, 1)
                        f += 1
                for j in range(4):
                    pe.wait_ge(w_split, first + (6 + j + 3))
                    for oc in range(2):
                        for half in range(2):
                            pe.wait_ge(qkv_copied, l * 26 + (f - 5))
                            for k in range(KD):
                                last = product(ps[:, f % 6, 0:HALF], j % 2, k, oc, hn(hn_hi, k, HALF * half, HALF),
                                               hn(hn_lo, k, HALF * half, HALF), k == 0, k == KD - 1)
                            last.then_inc(products_done, 1)
                            f += 1
                with pe.Fori(0, HEADS1) as hd:
                    it = l * HEADS1 + hd
                    pe.wait_ge(qkv_copied, l * 26 + 26)
                    for i in range(2):
                        for half in range(2):
                            last = nc.tensor.matmul(ps[:, 2 * i + half, 0:HALF], rot,
                                                    qk_raw[:, ds(hd + 4 * i, 1), HALF * half:HALF * (half + 1)]
                                                    .rearrange(flat), start=True, stop=True)
                        last.then_inc(rot_done, 1)
                    pe.wait_ge(rope_done, it * 2 + 2)

                    def scores(t):
                        p0, n = tok_tile(t)
                        if t == 4:
                            pe.wait_ge(exp_done, it * NT1 + 4)
                        elif t >= 2:
                            pe.wait_ge(exp_done, it * NT1 + (t - 1))
                        keys = min(P * (t + 1), T1)
                        for c in range(2):
                            for b, a in enumerate(range(0, keys, 512)):
                                w = min(512, keys - a)
                                bank = 2 * (t % 2) + c if t < 4 else 2 * c + b
                                last = nc.tensor.matmul(ps[:, bank, 0:w], q_head[64 * c:64 * c + 64, p0:p0 + P],
                                                        k_head[64 * c:64 * c + 64, a:a + w], start=True, stop=True)
                        last.then_inc(scored, 1)

                    scores(0)
                    scores(1)
                    for t in range(NT1):
                        n = tok_tile(t)[1]
                        pe.wait_ge(diff_ready, it * NT1 + (t + 1))
                        if t >= 2:
                            pe.wait_ge(diff_t_ready, it * NT1 + (t - 1 if t < 4 else t))
                        for b, (a, _) in enumerate(key_blocks(t)):
                            at = 512 * (4 + t % 2) + P * b
                            last = nc.tensor.transpose(line[:, at:at + P], diff[:, t % 2, a:a + P], ident)
                        last.then_inc(diff_turned, 1)
                        if t + 2 < NT1:
                            scores(t + 2)
                        if t == 0:
                            pe.wait_ge(vh_ready, it + 1)
                        pe.wait_ge(diff_t_ready, it * NT1 + (t + 1))
                        if t >= 2:
                            pe.wait_ge(o_copied, it * NT1 + (t - 1))
                        blocks = key_blocks(t)
                        for b, (_, w) in enumerate(blocks):
                            last = nc.tensor.matmul(ps[:, 6 + t % 2, 0:n], v_head[0:w, b, :],
                                                    diff_t[0:w, t % 2, b * n:b * n + n],
                                                    start=(b == 0), stop=(b == len(blocks) - 1))
                        last.then_inc(pv_done, 1)
                    pe.wait_ge(exp_done, it * NT1 + NT1)
                    pe.wait_ge(o_copied, it * NT1 + NT1)
                for hd in range(HEADS1):
                    pe.wait_ge(sub_sq, l * 4 + (hd + 1))
                    for t in range(NT1):
                        last = nc.tensor.matmul(ps[:, 6, NT1 * hd + t:NT1 * hd + t + 1], sq[:, hd % 2, P * t:P * t + P],
                                                ones[:, 0:1], start=True, stop=True)
                    last.then_inc(sub_stat, 1)
                pe.wait_ge(sub_rstd, l + 1)
                for hd in range(HEADS1):
                    if hd >= 2:
                        pe.wait_ge(sub_t, l * 4 + (hd - 1))
                    spread(rstd, NT1 * hd, line[:, 1024 * (hd % 2):1024 * (hd % 2) + T1]).then_inc(sub_rows, 1)
                pe.wait_ge(conv_done, l * 4 + 4)
                for t in range(NT1):
                    for c in range(4):
                        last = nc.tensor.matmul(ps[:, 6, t:t + 1], conv[:, c * T1 + P * t:c * T1 + P * t + P],
                                                ones[:, 0:1], start=(t == 0 and c == 0), stop=(c == 3),
                                                skip_group_check=True)
                last.then_inc(ln_sum, 1)
                pe.wait_ge(ln_mean, l + 1)
                spread(rms, 0, mean_rows).then_inc(ln_mean_rows, 1)
                for c in range(4):
                    pe.wait_ge(ln_sq, l * 4 + (c + 1))
                    for t in range(NT1):
                        last = nc.tensor.matmul(ps[:, 6, t:t + 1], sq[:, c % 2, P * t:P * t + P], ones[:, 0:1],
                                                start=(t == 0 and c == 0), stop=(c == 3), skip_group_check=True)
                    last.then_inc(ln_stat, 1)
                pe.wait_ge(ln_rstd, l + 1)
                spread(rstd, 0, mean_rows).then_inc(ln_rows, 1)
                f = 0
                for j in range(4):
                    pe.wait_ge(w_split, first + (10 + j + 3))
                    for oc in range(2):
                        for half in range(2):
                            if f >= 8:
                                pe.wait_ge(h_added, l * ADDS + (f - 7))
                            for k in range(KD):
                                if f == 0:
                                    pe.wait_ge(mix_ready, l * KD + (k + 1))
                                last = product(ps[:, f % 8, 0:HALF], j % 2, k, oc, hn(hn_hi, k, HALF * half, HALF),
                                               hn(hn_lo, k, HALF * half, HALF), k == 0, k == KD - 1)
                            last.then_inc(products_done, 1)
                            f += 1
                norm(l * 2 + 1)
                at, glu_at = 14, 8
                for part, n in enumerate(FC):
                    with pe.Fori(0, n // 2) as i:
                        if part:
                            pe.wait_ge(h_added, l * ADDS + 32)
                        else:
                            pe.wait_ge(hn_ready, l * (2 * KD) + 2 * KD)
                        glu_pair(first + at + i * 2, l * GLUS + i * 4 + (glu_at - 4), None)
                    at += n
                    glu_at += 2 * n
                    with pe.Fori(0, 2) as bb:
                        pe.wait_ge(ff_ready, l * FFS + (sum(FC[:part + 1]) * 2 + 4))
                        for b in range(2):
                            for s in range(2):
                                pe.wait_ge(w_split, first + at + bb * 4 + (2 * b + s + 3))
                                for j in range(4):
                                    oc, half = j // 2, j % 2
                                    if s == 0:
                                        pe.wait_ge(h_added, l * ADDS + bb * 8 + (16 * part + 4 * b + j + 9))
                                    for k in range(n // 2):
                                        kf = s * n // 2 + k
                                        a = HALF * half
                                        last = product(ps[:, 4 * b + j, 0:HALF], s, k, oc, ff_hi[:, kf, a:a + HALF],
                                                       ff_lo[:, kf, a:a + HALF], kf == 0, kf == n - 1)
                                    if s == 1 or j == 3:
                                        last.then_inc(products_done, 1)
                    at += 8
            def norm2(idx):
                for c in range(KD):
                    pe.wait_ge(sq_ready, idx * KD + (c + 1))
                    for t in range(NT2):
                        last = nc.tensor.matmul(ps[:, 6, t:t + 1], sq[:, c % 2, tile(t)], ones[:, 0:1],
                                                start=(c == 0 and t == 0), stop=(c == KD - 1), skip_group_check=True)
                    last.then_inc(sq_used, 1)
                pe.wait_ge(rstd_ready, idx + 1)
                spread2(rstd, 0, 4).then_inc(rows_ready, 1)

            def spread2(col, at, bank):
                for t in range(NT2):
                    last = nc.tensor.matmul(ps[:, bank, tile(t)], col[:, at + t:at + t + 1].to_broadcast([P, P]), ident,
                                            start=True, stop=True)
                return last

            def column_sums(c, at, bank=6):
                for t in range(NT2):
                    last = nc.tensor.matmul(ps[:, bank, at + t:at + t + 1], sq[:, c % 2, tile(t)], ones[:, 0:1],
                                            start=True, stop=True)
                return last

            def fill(bank, slot, oc, hi, lo):
                for k in range(KD):
                    last = product(ps[:, bank, :], slot, k, oc, hx(hi, k, 0, SEQ), hx(lo, k, 0, SEQ), k == 0, k == KD - 1)
                return last.then_inc(products_done, 1)

            norm2(M0)
            norm2(M0 + 1)
            pe.wait_ge(ws_ready, 1)
            pe.wait_ge(hn_ready, (M0 + 1) * KD)
            for t in range(NT2):
                for k in range(KD):
                    for i, (x, w) in enumerate(((hn_hi, ws_hi), (hn_lo, ws_hi), (hn_hi, ws_lo))):
                        last = nc.tensor.matmul(ps[:, 5, 64 * t:64 * t + 64], hx(x, k, P * t, P), w[:, 64 * k:64 * k + 64],
                                                start=(k == 0 and i == 0), stop=(k == KD - 1 and i == 2))
            last.then_inc(small_done, 1)
            with pe.Fori(0, PN_Z // 2) as i:
                for f in range(4):
                    if f % 2 == 0:
                        pe.wait_ge(w_split, i * 2 + (N0 + f // 2 + 3))
                    pe.wait_ge(qkv_copied, i * 4 + (Q0 + f - 3))
                    fill(f, f // 2, f % 2, hn_hi, hn_lo)
            pe.wait_ge(g_ready, 1)
            g = g_log.rearrange(flat)
            nc.tensor.matmul(ps[:, 5, 0:32], tri, g, start=True, stop=True)
            nc.tensor.matmul(ps[:, 5, 32:64], blk, g, start=True, stop=True).then_inc(gc_done, 1)
            for c in range(16):
                pe.wait_ge(l2_sq, c + 1)
                column_sums(c, NT2 * c).then_inc(l2_stat, 1)
            with pe.Fori(0, 2) as hg:
                with pe.Fori(0, NT2) as t:
                    it = hg * NT2 + t
                    pe.wait_ge(cur_ready, it + 1)
                    for bank, kind in enumerate((1, 0, 2, 3)):
                        for hh in range(HG):
                            last = nc.tensor.matmul(ps[:, bank, tile(hh)],
                                                    cur[:, kind, hh:hh + 1].to_broadcast([P, P]), ident, start=True, stop=True)
                    last.then_inc(drows_done, 1)
                    pe.wait_ge(dv_ready, it + 1)
                    for hh in range(HG):
                        nc.tensor.transpose(ps[:, 5, tile(hh)], dv_t[:, hh, :], ident)
                    pe.wait_ge(dk_ready, it + 1)
                    for hh in range(HG):
                        last = nc.tensor.transpose(ps[:, 4, tile(hh)], dk_t[:, hh, :], ident)
                    last.then_inc(dturned, 1)
                    for hh in range(HG):
                        nc.tensor.matmul(ps[:, 6, tile(hh)], dk_t[:, hh, :], dkb_t[:, hh, :], start=True, stop=True)
                        last = nc.tensor.matmul(ps[:, 7, tile(hh)], dk_t[:, hh, :], dq_t[:, hh, :], start=True, stop=True)
                    last.then_inc(dkk_done, 1)
                    pe.wait_ge(da_ready, it + 1)
                    for n in range(LEVELS):
                        for pair in range(2):
                            if n:
                                pe.wait_ge(dx_ready, it * (2 * LEVELS) + (2 * n - 1 + pair))
                            for j in range(2):
                                hh = 2 * pair + j
                                last = nc.tensor.matmul(ps[:, pair, tile(j)], da_t[:, hh, :], dx[:, hh, :] if n else ident,
                                                        start=True, stop=True)
                            last.then_inc(p1_done, 1)
                        for pair in range(2):
                            pe.wait_ge(dp_ready, it * (2 * LEVELS) + (2 * n + 1 + pair))
                            for j in range(2):
                                hh = 2 * pair + j
                                if 0 < n < LEVELS - 1:
                                    nc.tensor.matmul(ps[:, 2 + pair, tile(j)], dx_t[:, hh, :], dp[:, hh, :],
                                                     start=True, stop=True)
                                last = nc.tensor.matmul(ps[:, 2 + pair, tile(2 + j)], dp[:, hh, :],
                                                        dx_t[:, hh, :] if n else ident, start=True, stop=True)
                            last.then_inc(delta_done, 1)
                    pe.wait_ge(dx_ready, it * (2 * LEVELS) + 2 * LEVELS)
                    for hh in range(HG):
                        last = nc.tensor.matmul(ps[:, 0, tile(hh)], dkbg[:, hh, :], dx_t[:, hh, :], start=True, stop=True)
                    last.then_inc(dw_done, 1)
                    pe.wait_ge(dqd_ready, it + 1)
                    for ch in range(2):
                        r = slice(CHUNK * ch, CHUNK * (ch + 1))
                        if ch == 0:
                            pe.wait_ge(dw_ready, it + 1)
                        else:
                            pe.wait_ge(state_ready, it * 2 + 1)
                        for hh in range(HG):
                            nc.tensor.matmul(ps[r, 4 + ch, tile(hh)], dw_t[:, hh, r], state[:, hh, :], start=True, stop=False)
                            last = nc.tensor.matmul(ps[r, 4 + ch, tile(hh)], dx_t[r, hh, r], dvb[r, hh, :],
                                                    start=False, stop=True)
                        last.then_inc(vn_done, 1)
                        for hh in range(HG):
                            c = P * hh + CHUNK * ch
                            nc.tensor.matmul(ps[:, 6, c:c + CHUNK], state[:, hh, :], dqd_t[:, hh, r],
                                             start=(ch == 0 and hh == 0), stop=False, skip_group_check=True)
                        pe.wait_ge(vn_ready, it * 2 + (ch + 1))
                        for hh in range(HG):
                            nc.tensor.matmul(ps[:, 7, tile(hh)], dke[r, hh, :], dvn[r, hh, :], start=True, stop=True)
                        for hh in range(HG):
                            c = P * hh + CHUNK * ch
                            last = nc.tensor.matmul(ps[:, 6, c:c + CHUNK], dvn[r, hh, :], dqk_t[r, hh, r],
                                                    start=False, stop=True, skip_group_check=True)
                        last.then_inc(s_done, 1)
            for c in range(DN_HEADS):
                pe.wait_ge(odn_sq, c + 1)
                column_sums(c, NT2 * c, 5).then_inc(odn_stat, 1)
            pe.wait_ge(odn_rstd, 1)
            for c in range(DN_HEADS):
                if c >= 2:
                    pe.wait_ge(odn_normed, c - 1)
                spread2(rstd, NT2 * c, 6 + c % 2).then_inc(odn_rows, 1)
                if c % 2 == 0:
                    pe.wait_ge(w_split, N0 + PN_Z + c // 2 + 3)
                if c >= 4:
                    pe.wait_ge(z_copied, c - 3)
                fill(c % 4, c // 2 % 2, c % 2, hn_hi, hn_lo)
            pe.wait_ge(z_copied, DN_HEADS)
            pe.wait_ge(odn_normed, DN_HEADS)
            f = 0
            items = 0

            def head_sums():
                nonlocal items
                pe.wait_ge(n_sq, items + 1)
                for t in range(NT2):
                    c = 2 * (NT2 * items + t)
                    last = nc.tensor.matmul(ps[:, 6, c:c + 2], sq[:, items % 2, tile(t)], halves, start=True, stop=True)
                last.then_inc(n_stat, 1)
                items += 1

            for pn in range(PN_NQ, PN_VS):
                pe.wait_ge(w_split, N0 + pn + 3)
                for oc in range(2):
                    if f >= 4:
                        pe.wait_ge(nsa_copied, f - 3)
                    fill(f % 4, pn % 2, oc, hn_hi, hn_lo)
                    f += 1
                    if 2 <= f <= 9 or f >= 13:
                        head_sums()

            def head_rows_of(m):
                if m >= 2:
                    pe.wait_ge(n_scaled, m - 1)
                for t in range(NT2):
                    for i in range(2):
                        c = 2 * (NT2 * m + t) + i
                        last = nc.tensor.matmul(ps[HD * i:HD * (i + 1), 4 + m % 2, tile(t)],
                                                n_rstd[:, c:c + 1].to_broadcast([P, HD]), ident, start=True, stop=True)
                last.then_inc(n_rows, 1)

            for j in range(2):
                pe.wait_ge(w_split, N0 + PN_VS + j + 3)
                for t in range(NT2):
                    pe.wait_ge(nsa_copied, f - 3)
                    for k in range(KD):
                        for i, (x, w) in enumerate(((hn_hi, whi), (hn_lo, whi), (hn_hi, wlo))):
                            last = nc.tensor.matmul(ps[:, f % 4, 0:PW], hx(x, k, P * t, P),
                                                    w[:, (PN_VS + j) % 2, k * PW:(k + 1) * PW],
                                                    start=(k == 0 and i == 0), stop=(k == KD - 1 and i == 2))
                    last.then_inc(products_done, 1)
                    f += 1
                    if j == 0 and t < 12 - 10:
                        head_sums()
                    if j == 1:
                        if t == 0:
                            pe.wait_ge(n_rstd_ready, 1)
                        for m in range(3 * t, 3 * t + 3):
                            head_rows_of(m)

            def hidden(pos):
                for m in range(16):
                    nc.tensor.matmul(ps[:, 7, 0:GROUPS * N_CMP], w1[:, m, :],
                                     kcmp[:, :, 2 * m:2 * m + 16 * (N_CMP - 1) + 1:16], start=(m == 0), stop=(m == 15))
                for m in range(16):
                    last = nc.tensor.matmul(ps[:, 7, 256:257], w1[:, m, :], dn_cols[:, pos + m:pos + m + 1],
                                            start=(m == 0), stop=(m == 15))
                last.then_inc(hidden_done, 1)

            pe.wait_ge(w1_in, 16)
            pe.wait_ge(nsa_copied, 10)
            hidden(96)
            pe.wait_ge(w_split, N0 + PN_VC + 3)
            for oc in range(2):
                pe.wait_ge(nsa_copied, f - 3)
                fill(f % 4, PN_VC % 2, oc, hn_hi, hn_lo)
                f += 1
                if oc == 0:
                    pe.wait_ge(gelu_ready, 1)
                    nc.tensor.matmul(ps[:, 7, P:2 * P], w2k, c_gelu, start=True, stop=True).then_inc(kc_done, 1)
            pe.wait_ge(kc_sq, 1)
            nc.tensor.matmul(ps[:, 6, 96:97], sq[:, 0, 0:P], halves[:, 0:1], start=True, stop=True).then_inc(kc_stat, 1)
            pe.wait_ge(w1_in, 32)
            pe.wait_ge(nsa_copied, f)
            hidden(112)
            pe.wait_ge(kc_rstd, 1)
            nc.tensor.matmul(ps[:, 5, 0:P], n_rstd[:, 96:97].to_broadcast([P, P]), ident, start=True, stop=True
                             ).then_inc(kc_rows, 1)
            pe.wait_ge(gelu_ready, 2)
            for g in range(GROUPS):
                for r in range(REP):
                    last = nc.tensor.matmul(ps[32 * r:32 * r + 32, 4, HD * g:HD * (g + 1)],
                                            c_gelu[:, N_CMP * g:N_CMP * g + 32], w2v, start=True, stop=True)
            last.then_inc(vc_done, 1)
            pe.wait_ge(kc_ready, 1)
            pe.wait_ge(vc_ready, 1)
            with pe.Fori(0, GROUPS) as g:
                def query(t, r):
                    hp = HD * (r % 2)
                    return slice(hp, hp + HD), q_grp[hp:hp + HD, r // 2, tile(t)]

                def selected_scores(t):
                    if t == 0:
                        pe.wait_ge(kg_ready, g + 1)
                    else:
                        pe.wait_ge(tops_ready, g * (2 * NT2) + 2 * t)
                    for r in range(REP):
                        rows, q = query(t, r)
                        last = nc.tensor.matmul(ps[:, r, 0:P * (t + 1)], q, k_grp[rows, 0, 0:P * (t + 1)],
                                                start=True, stop=True)
                        last.then_inc(slc_scored, 1)

                def window_scores(t):
                    for r in range(REP):
                        rows, q = query(t, r)
                        a, w = first_key(t), P * (t + 1) - first_key(t)
                        pe.wait_ge(slc_read, g * (REP * NT2) + (REP * t + r + 1))
                        nc.tensor.matmul(ps[:, r, 0:w], q, k_grp[rows, 1, a:a + w], start=True, stop=True)
                        last = nc.tensor.matmul(ps[:, r, SEQ - P:SEQ - P + N_CMP], q, kc_grp[rows, :], start=True, stop=True)
                        last.then_inc(win_scored, 1)

                def outputs(t, part):
                    n = sum(BLOCKS[:t])
                    slot = t % 2
                    blocks = [(p_slc[slot], 0, b, P * b) for b in range(t + 1)]
                    blocks += [(p_win[slot], 1, first_key(t) // P + b, P * b) for b in range(min(t + 1, 3))]
                    blocks.append((p_cmp[slot], None, None, 0))

                    def turn(i):
                        p, branch, b, at = blocks[i]
                        if n + i >= 2:
                            pe.wait_ge(p_t_ready, g * BLOCKS_G + (n + i - 1))
                        if branch is None:
                            last = nc.tensor.transpose(ps[:, 4 + (n + i) % 2, 0:P], p.rearrange(flat), ident)
                        else:
                            for r in range(REP):
                                last = nc.tensor.transpose(ps[:, 4 + (n + i) % 2, tile(r)], p[:, r, at:at + P], ident)
                        last.then_inc(p_turned, 1)

                    own = range(0, t + 1) if part == 0 else range(t + 1, len(blocks))
                    pe.wait_ge(p_ready, g * (2 * NT2) + (2 * t + part + 1))
                    if t == 0 and part == 0:
                        pe.wait_ge(vg_ready, g + 1)
                    turn(own[0])
                    for i in own:
                        p, branch, b, at = blocks[i]
                        if i + 1 in own:
                            turn(i + 1)
                        pe.wait_ge(p_t_ready, g * BLOCKS_G + (n + i + 1))
                        if branch is None:
                            last = nc.tensor.matmul(ps[0:HD, 6, :], vc_grp, pc_t, start=False, stop=True, skip_group_check=True)
                        else:
                            last = nc.tensor.matmul(ps[0:HD, 6, :], v_grp[:, branch, b, :], p_t[:, (n + i) % 2, :],
                                                    start=(i == 0), stop=False, skip_group_check=True)
                        last.then_inc(pv2_done, 1)

                selected_scores(0)
                window_scores(0)
                for t in range(NT2):
                    if t + 1 < NT2:
                        selected_scores(t + 1)
                    outputs(t, 0)
                    if t + 1 < NT2:
                        window_scores(t + 1)
                    outputs(t, 1)
                pe.wait_ge(att_copied, g * NT2 + NT2)
            for at, ready in ((PN_MDN, 0), (PN_MNS, KD)):
                for j in range(4):
                    b = 4 * (j % 2)
                    pairs = (at - PN_MDN) // 2 + j
                    pe.wait_ge(w_split, N0 + at + 2 * j + 3)
                    if pairs >= 2:
                        pe.wait_ge(merged_part, 2 * pairs - 2)
                    else:
                        pe.wait_ge(att_copied, GROUPS * NT2)
                    for oc in range(2):
                        fill(b + oc, 0, oc, hn_hi, hn_lo)
                    pe.wait_ge(w_split, N0 + at + 2 * j + 4)
                    if j == 0:
                        pe.wait_ge(o_ready, ready + KD)
                    for oc in range(2):
                        fill(b + 2 + oc, 1, oc, o_hi.rearrange(flat), o_lo.rearrange(flat))
            pe.wait_ge(merged_part, 16)
            for f in range(KD):
                if f % 2 == 0:
                    pe.wait_ge(w_split, N0 + PN_WO + f // 2 + 3)
                for k in range(KD):
                    if f == 0:
                        pe.wait_ge(merged_ready, k + 1)
                    last = product(ps[:, f, :], f // 2 % 2, k, f % 2, hx(hn_hi, k, 0, SEQ), hx(hn_lo, k, 0, SEQ),
                                   k == 0, k == KD - 1)
                last.then_inc(products_done, 1)
            pe.wait_ge(x2_added, KD)
            norm2(M0 + 2)
            for part in range(2):
                with pe.Fori(0, 4) as i:
                    for f in range(4):
                        if part == 0 and f == 0:
                            pe.wait_ge(hn_ready, (M0 + 2) * KD)
                        if f % 2 == 0:
                            pe.wait_ge(w_split, i * 2 + (N0 + PN_UP[part] + f // 2 + 3))
                        if part:
                            pe.wait_ge(x2_added, 2 * KD)
                        pe.wait_ge(relu_sq_ready, i * 4 + (16 * part + f + 1))
                        fill(f, f // 2, f % 2, hn_hi, hn_lo)
                pe.wait_ge(relu_sq_ready, 16 * part + 20)
                def down(panel_at, slot, first, kf):
                    pe.wait_ge(w_split, panel_at + 3)
                    for kk in range(2):
                        x_hi = f_hi[:, kf(kk), :].rearrange(flat)
                        x_lo = f_lo[:, kf(kk), :].rearrange(flat)
                        for c in range(KD):
                            w0 = D * kk + P * c
                            for j, (w, x) in enumerate(((whi, x_hi), (whi, x_lo), (wlo, x_hi))):
                                last = nc.tensor.matmul(ps[:, c, :], w[:, slot, w0:w0 + P], x,
                                                        start=(first and kk == 0 and j == 0), stop=False,
                                                        skip_group_check=True)
                    last.then_inc(products_done, 1)

                pe.wait_ge(f_ready, 16 * part + 16 + 2)
                first_panel = N0 + PN_DN[part]
                for s in range(2):
                    down(first_panel + s, s, s == 0, lambda kk: slice(2 * s + kk, 2 * s + kk + 1))
                with pe.Fori(1, 4) as i:
                    for s in range(2):
                        down(i * 2 + (first_panel + s), s, False, lambda kk: ds(i * 4 + (2 * s + kk), 1))
            for c in range(KD):
                pe.wait_ge(x2_added, 2 * KD + c + 1)
                for t in range(NT2):
                    last = nc.tensor.transpose(ps[:, c, tile(t)], x2[:, c, tile(t)], ident)
                last.then_inc(y_turned, 1)

        @block.scalar
        def _(act):
            def upper(n, use, slot, used):
                act.wait_ge(raw_in[slot], use * 16 + 16)
                if used is not None:
                    act.wait_ge(products_done, used)
                nc.scalar.copy(whi[:, slot, :], wraw[:, slot, :]).then_inc(w_hi, 1)

            def norm(idx, src, ready):
                for c in range(KD):
                    if c >= 2:
                        act.wait_ge(sq_used, idx * KD + (c - 1))
                    nc.scalar.activation(sq[:, c % 2, 0:T1], src(c), ACT.Square).then_inc(sq_ready, 1)
                act.wait_ge(sq_used, idx * KD + KD)
                nc.scalar.activation(rms[:, 0:NT1], ps[:, 6, 0:NT1], ACT.Sqrt, bias=eps5,
                                     scale=1.0 / D).then_inc(rms_ready, 1)
                if ready:
                    for c in range(KD):
                        act.wait_ge(t_ready, idx * KD + (c + 1))
                        nc.scalar.copy(hn(hn_hi, c, 0, T1), t_chunk[:, c % 2, :]).then_inc(hi_ready, 1)

            act.wait_ge(lam_dots, 1)
            nc.scalar.activation(lam_exp, lam_dot, ACT.Exp).then_inc(lam_exps, 1)
            for s in range(2):
                upper(None, 0, s, None)

            with act.Fori(0, DEPTH) as l:
                use0 = l * (PANELS_L // 2)
                ev = l * EVENTS

                def chunk(c):
                    return h[:, c, :]

                act.wait_ge(h_ready, l + 1)
                norm(l * 2, chunk, True)
                for p in range(2):
                    for j in range(4):
                        act.wait_ge(products_done, ev + (EV_GLU + 8 * p + j + 1))
                        nc.scalar.activation(glu_gate[:, j, :], ps[:, j, 0:HALF], ACT.Sigmoid,
                                             bias=lay[:, VEC["gate_bias"] + 2 * p + j // 2:][:, 0:1]
                                             ).then_inc(gate_act, 1)
                    upper(None, use0 + (p + 1), 0, ev + (EV_GLU + 8 * p + 4))
                    upper(None, use0 + (p + 1), 1, ev + (EV_GLU + 8 * p + 8))
                f = 0
                for j in range(2):
                    for t in range(NT1):
                        n = tok_tile(t)[1]
                        act.wait_ge(products_done, ev + (EV_V + f + 1))
                        nc.scalar.copy(v_tok[0:n, t, PW * j:PW * (j + 1)], ps[0:n, f % 6, 0:PW]).then_inc(qkv_copied, 1)
                        f += 1
                    upper(None, use0 + 3, j, ev + (EV_V + f))
                for j in range(4):
                    for oc in range(2):
                        for half in range(2):
                            act.wait_ge(products_done, ev + (EV_V + f + 1))
                            nc.scalar.copy(qk_raw[:, 2 * j + oc, HALF * half:HALF * (half + 1)],
                                           ps[:, f % 6, 0:HALF]).then_inc(qkv_copied, 1)
                            f += 1
                    upper(None, use0 + (4 + j // 2), j % 2, ev + (EV_V + f))
                with act.Fori(0, HEADS1) as hd:
                    it = l * HEADS1 + hd

                    def exponentials(t):
                        n = tok_tile(t)[1]
                        keys = min(P * (t + 1), T1)
                        act.wait_ge(max_ready, it * NT1 + (t + 1))
                        if t >= 2:
                            act.wait_ge(diff_ready, it * NT1 + (t - 1))
                        s = scores_of(t)
                        for c in range(2):
                            last = nc.scalar.activation(probs4[0:n, t % 2, c, 0:keys], s[:, c, :], ACT.Exp,
                                                        bias=neg_top[0:n, t % 2, c:c + 1], scale=0.125,
                                                        accum_out=mass[0:n, t % 2, c:c + 1])
                        last.then_inc(exp_done, 1)

                    exponentials(0)
                    for t in range(NT1):
                        p0, n = tok_tile(t)
                        if t + 1 < NT1:
                            exponentials(t + 1)
                        act.wait_ge(diff_turned, it * NT1 + (t + 1))
                        if t >= 2:
                            act.wait_ge(pv_done, it * NT1 + (t - 1))
                        w = n * len(key_blocks(t))
                        at = 512 * (4 + t % 2)
                        turned = line[:, at:at + P * len(key_blocks(t))].rearrange("p (b n) -> p b n", n=P)
                        nc.scalar.copy(diff_t[:, t % 2, 0:w].rearrange("p (b n) -> p b n", n=n),
                                       turned[:, :, 0:n]).then_inc(diff_t_ready, 1)
                        act.wait_ge(pv_done, it * NT1 + (t + 1))
                        nc.scalar.copy(o_raw[:, ds(hd, 1), p0:p0 + n].rearrange(flat),
                                       ps[:, 6 + t % 2, 0:n]).then_inc(o_copied, 1)
                act.drain()
                for hd in range(HEADS1):
                    if hd >= 2:
                        act.wait_ge(sub_stat, l * 4 + (hd - 1))
                    nc.scalar.activation(sq[:, hd % 2, 0:T1], o_raw[:, hd, :], ACT.Square).then_inc(sub_sq, 1)
                act.wait_ge(sub_stat, l * 4 + 4)
                nc.scalar.activation(rms[:, 0:4 * NT1], ps[:, 6, 0:4 * NT1], ACT.Sqrt, bias=eps5,
                                     scale=1.0 / P).then_inc(sub_rms, 1)
                for c in range(4):
                    act.wait_ge(ln_centred, l * 4 + (c + 1))
                    if c >= 2:
                        act.wait_ge(ln_stat, l * 4 + (c - 1))
                    nc.scalar.activation(sq[:, c % 2, 0:T1], conv[:, c * T1:(c + 1) * T1],
                                         ACT.Square).then_inc(ln_sq, 1)
                act.wait_ge(ln_stat, l * 4 + 4)
                nc.scalar.activation(rms[:, 0:NT1], ps[:, 6, 0:NT1], ACT.Sqrt, bias=eps5,
                                     scale=1.0 / 512).then_inc(ln_rms, 1)
                for c in range(4):
                    act.wait_ge(ln_t, l * 4 + (c + 1))
                    nc.scalar.activation(conv[:, c * T1:(c + 1) * T1], conv[:, c * T1:(c + 1) * T1], ACT.Silu,
                                         bias=lay[:, VEC["ln_b"] + c:][:, 0:1],
                                         scale=lay[:, VEC["ln_g"] + c:][:, 0:1]).then_inc(ln_silu, 1)
                for j in range(4):
                    upper(None, use0 + (6 + j // 2), j % 2, ev + (EV_OUT + 4 * j + 4))
                act.wait_ge(h_added, l * ADDS + 16)
                norm(l * 2 + 1, chunk, True)
                use, glu_at = 7, 8
                for part, n in enumerate(FC):
                    with act.Fori(0, n // 2) as i:
                        e = ev + EV_FF[part] + i * 8
                        for j in range(4):
                            act.wait_ge(products_done, e + (j + 1))
                            nc.scalar.activation(glu_gate[:, j, :], ps[:, j, 0:HALF], ACT.Silu).then_inc(gate_act, 1)
                        for s in range(2):
                            upper(None, use0 + use + i + 1, s, e + (4 * s + 4))
                    use += n // 2
                    with act.Fori(0, 4) as b:
                        e = ev + EV_DOWN[part] + b * 5
                        if part == 0:
                            for s in range(2):
                                upper(None, use0 + use + b + 1, s, e + (4 * s + 1))
                        else:
                            for s in range(2):
                                upper(None, use0 + use + b + 1, s, e + (4 * s + 1))
                    use += 4
            def follow(pn, event):
                n = N0 + pn + 2
                upper(None, n // 2, n % 2, E0 + event)

            def square(c, src, ready):
                nc.scalar.activation(sq[:, c % 2, 0:SEQ], src, ACT.Square).then_inc(ready, 1)

            def norm2(idx, src, eps, split):
                for c in range(KD):
                    if c >= 2:
                        act.wait_ge(sq_used, idx * KD + (c - 1))
                    src_ready, value = src(c)
                    act.wait_ge(*src_ready)
                    square(c, value, sq_ready)
                act.wait_ge(sq_used, idx * KD + KD)
                nc.scalar.activation(rms[:, 0:NT2], ps[:, 6, 0:NT2], ACT.Sqrt, bias=eps, scale=1.0 / D
                                     ).then_inc(rms_ready, 1)
                if split is not None:
                    for c in range(KD):
                        act.wait_ge(t_ready, split * KD + (c + 1))
                        nc.scalar.copy(hx(hn_hi, c, 0, SEQ), t2[:, c % 2, :]).then_inc(hi_ready, 1)

            norm2(M0, lambda c: ((h_ready, X0), h[:, c, N_META:T1]), eps5, None)
            nc.scalar.copy(ws_hi, w_small.rearrange(flat)).then_inc(ws_hi_ready, 1)
            norm2(M0 + 1, lambda c: ((x2_ready, c + 1), x2[:, c, :]), eps6, M0)
            act.wait_ge(small_done, 1)
            small = ps[:, 5, 0:NT2 * 64].rearrange("p (t n) -> p t n", t=NT2)
            nc.scalar.activation(gates, small[:, :, 16:64], ACT.Sigmoid)
            nc.scalar.activation(beta, small[:, :, 0:DN_HEADS], ACT.Sigmoid).then_inc(small_act, 1)
            nc.scalar.activation(a_exp[:, 0, :], head_rows[:, 0, :], ACT.Exp)
            act.wait_ge(a_abs_ready, 1)
            nc.scalar.activation(a_ln.rearrange(flat), a_abs.rearrange(flat), ACT.Exp, scale=-1.0)
            act.drain()
            nc.scalar.activation(a_ln.rearrange(flat), a_ln.rearrange(flat), ACT.Ln, bias=ones[:, 0:1]).then_inc(a_ln_ready, 1)
            with act.Fori(0, PN_Z // 2) as i:
                def swish(f):
                    act.wait_ge(dconv_done, i * 4 + (f + 3))
                    nc.scalar.activation(qkv[:, ds(i * 4 + f, 1), :].rearrange(flat), taps_sum[:, f % 2, :], ACT.Silu
                                         ).then_inc(silu_done, 1)

                for f in range(4):
                    act.wait_ge(products_done, i * 4 + (E0 + f + 1))
                    act.wait_ge(dconv_done, i * 4 + (f + 1))
                    nc.scalar.copy(taps[:, f % 2, 3:], ps[:, f, :]).then_inc(qkv_copied, 1)
                    if f % 2:
                        upper(None, i + (N0 + 2) // 2, f // 2, i * 4 + (E0 + f + 1))
                    if f:
                        swish(f - 1)
                swish(3)
            act.drain()
            for c in range(16):
                if c >= 2:
                    act.wait_ge(l2_stat, c - 1)
                square(c, qkv[:, c, :], l2_sq)
            act.wait_ge(gc_done, 1)
            nc.scalar.copy(g_cum.rearrange(flat), ps[:, 5, 0:32]).then_inc(gc_copied, 1)
            act.wait_ge(l2_stat, 16)
            nc.scalar.activation(l2_rms.rearrange(flat), ps[:, 6, 0:64], ACT.Sqrt, bias=eps6).then_inc(l2_rms_ready, 1)
            act.drain()
            nc.scalar.activation(g_exp.rearrange(flat), g_cum.rearrange(flat), ACT.Exp)
            act.wait_ge(g_rest_ready, 1)
            nc.scalar.activation(ke_exp.rearrange(flat), g_rest.rearrange(flat), ACT.Exp).then_inc(decays_ready, 1)
            with act.Fori(0, 2) as hg:
                with act.Fori(0, NT2) as t:
                    it = hg * NT2 + t
                    nc.scalar.activation(dv_t, qkv[:, ds(hg * HG + 16, HG), ds(t * P, P)], ACT.Copy).then_inc(dv_ready, 1)
                    act.wait_ge(dec_ready, it + 1)
                    nc.scalar.activation(decay, decay, ACT.Exp)
                    nc.scalar.activation(g_rows.rearrange(flat), ps[:, 3, :], ACT.Exp).then_inc(dexp_done, 1)
                    act.wait_ge(dw_done, it + 1)
                    nc.scalar.mul(dw_t, by_head(0), -1.0).then_inc(dw_ready, 1)
                    for ch in range(2):
                        r = slice(CHUNK * ch, CHUNK * (ch + 1))
                        act.wait_ge(vn_done, it * 2 + (ch + 1))
                        nc.scalar.copy(dvn[r, :, :], by_head(4 + ch)[r, :, :]).then_inc(vn_ready, 1)
            act.wait_ge(do_copied, 2 * NT2)
            for c in range(DN_HEADS):
                if c >= 2:
                    act.wait_ge(odn_stat, c - 1)
                square(c, qkv[:, 16 + c, :], odn_sq)
            act.wait_ge(odn_stat, DN_HEADS)
            nc.scalar.activation(rms, ps[:, 5, 0:32], ACT.Sqrt, bias=eps6, scale=1.0 / P).then_inc(odn_rms, 1)
            for c in range(DN_HEADS):
                act.wait_ge(products_done, E0 + EV_Z + c + 1)
                if c >= 2:
                    act.wait_ge(odn_ready, c - 1)
                nc.scalar.activation(z_act[:, c % 2, :], ps[:, c % 4, :], ACT.Silu).then_inc(z_copied, 1)
                if c % 2:
                    follow(PN_Z + c // 2, EV_Z + c + 1)
            f = 0
            items = 0

            def raw_head(dst, bank):
                nonlocal items
                nc.scalar.copy(dst, ps[:, bank, :])
                if items >= 2:
                    act.wait_ge(n_stat, items - 1)
                square(items, ps[:, bank, :], n_sq)
                act.drain().then_inc(nsa_copied, 1)
                items += 1

            def to_compress(bank, oc):
                for i in range(2):
                    src = ps[HD * i:HD * (i + 1), bank, :]
                    nc.scalar.copy(kcmp[0:HD, 2 * oc + i, :], src)
                    nc.scalar.copy(kcmp[HD:P, 2 * oc + i, 0:SEQ - 1], src[:, 1:SEQ])
                act.drain().then_inc(nsa_copied, 1)

            act.wait_ge(odn_ready, DN_HEADS)
            for pn in range(PN_NQ, PN_VS):
                for oc in range(2):
                    act.wait_ge(products_done, E0 + EV_NQ + f + 1)
                    if pn < PN_KC:
                        raw_head(nq[:, f, :], f % 4)
                    elif pn == PN_KC:
                        to_compress(f % 4, oc)
                    else:
                        raw_head(k_raw[:, f - 10, :], f % 4)
                    f += 1
                follow(pn, EV_NQ + f)
            for j, dst in enumerate((vs, vw)):
                for t in range(NT2):
                    act.wait_ge(products_done, E0 + EV_NQ + f + 1)
                    nc.scalar.copy(dst[:, t, :], ps[:, f % 4, 0:PW]).then_inc(nsa_copied, 1)
                    f += 1
                    if j == 0 and t == 2:
                        act.wait_ge(n_stat, 12)
                        nc.scalar.activation(n_rms[:, 0:96], ps[:, 6, 0:96], ACT.Sqrt, bias=eps6, scale=1.0 / HD
                                             ).then_inc(n_rms_ready, 1)
                follow(PN_VS + j, EV_NQ + f)

            def gelu(n):
                act.wait_ge(hidden_done, n)
                nc.scalar.copy(pos_sum, ps[:, 7, 256:257])
                act.drain()
                nc.scalar.activation(c_gelu[:, 0:GROUPS * N_CMP], ps[:, 7, 0:GROUPS * N_CMP], ACT.Gelu_apprx_tanh,
                                     bias=pos_sum)
                act.drain().then_inc(gelu_ready, 1)

            act.wait_ge(n_scaled, 12)
            act.wait_ge(c_pad_ready, 1)
            gelu(1)
            act.wait_ge(products_done, E0 + EV_VC + 1)
            act.wait_ge(hidden_done, 1)
            to_compress(f % 4, 0)
            f += 1
            act.wait_ge(kc_done, 1)
            nc.scalar.copy(kc_raw, ps[:, 7, P:2 * P])
            nc.scalar.activation(
                sq[:, 0, 0:P], ps[:, 7, P:2 * P], ACT.Square)
            act.drain().then_inc(kc_sq, 1)
            act.wait_ge(products_done, E0 + EV_VC + 2)
            to_compress(f % 4, 1)
            f += 1
            follow(PN_VC, EV_VC + 2)
            act.wait_ge(kc_stat, 1)
            nc.scalar.activation(n_rms[:, 96:97], ps[:, 6, 96:97], ACT.Sqrt, bias=eps6, scale=1.0 / HD).then_inc(kc_rms, 1)
            gelu(2)
            act.wait_ge(vc_done, 1)
            nc.scalar.copy(vc, ps[:, 4, 0:PW].rearrange("p (g d) -> p g d", g=GROUPS)).then_inc(vc_ready, 1)
            act.wait_ge(n_scaled, 12)
            with act.Fori(0, GROUPS) as g:
                def exponentials(t, part):
                    slot = t % 2
                    branches = ((0, p_slc[slot], P * (t + 1)), (1, p_win[slot], P * min(t + 1, 3)), (2, p_cmp[slot], N_CMP))
                    act.wait_ge(tops_ready, g * (2 * NT2) + (2 * t + part + 1))
                    for i, p, w in branches[0:1] if part == 0 else branches[1:]:
                        for r in range(REP):
                            nc.scalar.activation(p[:, r, 0:w], p[:, r, 0:w], ACT.Exp, bias=s_neg[:, i, r:r + 1],
                                                 accum_out=s_mass[:, i, r:r + 1])
                    act.drain().then_inc(exps_done, 1)

                def copies(t, part):
                    n, bank = sum(BLOCKS[:t]), 4
                    for i in range(0, t + 1) if part == 0 else range(t + 1, BLOCKS[t]):
                        act.wait_ge(p_turned, g * BLOCKS_G + (n + i + 1))
                        act.wait_ge(pv2_done, g * BLOCKS_G + max(1, n + i))
                        bank = 4 + (n + i) % 2
                        if i < BLOCKS[t] - 1:
                            nc.scalar.copy(p_t[:, (n + i) % 2, :], ps[:, bank, :]).then_inc(p_t_ready, 1)
                        else:
                            for r in range(REP):
                                rows = slice(32 * r, 32 * r + 32)
                                nc.scalar.copy(pc_t[rows, tile(r)], ps[rows, bank, 0:P])
                            act.drain().then_inc(p_t_ready, 1)

                for part in range(2):
                    exponentials(0, part)
                for t in range(NT2):
                    for part in range(2):
                        copies(t, part)
                        if t + 1 < NT2:
                            exponentials(t + 1, part)
            act.wait_ge(att_copied, GROUPS * NT2)

            def split_out(src):
                for c in range(KD):
                    nc.scalar.copy(o_hi[:, c, :], src(c)).then_inc(o_hi_ready, 1)

            split_out(lambda c: qkv[:, 16 + c, :])
            for m, (pn, ev) in enumerate(((PN_MDN, EV_MDN), (PN_MNS, EV_MNS))):
                for j in range(4):
                    b = 4 * (j % 2)
                    for oc in range(2):
                        act.wait_ge(products_done, E0 + ev + 4 * j + oc + 1)
                        if 4 * m + j >= 1:
                            act.wait_ge(merged_part, 2 * (4 * m + j) + oc - 1)
                        nc.scalar.activation(sig[:, oc, :], ps[:, b + oc, :], ACT.Sigmoid).then_inc(sig_ready, 1)
                    follow(pn + 2 * j, ev + 4 * j + 2)
                    follow(pn + 2 * j + 1, ev + 4 * j + 4)
                if m == 0:
                    split_out(lambda c: nq[:, c, :])
            for c in range(KD):
                act.wait_ge(merged_part, KD + c + 1)
                nc.scalar.copy(hx(hn_hi, c, 0, SEQ), merged[:, c, :]).then_inc(merged_hi, 1)
            for j in range(4):
                follow(PN_WO + j, EV_WO + 2 * j + 2)
            norm2(M0 + 2, lambda c: ((x2_added, c + 1), x2[:, c, :]), eps6, M0 + 1)
            for part in range(2):
                with act.Fori(0, 4) as i:
                    for f in range(4):
                        e = i * 4 + (E0 + EV_UP[part] + f + 1)
                        act.wait_ge(products_done, e)
                        act.wait_ge(relu_sq_ready, i * 4 + (16 * part + f + 3))
                        nc.scalar.activation(relu[:, f % 2, :], ps[:, f, :], ACT.Relu).then_inc(relu_ready, 1)
                        if f % 2:
                            upper(None, i + (N0 + PN_UP[part] + 2) // 2, f // 2, e)
                if part == 0:
                    with act.Fori(0, 4) as i:
                        for s in range(2):
                            upper(None, i + (N0 + PN_DN[0] + 2) // 2, s, i * 2 + (E0 + EV_DN[0] + s + 1))
                else:
                    with act.Fori(0, 3) as i:
                        for s in range(2):
                            upper(None, i + (N0 + PN_DN[1] + 2) // 2, s, i * 2 + (E0 + EV_DN[1] + s + 1))
            for c in range(KD):
                act.wait_ge(y_turned, c + 1)
                nc.scalar.copy(y_tok[:, :, P * c:P * (c + 1)], ps[:, c, :].rearrange("p (t n) -> p t n", t=NT2)
                               ).then_inc(y_copied, 1)

        @block.vector
        def _(dve):
            def norm(idx, src, gain, dst=None):
                dve.wait_ge(rms_ready, idx + 1)
                nc.vector.reciprocal(rstd[:, 0:NT1], rms[:, 0:NT1]).then_inc(rstd_ready, 1)
                dve.wait_ge(rows_ready, idx + 1)
                for c in range(KD):
                    if c >= 2:
                        dve.wait_ge(hn_ready, idx * KD + (c - 1))
                    nc.vector.scalar_tensor_tensor(t_chunk[:, c % 2, :], src(c), gain(c), mean_rows,
                                                   ALU.mult, ALU.mult).then_inc(t_ready, 1)

            nc.vector.memset(ones, 1.0)
            nc.vector.memset(sq, 0.0)
            nc.vector.memset(diff, 0.0)
            for x in (hn_hi, hn_lo):
                nc.vector.memset(x[:, KD * T1:].bitcast(F32), 0.0)
            dve.wait_ge(setup_in, n_setup[0])
            for l in range(DEPTH):
                for i in range(2):
                    nc.vector.tensor_tensor_reduce(out=lam_prod[:, 2 * l + i, :], in0=lam_rows[:, 2 * i, 64 * l:64 * l + 64],
                                                   in1=lam_rows[:, 2 * i + 1, 64 * l:64 * l + 64], scale=1.0, scalar=0.0,
                                                   op0=ALU.mult, op1=ALU.add, accum_out=lam_dot[:, 2 * l + i:2 * l + i + 1])
            dve.drain().then_inc(lam_dots, 1)
            for c in range(KD):
                dve.wait_ge(x_turned, c + 1)
                nc.vector.tensor_copy(h[:, c, N_META:T1], ps[:, c % 4, :]).then_inc(h_copied, 1)
            dve.wait_ge(x_turned, KD + 1)
            nc.vector.tensor_copy(h[:, :, 0:N_META],
                                  ps[:, 4, 0:N_META * KD].rearrange("p (c n) -> p c n", c=KD))
            dve.wait_ge(cols_turned, 1)
            nc.vector.tensor_copy(vec_cols, ps[:, 5, 0:103])
            nc.vector.tensor_copy(conv_cols, ps[:, 6, 0:DEPTH * TAPS * 4])
            nc.vector.tensor_copy(dn_cols, ps[:, 7, 0:P])
            dve.wait_ge(lam_exps, 1)
            e = lam_exp.rearrange("p (l i) -> p l i", i=2)
            nc.vector.tensor_tensor(neg_lam, e[:, :, 1], e[:, :, 0], ALU.subtract)
            dve.drain()
            nc.vector.tensor_tensor(neg_lam, neg_lam, lam_init, ALU.subtract)
            dve.drain().then_inc(h_ready, 1)

            with dve.Fori(0, DEPTH) as l:
                ev = l * EVENTS
                nc.vector.tensor_copy(lay, vec_cols[:, ds(l * 37, 37)])
                nc.vector.tensor_copy(lay_conv, conv_cols[:, ds(l * (TAPS * 4), TAPS * 4)])
                nc.vector.tensor_copy(lay_neg_lam, neg_lam[:, ds(l, 1)])
                nc.vector.tensor_copy(weight2[:, 0:1], lam_rest[:, ds(l, 1)])
                dve.drain()
                nc.vector.tensor_tensor(sub_gain, lay[:, VEC["sub"]:VEC["sub"] + 1], weight2[:, 0:1], ALU.mult)
                nc.vector.memset(z[:, :, 0:TAPS - 1], 0.0)
                nc.vector.memset(conv[:, 4 * T1:], 0.0)
                dve.drain()

                def chunk(c):
                    return h[:, c, :]

                norm(l * 2, chunk, lambda c: lay[:, VEC["norm1"] + c:][:, 0:1])
                for p in range(2):
                    for j in range(4):
                        c, half = 2 * p + j // 2, j % 2
                        dve.wait_ge(products_done, ev + (EV_GLU + 8 * p + 4 + j + 1))
                        dve.wait_ge(gate_act, l * GLUS + (4 * p + j + 1))
                        at = TAPS - 1 + HALF * half
                        nc.vector.scalar_tensor_tensor(z[:, c, at:at + HALF], ps[:, 4 + j, 0:HALF],
                                                       lay[:, VEC["a_bias"] + c:][:, 0:1], glu_gate[:, j, :],
                                                       ALU.add, ALU.mult).then_inc(glu_used, 1)
                dve.drain()
                nc.vector.memset(q_head[:, T1:], 0.0)
                for c in range(4):
                    if c:
                        dve.drain()
                    nc.vector.tensor_scalar(conv_acc, z[:, c, 0:T1], lay_conv[:, c:c + 1],
                                            lay[:, VEC["conv_b"] + c:][:, 0:1], ALU.mult, ALU.add)
                    for j in range(1, TAPS):
                        dve.drain()
                        last = nc.vector.scalar_tensor_tensor(
                            conv_acc if j < TAPS - 1 else conv[:, c * T1:(c + 1) * T1], z[:, c, j:j + T1],
                            lay_conv[:, 4 * j + c:4 * j + c + 1], conv_acc, ALU.mult, ALU.add)
                    last.then_inc(conv_done, 1)
                with dve.Fori(0, HEADS1) as hd:
                    it = l * HEADS1 + hd
                    for i, dst in enumerate((q_head, k_head)):
                        dve.wait_ge(rot_done, it * 2 + (i + 1))
                        nc.vector.tensor_tensor(rope_b[:, i, :].rearrange("p (b n) -> p b n", b=2),
                                                ps[:, 2 * i:2 * i + 2, 0:HALF],
                                                sin.rearrange("p (b n) -> p b n", b=2), ALU.mult)
                        dve.drain()
                        dve.wait_ge(rope_a_ready, it * 2 + (i + 1))
                        nc.vector.tensor_tensor(dst[:, 0:T1], rope_a[:, i, :], rope_b[:, i, :], ALU.add).then_inc(rope_done, 1)

                    def maxima(t):
                        n = tok_tile(t)[1]
                        keys = min(P * (t + 1), T1)
                        s = scores_of(t)
                        dve.wait_ge(scored, it * NT1 + (t + 1))
                        own = s[:, :, P * t:keys]
                        nc.vector.tensor_tensor(own, own, causal[0:n, 0:n].unsqueeze(1).to_broadcast([n, 2, n]), ALU.add)
                        dve.drain()
                        nc.vector.reduce_max(top[0:n, t % 2, :], s, AX.X)
                        dve.drain()
                        nc.vector.tensor_scalar(neg_top[0:n, t % 2, :], top[0:n, t % 2, :], -0.125, None,
                                                ALU.mult).then_inc(max_ready, 1)

                    def difference(t):
                        n = tok_tile(t)[1]
                        keys = min(P * (t + 1), T1)
                        dve.wait_ge(exp_done, it * NT1 + (t + 1))
                        nc.vector.reciprocal(weight[0:n, t % 2, :], mass[0:n, t % 2, :])
                        dve.drain()
                        nc.vector.tensor_tensor(weight2[0:n, t % 2:t % 2 + 1], weight[0:n, t % 2, 1:2],
                                                lay_neg_lam[0:n, :], ALU.mult)
                        dve.drain()
                        p2 = probs4[0:n, t % 2, 1, 0:keys]
                        nc.vector.tensor_scalar(p2, p2, weight2[0:n, t % 2:t % 2 + 1], None, ALU.mult)
                        dve.drain()
                        if t >= 2:
                            dve.wait_ge(diff_turned, it * NT1 + (t - 1))
                        nc.vector.scalar_tensor_tensor(diff[0:n, t % 2, 0:keys], probs4[0:n, t % 2, 0, 0:keys],
                                                       weight[0:n, t % 2, 0:1], p2, ALU.mult, ALU.add
                                                       ).then_inc(diff_ready, 1)

                    maxima(0)
                    for t in range(NT1):
                        if t + 1 < NT1:
                            maxima(t + 1)
                        difference(t)
                dve.wait_ge(sub_rms, l + 1)
                nc.vector.reciprocal(rstd[:, 0:4 * NT1], rms[:, 0:4 * NT1]).then_inc(sub_rstd, 1)
                for hd in range(HEADS1):
                    dve.wait_ge(sub_rows, l * 4 + (hd + 1))
                    if hd >= 2:
                        dve.wait_ge(mix_ready, l * KD + (hd - 1))
                    nc.vector.scalar_tensor_tensor(t_chunk[:, hd % 2, :], o_raw[:, hd, :], sub_gain,
                                                   line[:, 1024 * (hd % 2):1024 * (hd % 2) + T1],
                                                   ALU.mult, ALU.mult).then_inc(sub_t, 1)
                    dve.drain()
                    nc.vector.tensor_copy(hn(hn_hi, hd, 0, T1), t_chunk[:, hd % 2, :]).then_inc(mix_hi, 1)
                dve.wait_ge(ln_sum, l + 1)
                nc.vector.tensor_scalar(rms[:, 0:NT1], ps[:, 6, 0:NT1], 1.0 / 512, None, ALU.mult).then_inc(ln_mean, 1)
                dve.wait_ge(ln_mean_rows, l + 1)
                for c in range(4):
                    x = conv[:, c * T1:(c + 1) * T1]
                    nc.vector.tensor_tensor(x, x, mean_rows, ALU.subtract).then_inc(ln_centred, 1)
                dve.wait_ge(ln_rms, l + 1)
                nc.vector.reciprocal(rstd[:, 0:NT1], rms[:, 0:NT1]).then_inc(ln_rstd, 1)
                dve.wait_ge(ln_rows, l + 1)
                for c in range(4):
                    x = conv[:, c * T1:(c + 1) * T1]
                    nc.vector.tensor_tensor(x, x, mean_rows, ALU.mult).then_inc(ln_t, 1)
                for c in range(4):
                    dve.wait_ge(ln_silu, l * 4 + (c + 1))
                    nc.vector.tensor_copy(hn(hn_hi, 4 + c, 0, T1), conv[:, c * T1:(c + 1) * T1]).then_inc(mix_hi, 1)
                for f in range(16):
                    dve.wait_ge(products_done, ev + (EV_OUT + f + 1))
                    x = h[:, f // 2, HALF * (f % 2):HALF * (f % 2 + 1)]
                    nc.vector.tensor_tensor(x, x, ps[:, f % 8, 0:HALF], ALU.add).then_inc(h_added, 1)
                norm(l * 2 + 1, chunk, lambda c: lay[:, VEC["norm2"] + c:][:, 0:1])
                glu_at, ff_at = 8, 0
                for part, n in enumerate(FC):
                    with dve.Fori(0, n // 2) as i:
                        e = ev + EV_FF[part] + i * 8
                        for j in range(4):
                            oc, half = j // 2, j % 2
                            dve.wait_ge(products_done, e + (4 + j + 1))
                            dve.wait_ge(gate_act, l * GLUS + i * 4 + (glu_at + j + 1))
                            dve.wait_ge(ff_ready, l * FFS + i * 4 + (ff_at + j + 1))
                            nc.vector.tensor_tensor(glu_val[:, j, :], ps[:, 4 + j, 0:HALF], glu_gate[:, j, :],
                                                    ALU.mult).then_inc(glu_used, 1)
                            dve.drain()
                            nc.vector.tensor_copy(
                                ff_hi[:, ds(i * 2 + oc, 1), HALF * half:HALF * (half + 1)].rearrange(flat),
                                glu_val[:, j, :]).then_inc(ffv_hi, 1)
                    glu_at += 2 * n
                    ff_at += 2 * n
                    with dve.Fori(0, 2) as bb:
                        for b in range(2):
                            for j in range(4):
                                dve.wait_ge(products_done, ev + EV_DOWN[part] + bb * 10 + (5 * b + 1 + j + 1))
                                x = h[:, ds(bb * 4 + (2 * b + j // 2), 1), HALF * (j % 2):HALF * (j % 2 + 1)].rearrange(flat)
                                nc.vector.tensor_tensor(x, x, ps[:, 4 * b + j, 0:HALF], ALU.add).then_inc(h_added, 1)
                dve.drain().then_inc(h_ready, 1)
            def inverse_rms(idx):
                dve.wait_ge(rms_ready, idx + 1)
                nc.vector.reciprocal(rstd[:, 0:NT2], rms[:, 0:NT2]).then_inc(rstd_ready, 1)
                dve.wait_ge(rows_ready, idx + 1)

            def norm2(idx, split, gain):
                inverse_rms(idx)
                for c in range(KD):
                    if c >= 2:
                        dve.wait_ge(hn_ready, split * KD + (c - 1))
                    nc.vector.scalar_tensor_tensor(t2[:, c % 2, :], x2[:, c, :], col(gain + c), ps[:, 4, :],
                                                   ALU.mult, ALU.mult).then_inc(t_ready, 1)

            inverse_rms(M0)
            for c in range(KD):
                nc.vector.scalar_tensor_tensor(x2[:, c, :], h[:, c, N_META:T1], col(FINAL + c), ps[:, 4, :],
                                               ALU.mult, ALU.mult).then_inc(x2_ready, 1)
            dve.drain()
            norm2(M0 + 1, M0, NORM_MIX)
            dve.wait_ge(small_act, 1)
            small = ps[:, 5, 0:NT2 * 64].rearrange("p (t n) -> p t n", t=NT2)
            nc.vector.tensor_tensor(a_dt, small[:, :, DN_HEADS:2 * DN_HEADS], wide(head_rows[:, 1, :], [P, NT2, DN_HEADS], 1),
                                    ALU.add)
            dve.drain()
            flat_a = a_dt.rearrange(flat)
            nc.vector.scalar_tensor_tensor(a_abs.rearrange(flat), flat_a, -1.0, flat_a, ALU.mult, ALU.max
                                           ).then_inc(a_abs_ready, 1)
            dve.wait_ge(hn_ready, (M0 + 1) * KD)
            nc.vector.memset(taps[:, :, 0:3], 0.0).then_inc(dconv_done, 2)
            dve.wait_ge(a_ln_ready, 1)
            nc.vector.scalar_tensor_tensor(a_sp.rearrange(flat), flat_a, 0.0, a_ln.rearrange(flat), ALU.max, ALU.add)
            dve.drain()
            nc.vector.scalar_tensor_tensor(g_log, a_sp, -1.0, wide(a_exp[:, 0, :], [P, NT2, DN_HEADS], 1),
                                           ALU.mult, ALU.mult).then_inc(g_ready, 1)
            nc.vector.memset(slope4, 0.0).then_inc(silu_done, 2)
            with dve.Fori(0, PN_Z // 2) as i:
                dve.drain()
                nc.vector.tensor_copy(tap_w, dn_cols[:, 0:96].rearrange("p (j c) -> p j c", j=4)[:, :, ds(i * 4, 4)])
                for f in range(4):
                    dve.drain()
                    dve.wait_ge(qkv_copied, i * 4 + (Q0 + f + 1))
                    dve.wait_ge(silu_done, i * 4 + (f + 1))
                    acc = taps_sum[:, f % 2, :]
                    nc.vector.tensor_scalar(acc, taps[:, f % 2, 0:SEQ], tap_w[:, 0, f:f + 1], None, ALU.mult)
                    for j in range(1, 4):
                        dve.drain()
                        last = nc.vector.scalar_tensor_tensor(acc, taps[:, f % 2, j:j + SEQ], tap_w[:, j, f:f + 1], acc,
                                                              ALU.mult, ALU.add)
                    last.then_inc(dconv_done, 1)
            dve.wait_ge(gc_copied, 1)
            nc.vector.tensor_tensor(g_rest.rearrange(flat), ps[:, 5, 32:64], g_cum.rearrange(flat), ALU.subtract
                                    ).then_inc(g_rest_ready, 1)
            dve.wait_ge(l2_rms_ready, 1)
            nc.vector.reciprocal(l2_inv, l2_rms)
            dve.wait_ge(decays_ready, 1)
            dve.drain()
            for hg in range(2):
                heads = slice(HG * hg, HG * (hg + 1))
                dst = col_tab[:, NT2 * hg:NT2 * (hg + 1), :, :]
                nc.vector.tensor_scalar(dst[:, :, 0, :], l2_inv[:, heads, :].rearrange("p h t -> p t h"), P ** -0.5, None,
                                        ALU.mult)
                nc.vector.tensor_copy(dst[:, :, 1, :], l2_inv[:, DN_HEADS + HG * hg:DN_HEADS + HG * (hg + 1), :]
                                      .rearrange("p h t -> p t h"))
                nc.vector.tensor_copy(dst[:, :, 2, :], beta[:, :, heads])
                nc.vector.tensor_copy(dst[:, :, 3, :], g_cum[:, :, heads])
                nc.vector.tensor_tensor(dst[:, :, 4, :], beta[:, :, heads], g_exp[:, :, heads], ALU.mult)
                nc.vector.tensor_copy(dst[:, :, 5, :], ke_exp[:, :, heads])
            with dve.Fori(0, 2) as hg:
                dve.drain()
                nc.vector.memset(state, 0.0)
                with dve.Fori(0, NT2) as t:
                    it = hg * NT2 + t
                    dve.drain()
                    nc.vector.tensor_copy(cur, col_tab[:, ds(it, 1), :, :].rearrange("p a k h -> p (a k) h")
                                          ).then_inc(cur_ready, 1)
                    dve.wait_ge(drows_done, it + 1)
                    nc.vector.tensor_tensor(dk_t, qkv[:, ds(hg * HG + 8, HG), ds(t * P, P)], by_head(0), ALU.mult)
                    nc.vector.tensor_tensor(dq_t, qkv[:, ds(hg * HG, HG), ds(t * P, P)], by_head(1), ALU.mult)
                    dve.drain()
                    nc.vector.tensor_tensor(dkb_t, dk_t, by_head(2), ALU.mult).then_inc(dk_ready, 1)
                    for hh in range(HG):
                        last = nc.vector.scalar_tensor_tensor(decay[:, hh, :], ps[:, 3, tile(hh)], cur[:, 3, hh:hh + 1],
                                                              decay_mask, ALU.subtract, ALU.add)
                    last.then_inc(dec_ready, 1)
                    dve.wait_ge(dexp_done, it + 1)
                    dve.wait_ge(dkk_done, it + 1)
                    nc.vector.tensor_tensor(da_t, by_head(6), decay, ALU.mult).then_inc(da_ready, 1)
                    eye = wide(ident, [P, 2, P], 1)
                    aside = [(dqk_t, by_head(7), decay), (dkbg, by_head(4), wide(cur[:, 4, :], [P, HG, P], 2)),
                             (dke, by_head(4), wide(cur[:, 5, :], [P, HG, P], 2)),
                             (dvb, by_head(5), wide(cur[:, 2, :], [P, HG, P], 2))]
                    for n in range(LEVELS):
                        mask = wide(levels[:, P * n:P * (n + 1)], [P, 2, P], 1)
                        for pair in range(2):
                            heads = slice(2 * pair, 2 * pair + 2)
                            dve.wait_ge(p1_done, it * (2 * LEVELS) + (2 * n + 1 + pair))
                            nc.vector.tensor_tensor(dp[:, heads, :], by_head(pair)[:, 0:2, :], mask, ALU.mult
                                                    ).then_inc(dp_ready, 1)
                        if n == 0:
                            dve.drain()
                            nc.vector.tensor_tensor(dx, wide(ident, [P, HG, P], 1), dp, ALU.subtract)
                        elif n <= len(aside):
                            dst, a, b = aside[n - 1]
                            nc.vector.tensor_tensor(dst, a, b, ALU.mult)
                        for pair in range(2):
                            heads = slice(2 * pair, 2 * pair + 2)
                            dve.wait_ge(delta_done, it * (2 * LEVELS) + (2 * n + 1 + pair))
                            if 0 < n < LEVELS - 1:
                                nc.vector.tensor_tensor(dx[:, heads, :], dx[:, heads, :], by_head(2 + pair)[:, 0:2, :],
                                                        ALU.subtract)
                            nc.vector.tensor_tensor(dx_t[:, heads, :], dx_t[:, heads, :] if n else eye,
                                                    by_head(2 + pair)[:, 2:4, :], ALU.subtract).then_inc(dx_ready, 1)
                        dve.drain()
                    for ch in range(2):
                        dve.drain()
                        dve.wait_ge(s_done, it * 2 + (ch + 1))
                        for hh in range(HG):
                            c = CHUNK * (ch + 1) - 1
                            last = nc.vector.scalar_tensor_tensor(state[:, hh, :], state[:, hh, :], g_rows[:, hh, c:c + 1],
                                                                  ps[:, 7, tile(hh)], ALU.mult, ALU.add)
                        last.then_inc(state_ready, 1)
                    nc.vector.tensor_copy(qkv[:, ds(hg * HG + 16, HG), ds(t * P, P)], by_head(6)).then_inc(do_copied, 1)
                    dve.drain()
            dve.wait_ge(odn_rms, 1)
            nc.vector.reciprocal(rstd, rms).then_inc(odn_rstd, 1)
            for c in range(DN_HEADS):
                o = qkv[:, 16 + c, :]
                dve.wait_ge(odn_rows, c + 1)
                nc.vector.scalar_tensor_tensor(o, o, col(DN_OUT), ps[:, 6 + c % 2, :], ALU.mult, ALU.mult
                                               ).then_inc(odn_normed, 1)
                dve.drain()
                dve.wait_ge(z_copied, c + 1)
                nc.vector.tensor_tensor(o, o, z_act[:, c % 2, :], ALU.mult).then_inc(odn_ready, 1)
            nc.vector.tensor_scalar(q_gain, col(QN), HD ** -0.5, None, ALU.mult)
            dve.wait_ge(n_rms_ready, 1)
            nc.vector.reciprocal(n_rstd[:, 0:96], n_rms[:, 0:96]).then_inc(n_rstd_ready, 1)
            dve.drain()
            for m in range(12):
                dve.wait_ge(n_rows, m + 1)
                rows = ps[:, 4 + m % 2, :]
                if m < KD:
                    last = nc.vector.scalar_tensor_tensor(nq[:, m, :], nq[:, m, :], q_gain, rows, ALU.mult, ALU.mult)
                else:
                    dst, gain = ((ks2, KS_N), (kw2, KW_N))[(m - KD) // 2]
                    for i in range(2):
                        own = slice(HD * i, HD * (i + 1))
                        for half in range(2):
                            last = nc.vector.scalar_tensor_tensor(
                                dst[HD * half:HD * (half + 1), (m - KD) % 2 * 2 + i, :], k_raw[own, m - KD, :],
                                col(gain)[own, :], rows[own, :], ALU.mult, ALU.mult)
                last.then_inc(n_scaled, 1)
            dve.drain()
            nc.vector.memset(c_gelu[:, GROUPS * N_CMP:], 0.0).then_inc(c_pad_ready, 1)
            dve.wait_ge(kc_rms, 1)
            nc.vector.reciprocal(n_rstd[:, 96:97], n_rms[:, 96:97]).then_inc(kc_rstd, 1)
            dve.wait_ge(kc_rows, 1)
            nc.vector.scalar_tensor_tensor(kc2, kc_raw, col(KC_N), ps[:, 5, 0:P], ALU.mult, ALU.mult).then_inc(kc_ready, 1)
            dve.drain()
            dve.wait_ge(vc_ready, 1)
            nc.vector.memset(pc_t, 0.0)
            nc.vector.memset(p_cmp[0][:, :, N_CMP:], 0.0)
            dve.wait_ge(w_split, N0 + PN_MDN + 4)
            nc.vector.memset(p_cmp[1][:, :, N_CMP:], 0.0).then_inc(pv2_done, 1)
            with dve.Fori(0, GROUPS) as g:
                dve.drain()
                nc.vector.tensor_copy(slope4, neg_slope[:, ds(g * REP, REP)])
                dve.drain()

                def parts(t):
                    slot = t % 2
                    return ((p_slc[slot], P * (t + 1)), (p_win[slot], P * min(t + 1, 3)), (p_cmp[slot], N_CMP))

                def maxima(t):
                    (slc, w_slc), (win, w_win), (cmp, _) = parts(t)
                    for r in range(REP):
                        dve.wait_ge(slc_scored, g * (REP * NT2) + (REP * t + r + 1))
                        nc.vector.scalar_tensor_tensor(slc[:, r, 0:w_slc], dist[:, SEQ - w_slc:], slope4[:, r:r + 1],
                                                       ps[:, r, 0:w_slc], ALU.mult, ALU.add).then_inc(slc_read, 1)
                    dve.drain()
                    nc.vector.reduce_max(s_top[:, 0, :], slc[:, :, 0:w_slc], AX.X)
                    dve.drain()
                    nc.vector.tensor_scalar(s_neg[:, 0, :], s_top[:, 0, :], -1.0, None, ALU.mult).then_inc(tops_ready, 1)
                    for r in range(REP):
                        dve.wait_ge(win_scored, g * (REP * NT2) + (REP * t + r + 1))
                        nc.vector.scalar_tensor_tensor(win[:, r, 0:w_win], dist_win[:, SEQ - P - w_win:], slope4[:, r:r + 1],
                                                       ps[:, r, 0:w_win], ALU.mult, ALU.add)
                        nc.vector.scalar_tensor_tensor(cmp[:, r, 0:N_CMP], dist_cmp[:, N_CMP * t:N_CMP * (t + 1)],
                                                       slope4[:, r:r + 1], ps[:, r, SEQ - P:SEQ - P + N_CMP],
                                                       ALU.mult, ALU.add)
                    dve.drain()
                    nc.vector.reduce_max(s_top[:, 1, :], win[:, :, 0:w_win], AX.X)
                    nc.vector.reduce_max(s_top[:, 2, :], cmp[:, :, 0:N_CMP], AX.X)
                    dve.drain()
                    nc.vector.tensor_scalar(s_neg[:, 1:3, :], s_top[:, 1:3, :], -1.0, None, ALU.mult).then_inc(tops_ready, 1)

                def weigh(t):
                    for part, ids in enumerate(((0,), (1, 2))):
                        own = slice(ids[0], ids[-1] + 1)
                        dve.wait_ge(exps_done, g * (2 * NT2) + (2 * t + part + 1))
                        nc.vector.reciprocal(s_weight[:, own, :], s_mass[:, own, :])
                        dve.drain()
                        g3 = gates[:, t, ds(g * (3 * REP), 3 * REP)].rearrange("p (r i) -> p i r", i=3)
                        for i in ids:
                            nc.vector.tensor_tensor(s_weight[:, i, :], s_weight[:, i, :], g3[:, (1, 2, 0)[i], :], ALU.mult)
                        dve.drain()
                        if t == 0 and part == 1:
                            nc.vector.tensor_scalar(s_weight[:, 2, :], s_weight[:, 2, :], valid[:, 0:1], None, ALU.mult)
                            dve.drain()
                        for i in ids:
                            p, w = parts(t)[i]
                            if i == 2:
                                nc.vector.tensor_tensor(p[:, :, 0:w], p[:, :, 0:w], wide(s_weight[:, i, :], [P, REP, w], 2),
                                                        ALU.mult)
                            else:
                                for r in range(REP):
                                    nc.vector.tensor_scalar(p[:, r, 0:w], p[:, r, 0:w], s_weight[:, i, r:r + 1], None, ALU.mult)
                        dve.drain().then_inc(p_ready, 1)

                maxima(0)
                for t in range(NT2):
                    weigh(t)
                    if t + 1 < NT2:
                        maxima(t + 1)
                    dve.wait_ge(pv2_done, g * BLOCKS_G + (sum(BLOCKS[:t + 1]) + 1))
                    o = ps[0:HD, 6, :].rearrange("p (a b n) -> p a b n", b=2, n=P)
                    for b in range(2):
                        nc.vector.tensor_scalar(nq[HD * b:HD * (b + 1), ds(g * 2, 2), tile(t)], o[:, :, b, :], 1.0, None,
                                                ALU.mult)
                    dve.drain().then_inc(att_copied, 1)
            for m in range(2):
                for j in range(4):
                    for oc in range(2):
                        n = 8 * m + 2 * j + oc
                        dve.wait_ge(products_done, E0 + EV_MDN + 16 * m + 4 * j + 2 + oc + 1)
                        dve.wait_ge(sig_ready, n + 1)
                        proj = ps[:, 4 * (j % 2) + 2 + oc, :]
                        dst = merged[:, 2 * j + oc, :]
                        if m == 0:
                            nc.vector.tensor_tensor(dst, sig[:, oc, :], proj, ALU.mult).then_inc(merged_part, 1)
                        else:
                            nc.vector.tensor_tensor(sig[:, oc, :], sig[:, oc, :], proj, ALU.mult)
                            dve.drain()
                            nc.vector.tensor_tensor(dst, dst, sig[:, oc, :], ALU.add).then_inc(merged_part, 1)
                dve.drain()
            for f in range(KD):
                dve.wait_ge(products_done, E0 + EV_WO + f + 1)
                nc.vector.tensor_tensor(x2[:, f, :], x2[:, f, :], ps[:, f, :], ALU.add).then_inc(x2_added, 1)
            dve.drain()
            norm2(M0 + 2, M0 + 1, NORM_MLP)
            nc.vector.memset(slope4, 0.0).then_inc(relu_sq_ready, 4)
            for part in range(2):
                with dve.Fori(0, 4) as i:
                    for f in range(4):
                        dve.wait_ge(relu_ready, i * 4 + (16 * part + f + 1))
                        dve.wait_ge(f_ready, i * 4 + (16 * part + f + 1))
                        if part:
                            dve.wait_ge(products_done, E0 + EV_DN[0] + 8)
                        u = relu_sq[:, f % 2, :]
                        nc.vector.scalar_tensor_tensor(u, ps[:, f, :], 0.0, relu[:, f % 2, :], ALU.max, ALU.mult
                                                       ).then_inc(relu_sq_ready, 1)
                        dve.drain()
                        nc.vector.tensor_copy(f_hi[:, ds(i * 4 + f, 1), :].rearrange(flat), u).then_inc(f_hi_ready, 1)
                dve.wait_ge(products_done, E0 + EV_DN[part] + 8)
                for c in range(KD):
                    nc.vector.tensor_tensor(x2[:, c, :], x2[:, c, :], ps[:, c, :], ALU.add).then_inc(x2_added, 1)
                dve.drain()

        @block.gpsimd
        def _(pool):
            def lower(n, slot):
                pool.wait_ge(w_hi, n + 1)
                nc.gpsimd.tensor_tensor(wlo[:, slot, :], wraw[:, slot, :], whi[:, slot, :].bitcast(F32),
                                        ALU.subtract).then_inc(w_split, 1)

            def norm(idx):
                for c in range(KD):
                    pool.wait_ge(hi_ready, idx * KD + (c + 1))
                    nc.gpsimd.tensor_tensor(hn(hn_lo, c, 0, T1), t_chunk[:, c % 2, :],
                                            hn(hn_hi, c, 0, T1).bitcast(F32), ALU.subtract).then_inc(hn_ready, 1)

            nc.gpsimd.memset(top, 0.0).then_inc(w_split, 2)
            nc.gpsimd.memset(neg_top, 0.0).then_inc(ff_ready, 4)
            for s in range(2):
                lower(s, s)
            with pool.Fori(0, DEPTH) as l:
                first = l * PANELS_L
                norm(l * 2)
                for j in range(10):
                    lower(first + (j + 2), j % 2)
                with pool.Fori(0, HEADS1) as hd:
                    it = l * HEADS1 + hd
                    pool.wait_ge(qkv_copied, l * 26 + 26)
                    for i in range(2):
                        nc.gpsimd.tensor_tensor(rope_a[:, i, :], qk_raw[:, ds(hd + 4 * i, 1), :].rearrange(flat),
                                                cos, ALU.mult).then_inc(rope_a_ready, 1)
                    nc.gpsimd.tensor_copy(v_head[:, 0:4, :], v_tok[:, 0:4, ds(hd * P, P)])
                    nc.gpsimd.tensor_copy(v_head[0:LAST, 4, :], v_tok[0:LAST, 4, ds(hd * P, P)]).then_inc(vh_ready, 1)
                    pool.wait_ge(rope_done, it * 2 + 2)
                    pool.wait_ge(pv_done, it * NT1 + NT1)
                for c in range(4):
                    pool.wait_ge(mix_hi, l * KD + (c + 1))
                    nc.gpsimd.tensor_tensor(hn(hn_lo, c, 0, T1), t_chunk[:, c % 2, :],
                                            hn(hn_hi, c, 0, T1).bitcast(F32), ALU.subtract).then_inc(mix_ready, 1)
                for c in range(4):
                    pool.wait_ge(mix_hi, l * KD + (4 + c + 1))
                    nc.gpsimd.tensor_tensor(hn(hn_lo, 4 + c, 0, T1), conv[:, c * T1:(c + 1) * T1],
                                            hn(hn_hi, 4 + c, 0, T1).bitcast(F32), ALU.subtract).then_inc(mix_ready, 1)
                for j in range(10, 14):
                    lower(first + (j + 2), j % 2)
                norm(l * 2 + 1)
                at, ff_at = 14, 0
                for part, n in enumerate(FC):
                    with pool.Fori(0, n // 2) as i:
                        lower(first + i * 2 + (at + 2), 0)
                        for j in range(4):
                            oc, half = j // 2, j % 2
                            pool.wait_ge(ffv_hi, l * FFS + i * 4 + (ff_at + j + 1))
                            a = HALF * half
                            nc.gpsimd.tensor_tensor(
                                ff_lo[:, ds(i * 2 + oc, 1), a:a + HALF].rearrange(flat), glu_val[:, j, :],
                                ff_hi[:, ds(i * 2 + oc, 1), a:a + HALF].rearrange(flat).bitcast(F32),
                                ALU.subtract).then_inc(ff_ready, 1)
                        lower(first + i * 2 + (at + 3), 1)
                    at += n
                    ff_at += 2 * n
                    with pool.Fori(0, 4) as b:
                        for s in range(2):
                            lower(first + b * 2 + (at + 2 + s), s)
                    at += 8
            def norm2(split):
                for c in range(KD):
                    pool.wait_ge(hi_ready, split * KD + (c + 1))
                    nc.gpsimd.tensor_tensor(hx(hn_lo, c, 0, SEQ), t2[:, c % 2, :], hx(hn_hi, c, 0, SEQ).bitcast(F32),
                                            ALU.subtract).then_inc(hn_ready, 1)

            pool.wait_ge(ws_hi_ready, 1)
            nc.gpsimd.tensor_tensor(ws_lo, w_small.rearrange(flat), ws_hi.bitcast(F32), ALU.subtract).then_inc(ws_ready, 1)
            norm2(M0)
            with pool.Fori(0, PN_Z // 2) as i:
                for s in range(2):
                    lower(i * 2 + (N0 + 2 + s), s)
            with pool.Fori(0, 2 * NT2) as it:
                pool.wait_ge(dexp_done, it + 1)
                nc.gpsimd.tensor_tensor(dqd_t, dq_t, g_rows, ALU.mult).then_inc(dqd_ready, 1)
            for pn in range(PN_Z, PN_NQ):
                lower(N0 + pn + 2, pn % 2)
            for pn in range(PN_NQ, PN_MDN):
                lower(N0 + pn + 2, pn % 2)
            pool.wait_ge(vc_ready, 1)
            pool.wait_ge(kc_ready, 1)
            with pool.Fori(0, GROUPS) as g:
                nc.gpsimd.tensor_copy(q_grp, nq[:, ds(g * 2, 2), :])
                for i, k in enumerate((ks2, kw2)):
                    nc.gpsimd.tensor_copy(k_grp[:, i, :], k[:, ds(g, 1), :].rearrange(flat))
                nc.gpsimd.tensor_copy(kc_grp, kc2[:, ds(g * N_CMP, N_CMP)])
                pool.drain().then_inc(kg_ready, 1)
                pool.wait_ge(pv2_done, g * BLOCKS_G + 1)
                for i, v in enumerate((vs, vw)):
                    nc.gpsimd.tensor_copy(v_grp[:, i, :, :], v[:, :, ds(g * HD, HD)])
                nc.gpsimd.tensor_copy(vc_grp, vc[:, ds(g, 1), :].rearrange(flat))
                pool.drain().then_inc(vg_ready, 1)
                pool.wait_ge(win_scored, g * (REP * NT2) + REP * NT2)
            def split_out(src, first):
                for c in range(KD):
                    pool.wait_ge(o_hi_ready, first + c + 1)
                    nc.gpsimd.tensor_tensor(o_lo[:, c, :], src(c), o_hi[:, c, :].bitcast(F32), ALU.subtract
                                            ).then_inc(o_ready, 1)

            split_out(lambda c: qkv[:, 16 + c, :], 0)
            for m, pn in enumerate((PN_MDN, PN_MNS)):
                for j in range(8):
                    lower(N0 + pn + j + 2, j % 2)
                if m == 0:
                    split_out(lambda c: nq[:, c, :], KD)
            for c in range(KD):
                pool.wait_ge(merged_hi, c + 1)
                nc.gpsimd.tensor_tensor(hx(hn_lo, c, 0, SEQ), merged[:, c, :], hx(hn_hi, c, 0, SEQ).bitcast(F32),
                                        ALU.subtract).then_inc(merged_ready, 1)
            for j in range(4):
                lower(N0 + PN_WO + j + 2, j % 2)
            norm2(M0 + 1)
            nc.gpsimd.memset(top, 0.0).then_inc(f_ready, 2)
            for part in range(2):
                with pool.Fori(0, 4) as i:
                    for f in range(4):
                        pool.wait_ge(f_hi_ready, i * 4 + (16 * part + f + 1))
                        nc.gpsimd.tensor_tensor(f_lo[:, ds(i * 4 + f, 1), :].rearrange(flat), relu_sq[:, f % 2, :],
                                                f_hi[:, ds(i * 4 + f, 1), :].rearrange(flat).bitcast(F32), ALU.subtract
                                                ).then_inc(f_ready, 1)
                        if f % 2:
                            lower(i * 2 + (N0 + PN_UP[part] + 2 + f // 2), f // 2)
                with pool.Fori(0, 4 - part) as i:
                    for s in range(2):
                        lower(i * 2 + (N0 + PN_DN[part] + 2 + s), s)


_INS = ["x", "meta_tokens", "norm1_g", "w_in", "b_glu", "conv_w", "conv_b", "conv_ln_g", "conv_ln_b", "lam_q1",
        "lam_k1", "lam_q2", "lam_k2", "subln_g", "w_out", "norm2_g", "w_gate_up", "w_down", "final_g", "norm_mix_2",
        "w_in_2", "dn_conv_2", "dn_a_log_2", "dn_dt_bias_2", "dn_out_norm_2", "nsa_q_norm_2", "nsa_k_norm_cmp_2",
        "nsa_k_norm_slc_2", "nsa_k_norm_win_2", "cmp_pos_k_2", "cmp_w1_k_2", "cmp_w2_k_2", "cmp_pos_v_2",
        "cmp_w1_v_2", "cmp_w2_v_2", "w_proj_dn_2", "w_proj_nsa_2", "w_out_2", "norm_mlp_2", "w_up_2", "w_down_2"]


def kernel(**inputs):
    import concourse.bacc as bacc
    from concourse.bass_utils import run_bass_kernel_spmd

    nc = bacc.Bacc("TRN2", target_bir_lowering=False, num_devices=1)
    arrays = {f"in_{n}": np.ascontiguousarray(inputs[n]) for n in _INS}
    arrays["table1"] = packed(first_constants())
    arrays["table2"] = packed(second_constants())
    aps = {n: nc.dram_tensor(n, a.shape, mybir.dt.from_np(a.dtype), kind="ExternalInput").ap()
           for n, a in arrays.items()}
    out = nc.dram_tensor("out", (1, SEQ, D), F32, kind="ExternalOutput").ap()
    hybrid_blocks(nc, {n: aps[f"in_{n}"] for n in _INS}, aps["table1"], aps["table2"], out)
    r = run_bass_kernel_spmd(nc, [arrays], core_ids=[0])
    return r.results[0]["out"]
```

```python
import math
from contextlib import ExitStack

import numpy as np

import concourse.bass as bass
from concourse import mybir

F32 = mybir.dt.float32
F32R = mybir.dt.float32r
ALU = mybir.AluOpType
ACT = mybir.ActivationFunctionType
AX = mybir.AxisListType
ds = bass.ds

P = 128
D = 1024
KD = D // P
SEQ = 512
N_META = 16
T1 = SEQ + N_META
HALF = T1 // 2
NT1 = 5
LAST = T1 - 4 * P
PADT = NT1 * P
DEPTH = 2
HEADS1 = 4
TAPS = 31
EARLY = 13
GROUP = 3
GROUPS1 = (TAPS - EARLY) // GROUP
LN_AT = 2 * NT1
TILES1 = HEADS1 * NT1
FF1 = 2816
FC = (12, 10)
PW = 256
PANEL = KD * PW
MASKED = -1e30

EV_GLU, EV_V, EV_QK, EV_OUT = 0, 16, 26, 42
EV_FF = (58, 126)
EV_DOWN = (106, 166)
EVENTS = 186
PANELS_L = 52
GLUS = 52
FFS = 44
ADDS = 48


def first_constants():
    pos = np.arange(T1, dtype=np.float32)
    inv = np.float32(10000.0) ** (-np.arange(0, 64, 2, dtype=np.float32) / np.float32(64))
    ang = (pos[None, :] * inv[np.arange(P) % 32][:, None]).astype(np.float32)
    rot = np.zeros((P, P), np.float32)
    for m in range(P):
        low = m % 64 < 32
        rot[m + 32 if low else m - 32, m] = -1.0 if low else 1.0
    q, k = np.arange(P)[:, None], np.arange(P)[None, :]
    lam = [0.8 - 0.6 * math.exp(-0.3 * l) for l in range(DEPTH)]
    return {
        "ident": np.eye(P, dtype=np.float32),
        "rot": rot,
        "cos": np.cos(ang, dtype=np.float32),
        "sin": np.sin(ang, dtype=np.float32),
        "causal": np.where(k <= q, 0.0, MASKED).astype(np.float32),
        "eps5": np.full((P, 1), 1e-5, np.float32),
        "eps6": np.full((P, 1), 1e-6, np.float32),
        "lam_init": np.tile(np.float32(lam), (P, 1)),
        "lam_rest": np.tile(np.float32([1.0 - v for v in lam]), (P, 1)),
    }


def packed(tables):
    return np.ascontiguousarray(np.concatenate(list(tables.values()), axis=1), np.float32)


def columns(tables):
    at, out = 0, {}
    for name, a in tables.items():
        out[name] = (at, a.shape[1])
        at += a.shape[1]
    return out, at

(EV_QKV, EV_Z, EV_NQ, EV_KC, EV_KS, EV_KW, EV_VS, EV_VW, EV_VC, EV_MDN, EV_MNS, EV_WO) = (
    0, 24, 32, 40, 42, 44, 46, 50, 54, 56, 72, 88)
EV_UP = (96, 120)
EV_DN = (112, 136)
(PN_QKV, PN_Z, PN_NQ, PN_KC, PN_KS, PN_KW, PN_VS, PN_VW, PN_VC, PN_MDN, PN_MNS, PN_WO) = (
    0, 12, 16, 20, 21, 22, 23, 24, 25, 26, 34, 42)
PN_UP = (46, 62)
PN_DN = (54, 70)
PANELS_2 = 78
NT2 = 4
DN_HEADS = 8
HG = 4
CHUNK = 64
LEVELS = 6
KINDS = 6
NSA_HEADS, GROUPS, REP, HD = 16, 4, 4, 64
N_CMP = (SEQ - 32) // 16 + 1
WINDOW = 256
FAR = 1e32
C_Z = 3072
C_BA = 4096
C_NQ = 4112
C_KC, C_VC, C_KS, C_VS, C_KW, C_VW = (C_NQ + 1024 + 256 * i for i in range(6))
C_GATE = C_VW + 256
C_MDN = C_GATE + 48
C_MNS = C_MDN + 1024


def second_constants():
    i, j = np.arange(P)[:, None], np.arange(P)[None, :]
    same = i // CHUNK == j // CHUNK
    out = {
        "tri": (same & (i <= j)).astype(np.float32),
        "blk": same.astype(np.float32),
        "decay_mask": np.where(same & (j >= i), 0.0, MASKED).astype(np.float32),
    }
    levels = []
    for n in range(LEVELS):
        s = 1 << n
        levels.append((i // (2 * s) == j // (2 * s)) & (i // s % 2 == 1) & (j // s % 2 == 0))
    out["levels"] = np.concatenate(levels, axis=1).astype(np.float32)
    d = i - np.arange(SEQ)[None, :] + (SEQ - P)
    out["dist"] = np.where(d >= 0, d, FAR).astype(np.float32)
    w = d[:, SEQ - P - WINDOW:]
    out["dist_win"] = np.where((w >= 0) & (w < WINDOW), w, FAR).astype(np.float32)
    c = [P * t + i - (16 * np.arange(N_CMP)[None, :] + 31) for t in range(NT2)]
    out["dist_cmp"] = np.concatenate([np.where(x >= 0, x, FAR) for x in c], axis=1).astype(np.float32)
    out["valid"] = np.concatenate([(P * t + i >= 31) for t in range(NT2)], axis=1).astype(np.float32)
    out["halves"] = (i // 64 == np.arange(2)[None, :]).astype(np.float32)
    out["neg_slope"] = np.tile(-(2.0 ** (-8.0 * np.arange(1, NSA_HEADS + 1) / NSA_HEADS)), (P, 1)).astype(np.float32)
    return out


def hybrid_blocks(nc, A, table1, table2, out):
    tab1, n1 = columns(first_constants())
    tab2, n2 = columns(second_constants())
    flat = "p a b -> p (a b)"

    with ExitStack() as ctx:
        base = -(-nc.sbuf_base // 64) * 64

        def put(name, shape, offset, dtype=F32):
            return nc.alloc_sbuf_tensor_at(name, shape, dtype, offset=offset)[:]

        def room(n):
            nonlocal base
            at, base = base, base + -(-n // 32) * 32
            return at

        def keep(name, shape, dtype=F32):
            return put(name, shape, room(4 * int(np.prod(shape[1:]))), dtype)

        const1_at = room(4 * n1)
        const1 = put("const1", [P, n1], const1_at)
        ident, rot, cos, sin, causal, eps5, eps6, lam_init, lam_rest = (
            const1[:, a:a + n] for a, n in tab1.values())
        ones = keep("ones", [P, 2])
        vec_cols = keep("vec_cols", [P, 103])
        conv_cols_at = room(4 * DEPTH * TAPS * 4)
        conv_cols = put("conv_cols", [P, DEPTH * TAPS * 4], conv_cols_at)
        dn_cols = keep("dn_cols", [P, 128])
        lay = keep("lay", [P, 37])
        lay_conv = keep("lay_conv", [P, TAPS * 4])
        sub_gain = keep("sub_gain", [P, 1])
        lam_dot = keep("lam_dot", [P, 2 * DEPTH])
        lam_exp = keep("lam_exp", [P, 2 * DEPTH])
        neg_lam = keep("neg_lam", [P, DEPTH])
        lay_neg_lam = keep("lay_neg_lam", [P, 1])
        rms = keep("rms", [P, 32])
        rstd = keep("rstd", [P, 32])
        top, neg_top, mass, weight = (keep(n, [P, 2, 2]) for n in ("top", "neg_top", "mass", "weight"))
        weight2 = keep("weight2", [P, 2])
        sq_at = room(4 * 2 * PADT)
        sq = put("sq", [P, 2, PADT], sq_at)
        wraw_at = room(4 * 2 * PANEL)
        wraw = put("wraw", [P, 2, PANEL], wraw_at)
        whi = keep("whi", [P, 2, PANEL], F32R)
        wlo = keep("wlo", [P, 2, PANEL], F32R)
        hn_hi = keep("hn_hi", [P, KD * T1 + PADT - T1], F32R)
        hn_lo = keep("hn_lo", [P, KD * T1 + PADT - T1], F32R)
        h_at = room(4 * KD * T1)
        h = put("h", [P, KD, T1], h_at)
        work = room(2 * 4 * FC[0] * T1)
        ff_hi = put("ff_hi", [P, FC[0], T1], work, F32R)
        ff_lo = put("ff_lo", [P, FC[0], T1], work + 4 * FC[0] * T1, F32R)
        x_tok = put("x_tok", [P, 4, D], work)
        meta_tok = put("meta_tok", [N_META, D], work + 16 * D)
        rows_vec = put("rows_vec", [103, P], work + 20 * D)
        rows_conv = put("rows_conv", [TAPS * 4, DEPTH, P], work + 20 * D + 512)
        rows_dn = put("rows_dn", [P, P], work + 20 * D + 1536)
        lam_rows = put("lam_rows", [P, 4, DEPTH * 64], work + 20 * D + 2048)
        lam_prod = put("lam_prod", [P, 2 * DEPTH, 64], work + 20 * D + 4096)
        qk_raw = put("qk_raw", [P, KD, T1], work)
        o_raw = qk_raw
        sq8 = put("sq8", [P, KD, PADT], work)
        v_at = work + 4 * KD * T1
        v_tok = put("v_tok", [P, NT1, 512], v_at)
        z = put("z", [P, 4, TAPS - 1 + T1], v_at + 4 * NT1 * 512)
        conv_at = v_at + 4 * NT1 * 512 + 16 * (TAPS - 1 + T1)
        conv = put("conv", [P, 4 * T1 + PADT - T1], conv_at)
        scratch = room(32 * 1024)
        t_chunk = put("t_chunk", [P, 2, T1], scratch)
        glu_gate = put("glu_gate", [P, 4, HALF], scratch + 8 * T1)
        glu_val = put("glu_val", [P, 4, HALF], scratch + 16 * T1)
        tap_prod = put("tap_prod", [P, GROUP, T1], scratch + 16 * T1)
        s_at = scratch
        rope_a = put("rope_a", [P, 2, T1], s_at)
        mean_sb = put("mean_sb", [P, T1], s_at + 8 * T1)
        rope_b = put("rope_b", [P, 2, T1], s_at + 8 * T1)
        s_at += 16 * T1
        probs4 = put("probs", [P, 2, 2, T1], s_at)
        diff = put("diff", [P, 2, PADT], s_at + 16 * T1)
        diff_t = put("diff_t", [P, 2, PADT], s_at + 16 * T1 + 8 * PADT)
        s_at += 16 * T1 + 16 * PADT
        assert s_at <= scratch + 32 * 1024
        const2 = keep("const2", [P, n2])
        (tri, blk, decay_mask, levels, dist, dist_win, dist_cmp, valid, halves, neg_slope) = (
            const2[:, a:a + n] for a, n in tab2.values())
        small_at = room(4 * KD * 64)
        w_small = put("w_small", [P, KD, 64], small_at)
        v_grp = put("v_grp", [P, 2, NT2, HD], small_at)
        head_rows = keep("head_rows", [P, 2, DN_HEADS])
        w2k = keep("w2k", [P, 2 * HD])
        w2v = keep("w2v", [P, HD])
        gates = keep("gates", [P, NT2, 48])
        col_tab = keep("col_tab", [P, 2 * NT2, KINDS, HG])
        cur = keep("cur", [P, KINDS, HG])
        tap_w = keep("tap_w", [P, 4, 4])
        n_rms = put("n_rms", [P, 97], conv_cols_at)
        n_rstd = put("n_rstd", [P, 97], conv_cols_at + 416)
        q_gain = keep("q_gain", [P, 1])
        pos_sum = keep("pos_sum", [P, 1])
        slope4 = keep("slope4", [P, REP])
        s_top, s_neg, s_mass, s_weight = (keep(n, [P, 3, REP]) for n in ("s_top", "s_neg", "s_mass", "s_weight"))
        assert base <= nc.sbuf_usable_end, base

        x2 = put("x2", [P, KD, SEQ], scratch)
        tmp = scratch + 4 * KD * SEQ
        t2 = put("t2", [P, 2, SEQ], tmp)
        qkv = put("qkv", [P, 24, SEQ], work)
        taps = put("taps", [P, 2, SEQ + 3], tmp)
        taps_sum = put("taps_sum", [P, 2, SEQ], tmp + 4160)
        ws_hi = put("ws_hi", [P, KD * 64], tmp + 8256, F32R)
        ws_lo = put("ws_lo", [P, KD * 64], tmp + 10304, F32R)
        (beta, a_dt, a_abs, a_ln, a_sp, g_log, g_cum, g_rest, g_exp, ke_exp, a_exp) = (
            put(n, [P, NT2, DN_HEADS], tmp + 12352 + 128 * i) for i, n in enumerate(
                ("beta", "a_dt", "a_abs", "a_ln", "a_sp", "g_log", "g_cum", "g_rest", "g_exp", "ke_exp", "a_exp")))
        l2_rms = put("l2_rms", [P, 16, NT2], tmp + 13760)
        l2_inv = put("l2_inv", [P, 16, NT2], tmp + 14016)
        dk_t, dkb_t, dq_t, dqd_t, dkbg, dke, dvb, da_t = (
            put(n, [P, HG, P], h_at + 2048 * i) for i, n in enumerate(
                ("dk_t", "dkb_t", "dq_t", "dqd_t", "dkbg", "dke", "dvb", "da_t")))
        dqk_t, decay, g_rows0, dx, dx_t, dp, dw_t, dvn = (
            put(n, [P, HG, P], tmp + 2048 * i) for i, n in enumerate(
                ("dqk_t", "decay", "g_rows0", "dx", "dx_t", "dp", "dw_t", "dvn")))
        g_rows = [g_rows0, put("g_rows1", [P, HG, P], sq_at)]
        rope_at = const1_at + 4 * 2 * P
        dv_t = put("dv_t", [P, HG, P], rope_at)
        state = put("state", [P, HG, P], rope_at + 2048)
        z_act = put("z_act", [P, 2, SEQ], tmp)
        nq = put("nq", [P, KD, SEQ], work)
        kcmp = put("kcmp", [P, GROUPS, SEQ], work + 16384)
        w1 = put("w1", [P, 16, P], work + 8192 + 16384)
        ks2 = put("ks2", [P, GROUPS, SEQ], h_at)
        kw2 = put("kw2", [P, GROUPS, SEQ], h_at + 8192)
        k_grp = put("k_grp", [P, 2, SEQ], rope_at)
        kc_grp = put("kc_grp", [P, N_CMP], rope_at + 4096)
        vs = put("vs", [P, NT2, GROUPS * HD], tmp)
        vw = put("vw", [P, NT2, GROUPS * HD], tmp + 4096)
        k_raw = put("k_raw", [P, 4, SEQ], tmp + 8192)
        p_t = put("p_t", [P, 2, REP * P], tmp + 8192)
        vc = put("vc", [P, GROUPS, HD], tmp + 12288)
        vc_grp = put("vc_grp", [P, HD], tmp + 13312)
        kc2 = put("kc2", [P, P], tmp + 13568)
        kc_raw = put("kc_raw", [P, P], tmp + 14080)
        pc_t = put("pc_t", [P, REP * P], tmp + 14080)
        c_gelu = put("c_gelu", [P, P], tmp + 14592)
        probs_at = (work + 16384, wraw_at)
        p_slc = [put(f"p_slc{i}", [P, REP, SEQ], at) for i, at in enumerate(probs_at)]
        p_win = [put(f"p_win{i}", [P, REP, SEQ - P], at + 8192) for i, at in enumerate(probs_at)]
        p_cmp = [put(f"p_cmp{i}", [P, REP, 32], at + 14336) for i, at in enumerate(probs_at)]
        q_grp = put("q_grp", [P, 2, SEQ], sq_at)
        o_hi = put("o_hi", [P, KD, SEQ], h_at, F32R)
        o_lo = put("o_lo", [P, KD, SEQ], tmp, F32R)
        merged = put("merged", [P, KD, SEQ], work + 16384)
        sig = put("sig", [P, 2, SEQ], sq_at)
        f_hi = put("f_hi", [P, 16, SEQ], h_at, F32R)
        f_lo = put("f_lo", [P, 16, SEQ], h_at + 32768, F32R)
        relu = put("relu", [P, 2, SEQ], sq_at)
        relu_sq = put("relu_sq", [P, 2, SEQ], rope_at)
        y_tok = put("y_tok", [P, NT2, D], tmp)

        ps = ctx.enter_context(nc.psum_tensor("ps", [P, 8, 512], F32))
        line = ps[:, :, :].rearrange(flat)

        def sem(name):
            return ctx.enter_context(nc.semaphore(name))

        x_in = sem("x_in")
        setup_in = sem("setup_in")
        tables_in = sem("tables_in")
        raw_in = [sem("raw_in0"), sem("raw_in1")]
        w_hi = sem("w_hi")
        w_split = sem("w_split")
        products_done = sem("products_done")
        x_turned = sem("x_turned")
        h_copied = sem("h_copied")
        cols_turned = sem("cols_turned")
        lam_dots = sem("lam_dots")
        lam_exps = sem("lam_exps")
        h_ready = sem("h_ready")
        sq_ready = sem("sq_ready")
        sq_dve = sem("sq_dve")
        sq_pool = sem("sq_pool")
        sums_done = sem("sums_done")
        rms_ready = sem("rms_ready")
        rstd_ready = sem("rstd_ready")
        rows_ready = sem("rows_ready")
        t_ready = sem("t_ready")
        hi_ready = sem("hi_ready")
        hn_ready = sem("hn_ready")
        gate_act = sem("gate_act")
        glu_used = sem("glu_used")
        ffv_hi = sem("ffv_hi")
        ff_ready = sem("ff_ready")
        qkv_copied = sem("qkv_copied")
        conv_done = sem("conv_done")
        h_added = sem("h_added")
        taps_ready = sem("taps_ready")
        taps_added = sem("taps_added")
        rope_a_ready = sem("rope_a_ready")
        rot_done = sem("rot_done")
        rope_done = sem("rope_done")
        scored = sem("scored")
        max_ready = sem("max_ready")
        exp_done = sem("exp_done")
        diff_ready = sem("diff_ready")
        diff_turned = sem("diff_turned")
        diff_t_ready = sem("diff_t_ready")
        pv_done = sem("pv_done")
        o_copied = sem("o_copied")
        sub_sq = sem("sub_sq")
        sub_stat = sem("sub_stat")
        sub_rms = sem("sub_rms")
        sub_rstd = sem("sub_rstd")
        sub_rows = sem("sub_rows")
        sub_t = sem("sub_t")
        ln_sum = sem("ln_sum")
        ln_mean = sem("ln_mean")
        ln_mean_rows = sem("ln_mean_rows")
        ln_mean_copied = sem("ln_mean_copied")
        ln_sq = sem("ln_sq")
        ln_stat = sem("ln_stat")
        ln_rms = sem("ln_rms")
        ln_rstd = sem("ln_rstd")
        ln_rows = sem("ln_rows")
        ln_t = sem("ln_t")
        ln_silu = sem("ln_silu")
        mix_hi = sem("mix_hi")
        mix_ready = sem("mix_ready")
        stored = sem("stored")

        x2_ready = sem("x2_ready")
        ws_hi_ready = sem("ws_hi_ready")
        ws_ready = sem("ws_ready")
        small_done = sem("small_done")
        small_act = sem("small_act")
        a_abs_ready = sem("a_abs_ready")
        a_ln_ready = sem("a_ln_ready")
        g_ready = sem("g_ready")
        gc_done = sem("gc_done")
        gc_copied = sem("gc_copied")
        g_rest_ready = sem("g_rest_ready")
        decays_ready = sem("decays_ready")
        dconv_done = sem("dconv_done")
        silu_done = sem("silu_done")
        l2_sq = sem("l2_sq")
        l2_stat = sem("l2_stat")
        l2_rms_ready = sem("l2_rms_ready")
        cur_ready = sem("cur_ready")
        drows_done = sem("drows_done")
        dk_ready = sem("dk_ready")
        dv_ready = sem("dv_ready")
        dec_ready = sem("dec_ready")
        dexp_done = sem("dexp_done")
        dqd_ready = sem("dqd_ready")
        dturned = sem("dturned")
        dkk_done = sem("dkk_done")
        da_ready = sem("da_ready")
        p1_done = sem("p1_done")
        dp_ready = sem("dp_ready")
        delta_done = sem("delta_done")
        dx_ready = sem("dx_ready")
        dw_done = sem("dw_done")
        dw_ready = sem("dw_ready")
        vn_done = sem("vn_done")
        vn_ready = sem("vn_ready")
        s_done = sem("s_done")
        state_ready = sem("state_ready")
        do_copied = sem("do_copied")
        odn_sq = sem("odn_sq")
        odn_stat = sem("odn_stat")
        odn_rms = sem("odn_rms")
        odn_rstd = sem("odn_rstd")
        odn_rows = sem("odn_rows")
        odn_normed = sem("odn_normed")
        z_copied = sem("z_copied")
        odn_ready = sem("odn_ready")
        nsa_copied = sem("nsa_copied")
        n_sq = sem("n_sq")
        n_stat = sem("n_stat")
        n_rms_ready = sem("n_rms_ready")
        n_rstd_ready = sem("n_rstd_ready")
        n_rows = sem("n_rows")
        n_scaled = sem("n_scaled")
        w1_in = sem("w1_in")
        hidden_done = sem("hidden_done")
        gelu_ready = sem("gelu_ready")
        kc_done = sem("kc_done")
        kc_sq = sem("kc_sq")
        kc_stat = sem("kc_stat")
        kc_rms = sem("kc_rms")
        kc_rstd = sem("kc_rstd")
        kc_rows = sem("kc_rows")
        kc_ready = sem("kc_ready")
        vc_done = sem("vc_done")
        vc_ready = sem("vc_ready")
        kg_ready = sem("kg_ready")
        vg_ready = sem("vg_ready")
        c_pad_ready = sem("c_pad_ready")
        slc_scored = sem("slc_scored")
        slc_read = sem("slc_read")
        win_scored = sem("win_scored")
        tops_ready = sem("tops_ready")
        exps_done = sem("exps_done")
        p_ready = sem("p_ready")
        p_turned = sem("p_turned")
        p_t_ready = sem("p_t_ready")
        pv2_done = sem("pv2_done")
        att_copied = sem("att_copied")
        o_hi_ready = sem("o_hi_ready")
        o_ready = sem("o_ready")
        sig_ready = sem("sig_ready")
        merged_part = sem("merged_part")
        merged_hi = sem("merged_hi")
        merged_ready = sem("merged_ready")
        x2_added = sem("x2_added")
        relu_ready = sem("relu_ready")
        relu_sq_ready = sem("relu_sq_ready")
        f_hi_ready = sem("f_hi_ready")
        f_ready = sem("f_ready")
        y_turned = sem("y_turned")
        y_copied = sem("y_copied")
        E0, N0 = DEPTH * EVENTS, DEPTH * PANELS_L
        Q0, M0, X0 = DEPTH * 26, 2 * DEPTH, DEPTH + 1

        def hx(x, k, start, n):
            return x[:, k * SEQ + start:k * SEQ + start + n]

        def tile(t):
            return slice(P * t, P * (t + 1))

        def by_head(bank):
            return ps[:, bank, :].rearrange("p (h n) -> p h n", h=HG)

        def col(name):
            return vec_cols[:, name:name + 1]

        BLOCKS = [(t + 1) + min(t + 1, 3) + 1 for t in range(NT2)]
        BLOCKS_G = sum(BLOCKS)

        def first_key(t):
            return P * max(0, t - 2)

        def wide(x, shape, axis):
            return x.unsqueeze(axis).to_broadcast(shape)
        block = ctx.enter_context(nc.Block())

        n_setup, n_tables = [0], [0]

        def tok_tile(t):
            return P * t, (P if t < 4 else LAST)

        def hn(x, k, start, n):
            return x[:, k * T1 + start:k * T1 + start + n]

        def scores_of(t):
            n, keys = tok_tile(t)[1], min(P * (t + 1), T1)
            if t < 4:
                return ps[0:n, 2 * (t % 2):2 * (t % 2) + 2, 0:keys]
            return ps[0:n, 0:4, :].rearrange("p (c b) w -> p c (b w)", c=2)[:, :, 0:keys]

        def key_blocks(t):
            return [(P * b, min(P, T1 - P * b)) for b in range(t + 1)]

        mean_rows = line[:, 2048:2048 + T1]
        conv_acc = line[:, 3072:3072 + T1]

        VEC = {"norm1": 0, "norm2": 8, "a_bias": 16, "gate_bias": 20, "conv_b": 24, "ln_g": 28,
               "ln_b": 32, "sub": 36}
        FINAL, NORM_MIX, NORM_MLP, DN_OUT, QN, KC_N, KS_N, KW_N = 74, 82, 90, 98, 99, 100, 101, 102

        @block.sync
        def _(sp):
            sp.dma_start(const1, table1).then_inc(x_in, 16)
            for t in range(4):
                sp.dma_start(x_tok[:, t, :], A["x"][0, P * t:P * (t + 1), :]).then_inc(x_in, 16)
            sp.dma_start(meta_tok, A["meta_tokens"]).then_inc(x_in, 16)
            w_in_2 = A["w_in_2"][0].rearrange("(k p) n -> p k n", p=P)

            def panel(n, slot, src):
                sp.wait_ge(w_split, n + 1)
                nk, w = src.shape[1], src.shape[2]
                dst = wraw[:, slot, 0:nk * w].rearrange("p (k n) -> p k n", k=nk)
                sp.dma_start(dst, src).then_inc(raw_in[slot], 16)

            w_in, w_out, w_gu, w_dn = (A[n].rearrange("d (k p) n -> d p k n", p=P)
                                       for n in ("w_in", "w_out", "w_gate_up", "w_down"))
            with sp.Fori(0, DEPTH) as l:
                first = l * PANELS_L
                cols = []
                for p in range(2):
                    cols += [2048 + PW * p, 1536 + PW * p]
                cols += [1024, 1024 + PW]
                for j, c in enumerate(cols):
                    panel(first + j, j % 2, w_in[l, :, :, c:c + PW])
                with sp.Fori(0, 2) as i:
                    for s in range(2):
                        panel(first + i * 2 + (6 + s), s, w_in[l, :, :, ds(i * (2 * PW) + s * PW, PW)])
                for j in range(4):
                    panel(first + 10 + j, j % 2, w_out[l, :, :, PW * j:PW * (j + 1)])
                at, k0 = 14, 0
                for n in FC:
                    with sp.Fori(0, n // 2) as i:
                        panel(first + at + i * 2, 0, w_gu[l, :, :, ds(i * PW + k0 * P, PW)])
                        panel(first + at + i * 2 + 1, 1,
                              w_gu[l, :, :, ds(i * PW + (k0 * P + FF1), PW)])
                    at += n
                    with sp.Fori(0, 4) as b:
                        for s in range(2):
                            ks = k0 + s * n // 2
                            panel(first + at + b * 2 + s, s,
                                  w_dn[l, :, ks:ks + n // 2, ds(b * PW, PW)])
                    at += 8
                    k0 += n
            def cols_of(name, c):
                return A[name][0].rearrange("(k p) n -> p k n", p=P)[:, :, c:c + PW]

            with sp.Fori(0, PN_Z // 2) as i:
                for s in range(2):
                    panel(i * 2 + (N0 + s), s, w_in_2[:, :, ds(i * (2 * PW) + s * PW, PW)])
            for j in range(4):
                panel(N0 + PN_Z + j, j % 2, w_in_2[:, :, C_Z + PW * j:C_Z + PW * (j + 1)])
            for j in range(4):
                panel(N0 + PN_NQ + j, j % 2, w_in_2[:, :, C_NQ + PW * j:C_NQ + PW * (j + 1)])
            sp.wait_ge(do_copied, 2 * NT2 + 1)
            sp.dma_start(w1, A["cmp_w1_k_2"][0].rearrange("(m p) n -> p m n", p=P)).then_inc(w1_in, 16)
            for j, c in enumerate((C_KC, C_KS, C_KW, C_VS, C_VW, C_VC)):
                n = PN_KC + j
                panel(N0 + n, n % 2, w_in_2[:, :, c:c + PW])
            sp.wait_ge(hidden_done, 1)
            sp.dma_start(w1, A["cmp_w1_v_2"][0].rearrange("(m p) n -> p m n", p=P)).then_inc(w1_in, 16)
            for pn, c, name in ((PN_MDN, C_MDN, "w_proj_dn_2"), (PN_MNS, C_MNS, "w_proj_nsa_2")):
                for j in range(4):
                    if pn == PN_MDN and j == 1:
                        sp.wait_ge(att_copied, GROUPS * NT2)
                    panel(N0 + pn + 2 * j, 0, w_in_2[:, :, c + PW * j:c + PW * (j + 1)])
                    panel(N0 + pn + 2 * j + 1, 1, cols_of(name, PW * j))
            for j in range(4):
                panel(N0 + PN_WO + j, j % 2, cols_of("w_out_2", PW * j))
            w_up = A["w_up_2"][0].rearrange("(k p) n -> p k n", p=P)
            w_down = A["w_down_2"][0].rearrange("(k p) n -> p k n", p=P)
            for part in range(2):
                with sp.Fori(0, 4) as i:
                    for s in range(2):
                        panel(i * 2 + (N0 + PN_UP[part] + s), s,
                              w_up[:, :, ds(i * (2 * PW) + (2048 * part + s * PW), PW)])
                with sp.Fori(0, 4) as i:
                    for s in range(2):
                        panel(i * 2 + (N0 + PN_DN[part] + s), s,
                              w_down[:, ds(i * 4 + (16 * part + 2 * s), 2), :])
            for half in range(2):
                sp.wait_ge(y_copied, 4 * half + 4)
                columns_of = slice(512 * half, 512 * (half + 1))
                sp.dma_start(out[0].rearrange("(t p) d -> p t d", p=P)[:, :, columns_of], y_tok[:, :, columns_of]
                             ).then_inc(stored, 16)
            sp.wait_ge(stored, 32)

        @block.tensor
        def _(pe):
            def product(dst, slot, k, oc, rhs_hi, rhs_lo, start, stop):
                c = k * PW + oc * P
                nc.tensor.matmul(dst, whi[:, slot, c:c + P], rhs_hi, start=start, stop=False)
                nc.tensor.matmul(dst, whi[:, slot, c:c + P], rhs_lo, start=False, stop=False)
                return nc.tensor.matmul(dst, wlo[:, slot, c:c + P], rhs_hi, start=False, stop=stop)

            def square_sums(c, begin, end):
                for t in range(NT1):
                    last = nc.tensor.matmul(ps[:, 6, t:t + 1], sq8[:, c, P * t:P * t + P], ones[:, 0:1],
                                            start=(begin and t == 0), stop=end, skip_group_check=True)
                return last

            def norm(idx, whole):
                if whole is not None:
                    pe.wait_ge(sq_pool, whole)
                    square_sums(0, True, False)
                    pe.wait_ge(sq_dve, idx + 1)
                    last = square_sums(KD // 2, False, True)
                else:
                    for c in (KD - 2, KD - 1):
                        pe.wait_ge(sq_ready, idx * KD + (c + 1))
                        last = square_sums(c, False, c == KD - 1)
                last.then_inc(sums_done, 1)
                pe.wait_ge(rstd_ready, idx + 1)
                spread(rstd, 0, mean_rows).then_inc(rows_ready, 1)

            def spread(col, at, rows):
                for t in range(NT1):
                    p0, n = tok_tile(t)
                    last = nc.tensor.matmul(rows[:, p0:p0 + n], col[:, at + t:at + t + 1].to_broadcast([P, P]),
                                            ident[:, 0:n], start=True, stop=True)
                return last

            pe.wait_ge(x_in, 16 * 6)
            for c in range(KD):
                if c >= 4:
                    pe.wait_ge(h_copied, c - 3)
                for t in range(4):
                    last = nc.tensor.transpose(ps[:, c % 4, P * t:P * t + P], x_tok[:, t, P * c:P * c + P], ident)
                last.then_inc(x_turned, 1)
            for c in range(KD):
                last = nc.tensor.transpose(ps[:, 4, N_META * c:N_META * (c + 1)],
                                           meta_tok[:, P * c:P * c + P], ident[0:N_META, 0:N_META])
            last.then_inc(x_turned, 1)
            pe.wait_ge(setup_in, n_setup[0])
            nc.tensor.transpose(ps[:, 5, 0:103], rows_vec[:, :], ident[0:103, 0:103])
            for l in range(DEPTH):
                nc.tensor.transpose(ps[:, 6, 124 * l:124 * l + 124], rows_conv[:, l, :], ident[0:124, 0:124])
            nc.tensor.transpose(ps[:, 7, 0:P], rows_dn, ident).then_inc(cols_turned, 1)

            with pe.Fori(0, DEPTH) as l:
                first = l * PANELS_L

                def glu_pair(n, glu_at, hn_at):
                    for s in range(2):
                        pe.wait_ge(w_split, n + (s + 3))
                        if hn_at is not None and s == 0:
                            for k in range(KD):
                                pe.wait_ge(hn_ready, hn_at + (k + 1))
                                for j in range(4):
                                    a = HALF * (j % 2)
                                    last = product(ps[:, j, 0:HALF], 0, k, j // 2, hn(hn_hi, k, a, HALF),
                                                   hn(hn_lo, k, a, HALF), k == 0, k == KD - 1)
                                    if k == KD - 1:
                                        last.then_inc(products_done, 1)
                            continue
                        for j in range(4):
                            oc, half = j // 2, j % 2
                            if glu_at is not None and s == 0:
                                pe.wait_ge(glu_used, glu_at + (j + 1))
                            for k in range(KD):
                                last = product(ps[:, 4 * s + j, 0:HALF], s, k, oc,
                                               hn(hn_hi, k, HALF * half, HALF),
                                               hn(hn_lo, k, HALF * half, HALF), k == 0, k == KD - 1)
                            last.then_inc(products_done, 1)

                norm(l * 2, l + 1)
                glu_pair(first, None, l * 2 * KD)
                glu_pair(first + 2, l * GLUS, None)
                pe.wait_ge(glu_used, l * GLUS + 8)
                f = 0
                for j in range(2):
                    pe.wait_ge(w_split, first + (4 + j + 3))
                    for t in range(NT1):
                        if f >= 6:
                            pe.wait_ge(qkv_copied, l * 26 + (f - 5))
                        for k in range(KD):
                            a = k * T1 + P * t
                            for i, (x, w) in enumerate(((hn_hi, whi), (hn_lo, whi), (hn_hi, wlo))):
                                last = nc.tensor.matmul(ps[:, f % 6, 0:PW], x[:, a:a + P],
                                                        w[:, j % 2, k * PW:(k + 1) * PW],
                                                        start=(k == 0 and i == 0), stop=(k == KD - 1 and i == 2))
                        last.then_inc(products_done, 1)
                        f += 1
                for j in range(4):
                    pe.wait_ge(w_split, first + (6 + j + 3))
                    for oc in range(2):
                        for half in range(2):
                            pe.wait_ge(qkv_copied, l * 26 + (f - 5))
                            for k in range(KD):
                                last = product(ps[:, f % 6, 0:HALF], j % 2, k, oc, hn(hn_hi, k, HALF * half, HALF),
                                               hn(hn_lo, k, HALF * half, HALF), k == 0, k == KD - 1)
                            last.then_inc(products_done, 1)
                            f += 1
                def raw(chunk, start, n):
                    return qk_raw.rearrange(flat)[:, chunk * T1 + start:chunk * T1 + start + n]

                pe.wait_ge(qkv_copied, l * 26 + 26)
                for m in range(KD):
                    chunk, b = m // 2 + 4 * (m % 2), 2 * (m % 3)
                    if m >= 3:
                        pe.wait_ge(rope_done, l * KD + (m - 2))
                    for half in range(2):
                        last = nc.tensor.matmul(ps[:, b + half, 0:HALF], rot, raw(chunk, HALF * half, HALF),
                                                start=True, stop=True)
                    last.then_inc(rot_done, 1)
                pe.wait_ge(conv_done, l * 3 + 3)
                pe.wait_ge(taps_added, l * GROUPS1 + GROUPS1)
                for t in range(NT1):
                    for c in range(4):
                        last = nc.tensor.matmul(ps[:, 6, t:t + 1], conv[:, c * T1 + P * t:c * T1 + P * t + P],
                                                ones[:, 0:1], start=(t == 0 and c == 0), stop=(c == 3),
                                                skip_group_check=True)
                last.then_inc(ln_sum, 1)
                pe.wait_ge(rope_done, l * KD + KD)
                pe.wait_ge(ln_mean, l + 1)
                spread(rms, 20, mean_rows).then_inc(ln_mean_rows, 1)
                def scores(u):
                    hd, t = u // NT1, u % NT1
                    p0, n = tok_tile(t)
                    if u >= 2:
                        pe.wait_ge(exp_done, l * TILES1 + (u if t in (0, 4) else u - 1))
                    keys = min(P * (t + 1), T1)
                    for c in range(2):
                        own = slice(64 * c, 64 * c + 64)
                        for b, a in enumerate(range(0, keys, 512)):
                            w = min(512, keys - a)
                            bank = 2 * (t % 2) + c if t < 4 else 2 * c + b
                            last = nc.tensor.matmul(ps[:, bank, 0:w], raw(hd, p0, P)[own, :], raw(4 + hd, a, w)[own, :],
                                                    start=True, stop=True)
                    last.then_inc(scored, 1)

                scores(0)
                scores(1)
                for u in range(TILES1):
                    hd, t = u // NT1, u % NT1
                    n = tok_tile(t)[1]
                    pe.wait_ge(diff_ready, l * TILES1 + (u + 1))
                    if u == 0:
                        pe.wait_ge(ln_mean_copied, l + 1)
                    if u >= 2:
                        pe.wait_ge(diff_t_ready, l * TILES1 + (u if t in (0, 4) else u - 1))
                    for b, (a, _) in enumerate(key_blocks(t)):
                        at = 512 * (4 + t % 2) + P * b
                        last = nc.tensor.transpose(line[:, at:at + P], diff[:, u % 2, a:a + P], ident)
                    last.then_inc(diff_turned, 1)
                    if u + 2 < TILES1:
                        scores(u + 2)
                    pe.wait_ge(diff_t_ready, l * TILES1 + (u + 1))
                    if u >= 2:
                        pe.wait_ge(o_copied, l * TILES1 + (u if t == 0 else u - 1))
                    if u == LN_AT:
                        pe.wait_ge(ln_sq, l + 1)
                        for i in range(NT1):
                            last = nc.tensor.matmul(ps[:, 6, 256 + i:257 + i], sq[:, 0, P * i:P * i + P], ones[:, 0:1],
                                                    start=True, stop=True)
                        last.then_inc(ln_stat, 1)
                    blocks = key_blocks(t)
                    for b, (_, w) in enumerate(blocks):
                        last = nc.tensor.matmul(ps[:, 6 + t % 2, 0:n], v_tok[0:w, b, P * hd:P * (hd + 1)],
                                                diff_t[0:w, u % 2, b * n:b * n + n],
                                                start=(b == 0), stop=(b == len(blocks) - 1))
                    last.then_inc(pv_done, 1)
                pe.wait_ge(exp_done, l * TILES1 + TILES1)
                pe.wait_ge(o_copied, l * TILES1 + TILES1)
                pe.wait_ge(ln_rstd, l + 1)
                spread(rstd, 20, mean_rows).then_inc(ln_rows, 1)
                for hd in range(HEADS1):
                    pe.wait_ge(sub_sq, l * 4 + (hd + 1))
                    for t in range(NT1):
                        last = nc.tensor.matmul(ps[:, 6, NT1 * hd + t:NT1 * hd + t + 1], sq[:, hd % 2, P * t:P * t + P],
                                                ones[:, 0:1], start=True, stop=True)
                    last.then_inc(sub_stat, 1)
                pe.wait_ge(sub_rstd, l + 1)
                for hd in range(HEADS1):
                    if hd >= 2:
                        pe.wait_ge(sub_t, l * 4 + (hd - 1))
                    spread(rstd, NT1 * hd, line[:, 1024 * (hd % 2):1024 * (hd % 2) + T1]).then_inc(sub_rows, 1)
                pe.wait_ge(ln_t, l * 4 + 4)
                pe.wait_ge(sub_t, l * 4 + 4)
                f = 0
                for j in range(4):
                    pe.wait_ge(w_split, first + (10 + j + 3))
                    for oc in range(2):
                        if f == 14:
                            pe.wait_ge(sq_dve, l * 2 + 2)
                            square_sums(0, True, False)
                        for half in range(2):
                            if f >= 6:
                                pe.wait_ge(h_added, l * ADDS + (f - 5))
                            for k in range(KD):
                                if f == 0:
                                    pe.wait_ge(mix_ready, l * KD + (k + 1))
                                last = product(ps[:, f % 6, 0:HALF], j % 2, k, oc, hn(hn_hi, k, HALF * half, HALF),
                                               hn(hn_lo, k, HALF * half, HALF), k == 0, k == KD - 1)
                            last.then_inc(products_done, 1)
                            f += 1
                norm(l * 2 + 1, None)
                at, glu_at = 14, 8
                for part, n in enumerate(FC):
                    with pe.Fori(0, n // 2) as i:
                        if part:
                            pe.wait_ge(h_added, l * ADDS + 32)
                        else:
                            pe.wait_ge(hn_ready, l * (2 * KD) + 2 * KD)
                        glu_pair(first + at + i * 2, l * GLUS + i * 4 + (glu_at - 4), None)
                    at += n
                    glu_at += 2 * n
                    with pe.Fori(0, 2) as bb:
                        pe.wait_ge(ff_ready, l * FFS + (sum(FC[:part + 1]) * 2 + 4))
                        for b in range(2):
                            for s in range(2):
                                pe.wait_ge(w_split, first + at + bb * 4 + (2 * b + s + 3))
                                for j in range(4):
                                    oc, half = j // 2, j % 2
                                    if s == 0:
                                        pe.wait_ge(h_added, l * ADDS + bb * 8 + (16 * part + 4 * b + j + 9))
                                    for k in range(n // 2):
                                        kf = s * n // 2 + k
                                        a = HALF * half
                                        last = product(ps[:, 4 * b + j, 0:HALF], s, k, oc, ff_hi[:, kf, a:a + HALF],
                                                       ff_lo[:, kf, a:a + HALF], kf == 0, kf == n - 1)
                                    if s == 1 or j == 3:
                                        last.then_inc(products_done, 1)
                    at += 8
            def norm2(idx):
                for i, (ready, n) in enumerate(((sq_pool, DEPTH + idx - M0 + 1), (sq_dve, idx + 1))):
                    pe.wait_ge(ready, n)
                    for t in range(NT2):
                        last = nc.tensor.matmul(ps[:, 6, t:t + 1], sq8[:, i * KD // 2, tile(t)], ones[:, 0:1],
                                                start=(i == 0 and t == 0), stop=(i == 1), skip_group_check=True)
                last.then_inc(sums_done, 1)
                pe.wait_ge(rstd_ready, idx + 1)
                spread2(rstd, 0, 4).then_inc(rows_ready, 1)

            def spread2(col, at, bank):
                for t in range(NT2):
                    last = nc.tensor.matmul(ps[:, bank, tile(t)], col[:, at + t:at + t + 1].to_broadcast([P, P]), ident,
                                            start=True, stop=True)
                return last

            def column_sums(c, at, bank=6):
                for t in range(NT2):
                    last = nc.tensor.matmul(ps[:, bank, at + t:at + t + 1], sq[:, c % 2, tile(t)], ones[:, 0:1],
                                            start=True, stop=True)
                return last

            def fill(bank, slot, oc, hi, lo):
                for k in range(KD):
                    last = product(ps[:, bank, :], slot, k, oc, hx(hi, k, 0, SEQ), hx(lo, k, 0, SEQ), k == 0, k == KD - 1)
                return last.then_inc(products_done, 1)

            norm2(M0)
            norm2(M0 + 1)
            pe.wait_ge(ws_ready, 1)
            pe.wait_ge(hn_ready, (M0 + 1) * KD)
            for t in range(NT2):
                for k in range(KD):
                    for i, (x, w) in enumerate(((hn_hi, ws_hi), (hn_lo, ws_hi), (hn_hi, ws_lo))):
                        last = nc.tensor.matmul(ps[:, 5, 64 * t:64 * t + 64], hx(x, k, P * t, P), w[:, 64 * k:64 * k + 64],
                                                start=(k == 0 and i == 0), stop=(k == KD - 1 and i == 2))
            last.then_inc(small_done, 1)
            with pe.Fori(0, PN_Z // 2) as i:
                for f in range(4):
                    if f % 2 == 0:
                        pe.wait_ge(w_split, i * 2 + (N0 + f // 2 + 3))
                    pe.wait_ge(qkv_copied, i * 4 + (Q0 + f - 3))
                    fill(f, f // 2, f % 2, hn_hi, hn_lo)
            pe.wait_ge(g_ready, 1)
            g = g_log.rearrange(flat)
            nc.tensor.matmul(ps[:, 5, 0:32], tri, g, start=True, stop=True)
            nc.tensor.matmul(ps[:, 5, 32:64], blk, g, start=True, stop=True).then_inc(gc_done, 1)
            for c in range(16):
                pe.wait_ge(l2_sq, c + 1)
                column_sums(c, NT2 * c).then_inc(l2_stat, 1)
            with pe.Fori(0, 2) as hg:
                def rows_of(t, i):
                    kind, bank = ((1, 1), (0, 2), (2, 3), (3, 0))[i]
                    pe.wait_ge(cur_ready, hg * NT2 + (t + 1))
                    for hh in range(HG):
                        last = nc.tensor.matmul(ps[:, bank, tile(hh)], cur[:, kind, hh:hh + 1].to_broadcast([P, P]), ident,
                                                start=True, stop=True)
                    last.then_inc(drows_done, 1)

                for i in range(4):
                    rows_of(0, i)
                for t in range(NT2):
                    it = hg * NT2 + t
                    pe.wait_ge(do_copied, it + 1)
                    pe.wait_ge(dv_ready, it + 1)
                    for hh in range(HG):
                        nc.tensor.transpose(ps[:, 5, tile(hh)], dv_t[:, hh, :], ident)
                    pe.wait_ge(dk_ready, it + 1)
                    for hh in range(HG):
                        last = nc.tensor.transpose(ps[:, 4, tile(hh)], dk_t[:, hh, :], ident)
                    last.then_inc(dturned, 1)
                    for hh in range(HG):
                        nc.tensor.matmul(ps[:, 6, tile(hh)], dk_t[:, hh, :], dkb_t[:, hh, :], start=True, stop=True)
                        last = nc.tensor.matmul(ps[:, 7, tile(hh)], dk_t[:, hh, :], dq_t[:, hh, :], start=True, stop=True)
                    last.then_inc(dkk_done, 1)
                    pe.wait_ge(da_ready, it + 1)
                    for n in range(LEVELS):
                        for pair in range(2):
                            if n:
                                pe.wait_ge(dx_ready, it * (2 * LEVELS) + (2 * n - 1 + pair))
                            for j in range(2):
                                hh = 2 * pair + j
                                last = nc.tensor.matmul(ps[:, pair, tile(j)], da_t[:, hh, :], dx[:, hh, :] if n else ident,
                                                        start=True, stop=True)
                            last.then_inc(p1_done, 1)
                        for pair in range(2):
                            pe.wait_ge(dp_ready, it * (2 * LEVELS) + (2 * n + 1 + pair))
                            for j in range(2):
                                hh = 2 * pair + j
                                if 0 < n < LEVELS - 1:
                                    nc.tensor.matmul(ps[:, 2 + pair, tile(j)], dx_t[:, hh, :], dp[:, hh, :],
                                                     start=True, stop=True)
                                last = nc.tensor.matmul(ps[:, 2 + pair, tile(2 + j)], dp[:, hh, :],
                                                        dx_t[:, hh, :] if n else ident, start=True, stop=True)
                            last.then_inc(delta_done, 1)
                    pe.wait_ge(dx_ready, it * (2 * LEVELS) + 2 * LEVELS)
                    for hh in range(HG):
                        last = nc.tensor.matmul(ps[:, 0, tile(hh)], dkbg[:, hh, :], dx_t[:, hh, :], start=True, stop=True)
                    last.then_inc(dw_done, 1)
                    if t + 1 < NT2:
                        rows_of(t + 1, 0)
                        rows_of(t + 1, 1)
                    pe.wait_ge(dqd_ready, it + 1)
                    for ch in range(2):
                        r = slice(CHUNK * ch, CHUNK * (ch + 1))
                        if ch == 0:
                            pe.wait_ge(dw_ready, it + 1)
                        else:
                            pe.wait_ge(state_ready, it * 2 + 1)
                        for hh in range(HG):
                            nc.tensor.matmul(ps[r, 4 + ch, tile(hh)], dw_t[:, hh, r], state[:, hh, :], start=True, stop=False)
                            last = nc.tensor.matmul(ps[r, 4 + ch, tile(hh)], dx_t[r, hh, r], dvb[r, hh, :],
                                                    start=False, stop=True)
                        last.then_inc(vn_done, 1)
                        if t + 1 < NT2:
                            rows_of(t + 1, 2 + ch)
                        for hh in range(HG):
                            c = P * hh + CHUNK * ch
                            nc.tensor.matmul(ps[:, 6, c:c + CHUNK], state[:, hh, :], dqd_t[:, hh, r],
                                             start=(ch == 0 and hh == 0), stop=False, skip_group_check=True)
                        pe.wait_ge(vn_ready, it * 2 + (ch + 1))
                        for hh in range(HG):
                            nc.tensor.matmul(ps[:, 7, tile(hh)], dke[r, hh, :], dvn[r, hh, :], start=True, stop=True)
                        for hh in range(HG):
                            c = P * hh + CHUNK * ch
                            last = nc.tensor.matmul(ps[:, 6, c:c + CHUNK], dvn[r, hh, :], dqk_t[r, hh, r],
                                                    start=False, stop=True, skip_group_check=True)
                        last.then_inc(s_done, 1)
            for c in range(DN_HEADS):
                pe.wait_ge(odn_sq, c + 1)
                column_sums(c, NT2 * c, 5).then_inc(odn_stat, 1)
            pe.wait_ge(odn_rstd, 1)
            for c in range(DN_HEADS):
                if c >= 2:
                    pe.wait_ge(odn_normed, c - 1)
                spread2(rstd, NT2 * c, 6 + c % 2).then_inc(odn_rows, 1)
                if c % 2 == 0:
                    pe.wait_ge(w_split, N0 + PN_Z + c // 2 + 3)
                if c >= 4:
                    pe.wait_ge(z_copied, c - 3)
                fill(c % 4, c // 2 % 2, c % 2, hn_hi, hn_lo)
            pe.wait_ge(z_copied, DN_HEADS)
            pe.wait_ge(odn_normed, DN_HEADS)
            f = 0
            items = 0

            def head_sums():
                nonlocal items
                pe.wait_ge(n_sq, items + 1)
                for t in range(NT2):
                    c = 2 * (NT2 * items + t)
                    last = nc.tensor.matmul(ps[:, 6, c:c + 2], sq[:, items % 2, tile(t)], halves, start=True, stop=True)
                last.then_inc(n_stat, 1)
                items += 1

            for pn in range(PN_NQ, PN_VS):
                pe.wait_ge(w_split, N0 + pn + 3)
                for oc in range(2):
                    if f >= 4:
                        pe.wait_ge(nsa_copied, f - 3)
                    fill(f % 4, pn % 2, oc, hn_hi, hn_lo)
                    f += 1
                    if 2 <= f <= 9 or f >= 13:
                        head_sums()

            def head_rows_of(m):
                if m >= 2:
                    pe.wait_ge(n_scaled, m - 1)
                for t in range(NT2):
                    for i in range(2):
                        c = 2 * (NT2 * m + t) + i
                        last = nc.tensor.matmul(ps[HD * i:HD * (i + 1), 4 + m % 2, tile(t)],
                                                n_rstd[:, c:c + 1].to_broadcast([P, HD]), ident, start=True, stop=True)
                last.then_inc(n_rows, 1)

            for j in range(2):
                pe.wait_ge(w_split, N0 + PN_VS + j + 3)
                for t in range(NT2):
                    pe.wait_ge(nsa_copied, f - 3)
                    for k in range(KD):
                        for i, (x, w) in enumerate(((hn_hi, whi), (hn_lo, whi), (hn_hi, wlo))):
                            last = nc.tensor.matmul(ps[:, f % 4, 0:PW], hx(x, k, P * t, P),
                                                    w[:, (PN_VS + j) % 2, k * PW:(k + 1) * PW],
                                                    start=(k == 0 and i == 0), stop=(k == KD - 1 and i == 2))
                    last.then_inc(products_done, 1)
                    f += 1
                    if j == 0 and t < 12 - 10:
                        head_sums()
                    if j == 1:
                        if t == 0:
                            pe.wait_ge(n_rstd_ready, 1)
                        for m in range(3 * t, 3 * t + 3):
                            head_rows_of(m)

            def hidden(pos):
                for m in range(16):
                    nc.tensor.matmul(ps[:, 7, 0:GROUPS * N_CMP], w1[:, m, :],
                                     kcmp[:, :, 2 * m:2 * m + 16 * (N_CMP - 1) + 1:16], start=(m == 0), stop=(m == 15))
                for m in range(16):
                    last = nc.tensor.matmul(ps[:, 7, 256:257], w1[:, m, :], dn_cols[:, pos + m:pos + m + 1],
                                            start=(m == 0), stop=(m == 15))
                last.then_inc(hidden_done, 1)

            pe.wait_ge(w1_in, 16)
            pe.wait_ge(nsa_copied, 10)
            hidden(96)
            pe.wait_ge(w_split, N0 + PN_VC + 3)
            for oc in range(2):
                pe.wait_ge(nsa_copied, f - 3)
                fill(f % 4, PN_VC % 2, oc, hn_hi, hn_lo)
                f += 1
                if oc == 0:
                    pe.wait_ge(gelu_ready, 1)
                    nc.tensor.matmul(ps[:, 7, P:2 * P], w2k, c_gelu, start=True, stop=True).then_inc(kc_done, 1)
            pe.wait_ge(kc_sq, 1)
            nc.tensor.matmul(ps[:, 6, 96:97], sq[:, 0, 0:P], halves[:, 0:1], start=True, stop=True).then_inc(kc_stat, 1)
            pe.wait_ge(w1_in, 32)
            pe.wait_ge(nsa_copied, f)
            hidden(112)
            pe.wait_ge(kc_rstd, 1)
            nc.tensor.matmul(ps[:, 5, 0:P], n_rstd[:, 96:97].to_broadcast([P, P]), ident, start=True, stop=True
                             ).then_inc(kc_rows, 1)
            pe.wait_ge(gelu_ready, 2)
            for g in range(GROUPS):
                for r in range(REP):
                    last = nc.tensor.matmul(ps[32 * r:32 * r + 32, 4, HD * g:HD * (g + 1)],
                                            c_gelu[:, N_CMP * g:N_CMP * g + 32], w2v, start=True, stop=True)
            last.then_inc(vc_done, 1)
            pe.wait_ge(kc_ready, 1)
            pe.wait_ge(vc_ready, 1)
            with pe.Fori(0, GROUPS) as g:
                def query(t, r):
                    hp = HD * (r % 2)
                    return slice(hp, hp + HD), q_grp[hp:hp + HD, r // 2, tile(t)]

                def selected_scores(t):
                    if t == 0:
                        pe.wait_ge(kg_ready, g + 1)
                    else:
                        pe.wait_ge(tops_ready, g * (2 * NT2) + 2 * t)
                    for r in range(REP):
                        rows, q = query(t, r)
                        last = nc.tensor.matmul(ps[:, r, 0:P * (t + 1)], q, k_grp[rows, 0, 0:P * (t + 1)],
                                                start=True, stop=True)
                        last.then_inc(slc_scored, 1)

                def window_scores(t):
                    for r in range(REP):
                        rows, q = query(t, r)
                        a, w = first_key(t), P * (t + 1) - first_key(t)
                        pe.wait_ge(slc_read, g * (REP * NT2) + (REP * t + r + 1))
                        nc.tensor.matmul(ps[:, r, 0:w], q, k_grp[rows, 1, a:a + w], start=True, stop=True)
                        last = nc.tensor.matmul(ps[:, r, SEQ - P:SEQ - P + N_CMP], q, kc_grp[rows, :], start=True, stop=True)
                        last.then_inc(win_scored, 1)

                def outputs(t, part):
                    n = sum(BLOCKS[:t])
                    slot = t % 2
                    blocks = [(p_slc[slot], 0, b, P * b) for b in range(t + 1)]
                    blocks += [(p_win[slot], 1, first_key(t) // P + b, P * b) for b in range(min(t + 1, 3))]
                    blocks.append((p_cmp[slot], None, None, 0))

                    def turn(i):
                        p, branch, b, at = blocks[i]
                        if n + i >= 2:
                            pe.wait_ge(p_t_ready, g * BLOCKS_G + (n + i - 1))
                        if branch is None:
                            last = nc.tensor.transpose(ps[:, 4 + (n + i) % 2, 0:P], p.rearrange(flat), ident)
                        else:
                            for r in range(REP):
                                last = nc.tensor.transpose(ps[:, 4 + (n + i) % 2, tile(r)], p[:, r, at:at + P], ident)
                        last.then_inc(p_turned, 1)

                    own = range(0, t + 1) if part == 0 else range(t + 1, len(blocks))
                    pe.wait_ge(p_ready, g * (2 * NT2) + (2 * t + part + 1))
                    if t == 0 and part == 0:
                        pe.wait_ge(vg_ready, g + 1)
                    turn(own[0])
                    for i in own:
                        p, branch, b, at = blocks[i]
                        if i + 1 in own:
                            turn(i + 1)
                        pe.wait_ge(p_t_ready, g * BLOCKS_G + (n + i + 1))
                        if branch is None:
                            last = nc.tensor.matmul(ps[0:HD, 6, :], vc_grp, pc_t, start=False, stop=True, skip_group_check=True)
                        else:
                            last = nc.tensor.matmul(ps[0:HD, 6, :], v_grp[:, branch, b, :], p_t[:, (n + i) % 2, :],
                                                    start=(i == 0), stop=False, skip_group_check=True)
                        last.then_inc(pv2_done, 1)

                selected_scores(0)
                window_scores(0)
                for t in range(NT2):
                    if t + 1 < NT2:
                        selected_scores(t + 1)
                    outputs(t, 0)
                    if t + 1 < NT2:
                        window_scores(t + 1)
                    outputs(t, 1)
                pe.wait_ge(att_copied, g * NT2 + NT2)
            for at, ready in ((PN_MDN, 0), (PN_MNS, KD)):
                for j in range(4):
                    b = 4 * (j % 2)
                    pairs = (at - PN_MDN) // 2 + j
                    pe.wait_ge(w_split, N0 + at + 2 * j + 3)
                    if pairs >= 2:
                        pe.wait_ge(merged_part, 2 * pairs - 2)
                    else:
                        pe.wait_ge(att_copied, GROUPS * NT2)
                    for oc in range(2):
                        fill(b + oc, 0, oc, hn_hi, hn_lo)
                    pe.wait_ge(w_split, N0 + at + 2 * j + 4)
                    if j == 0:
                        pe.wait_ge(o_ready, ready + KD)
                    for oc in range(2):
                        fill(b + 2 + oc, 1, oc, o_hi.rearrange(flat), o_lo.rearrange(flat))
            pe.wait_ge(merged_part, 16)
            for f in range(KD):
                if f % 2 == 0:
                    pe.wait_ge(w_split, N0 + PN_WO + f // 2 + 3)
                for k in range(KD):
                    if f == 0:
                        pe.wait_ge(merged_ready, k + 1)
                    last = product(ps[:, f, :], f // 2 % 2, k, f % 2, hx(hn_hi, k, 0, SEQ), hx(hn_lo, k, 0, SEQ),
                                   k == 0, k == KD - 1)
                last.then_inc(products_done, 1)
            pe.wait_ge(x2_added, KD)
            norm2(M0 + 2)
            for part in range(2):
                with pe.Fori(0, 4) as i:
                    for f in range(4):
                        if part == 0 and f == 0:
                            pe.wait_ge(hn_ready, (M0 + 2) * KD)
                        if f % 2 == 0:
                            pe.wait_ge(w_split, i * 2 + (N0 + PN_UP[part] + f // 2 + 3))
                        if part:
                            pe.wait_ge(x2_added, 2 * KD)
                        pe.wait_ge(relu_sq_ready, i * 4 + (16 * part + f + 1))
                        fill(f, f // 2, f % 2, hn_hi, hn_lo)
                pe.wait_ge(relu_sq_ready, 16 * part + 20)
                def down(panel_at, slot, first, kf):
                    pe.wait_ge(w_split, panel_at + 3)
                    for kk in range(2):
                        x_hi = f_hi[:, kf(kk), :].rearrange(flat)
                        x_lo = f_lo[:, kf(kk), :].rearrange(flat)
                        for c in range(KD):
                            w0 = D * kk + P * c
                            for j, (w, x) in enumerate(((whi, x_hi), (whi, x_lo), (wlo, x_hi))):
                                last = nc.tensor.matmul(ps[:, c, :], w[:, slot, w0:w0 + P], x,
                                                        start=(first and kk == 0 and j == 0), stop=False,
                                                        skip_group_check=True)
                    last.then_inc(products_done, 1)

                pe.wait_ge(f_ready, 16 * part + 16 + 2)
                first_panel = N0 + PN_DN[part]
                for s in range(2):
                    down(first_panel + s, s, s == 0, lambda kk: slice(2 * s + kk, 2 * s + kk + 1))
                with pe.Fori(1, 4) as i:
                    for s in range(2):
                        down(i * 2 + (first_panel + s), s, False, lambda kk: ds(i * 4 + (2 * s + kk), 1))
            for c in range(KD):
                pe.wait_ge(x2_added, 2 * KD + c + 1)
                for t in range(NT2):
                    last = nc.tensor.transpose(ps[:, c, tile(t)], x2[:, c, tile(t)], ident)
                last.then_inc(y_turned, 1)

        @block.scalar
        def _(act):
            loads = []

            def rows(a):
                return a.rearrange("(r w) -> r w", w=P)

            for l in range(DEPTH):
                for name, at in (("norm1_g", 0), ("norm2_g", 8), ("b_glu", 16), ("conv_b", 24),
                                 ("conv_ln_g", 28), ("conv_ln_b", 32), ("subln_g", 36)):
                    src = rows(A[name][l])
                    loads.append((rows_vec[37 * l + at:37 * l + at + src.shape[0], :], src))
                loads.append((rows_conv[:, l, :], A["conv_w"][l].rearrange("j (c w) -> (j c) w", w=P)))
            for name, at in (("final_g", FINAL), ("norm_mix_2", NORM_MIX), ("norm_mlp_2", NORM_MLP),
                             ("dn_out_norm_2", DN_OUT)):
                src = rows(A[name] if name == "final_g" else A[name][0])
                loads.append((rows_vec[at:at + src.shape[0], :], src))
            for name, at in (("nsa_q_norm_2", QN), ("nsa_k_norm_cmp_2", KC_N),
                             ("nsa_k_norm_slc_2", KS_N), ("nsa_k_norm_win_2", KW_N)):
                for half in range(2):
                    loads.append((rows_vec[at:at + 1, 64 * half:64 * half + 64], A[name]))
            loads.append((rows_dn[0:96, :], A["dn_conv_2"][0].rearrange("j (c w) -> (j c) w", w=P)))
            loads.append((rows_dn[96:112, :], A["cmp_pos_k_2"][0].rearrange("(m a) w -> m (a w)", a=2)))
            loads.append((rows_dn[112:128, :], A["cmp_pos_v_2"][0].rearrange("(m a) w -> m (a w)", a=2)))
            for i, name in enumerate(("lam_q1", "lam_k1", "lam_q2", "lam_k2")):
                loads.append((lam_rows[:, i, :], A[name].rearrange("a b -> (a b)").partition_broadcast(P)))
            n_setup[0] = 16 * len(loads)
            for dst, src in loads:
                act.dma_start(dst, src).then_inc(setup_in, 16)
            w_in_2 = A["w_in_2"][0].rearrange("(k p) n -> p k n", p=P)
            loads = [(const2, table2), (w_small[:, :, 0:16], w_in_2[:, :, C_BA:C_BA + 16]),
                     (w_small[:, :, 16:64], w_in_2[:, :, C_GATE:C_GATE + 48])]
            for i, name in enumerate(("dn_a_log_2", "dn_dt_bias_2")):
                loads.append((head_rows[:, i, :], A[name][0].partition_broadcast(P)))
            for half in range(2):
                loads.append((w2k[:, HD * half:HD * (half + 1)], A["cmp_w2_k_2"][0]))
            loads.append((w2v, A["cmp_w2_v_2"][0]))
            n_tables[0] = 16 * len(loads)
            for dst, src in loads:
                act.dma_start(dst, src).then_inc(tables_in, 16)

            def upper(use, slot, used):
                act.wait_ge(raw_in[slot], use * 16 + 16)
                if used is not None:
                    act.wait_ge(products_done, used)
                nc.scalar.copy(whi[:, slot, :], wraw[:, slot, :]).then_inc(w_hi, 1)

            def squares_of(idx, chunks, ready=None):
                for c in chunks:
                    if ready is not None:
                        act.wait_ge(h_added, ready + (2 * c + 2))
                    nc.scalar.activation(sq8[:, c, 0:T1], h[:, c, :], ACT.Square).then_inc(sq_ready, 1)

            def norm(idx):
                act.wait_ge(sums_done, idx + 1)
                nc.scalar.activation(rms[:, 0:NT1], ps[:, 6, 0:NT1], ACT.Sqrt, bias=eps5,
                                     scale=1.0 / D).then_inc(rms_ready, 1)
                for c in range(KD):
                    act.wait_ge(t_ready, idx * KD + (c + 1))
                    nc.scalar.copy(hn(hn_hi, c, 0, T1), t_chunk[:, c % 2, :]).then_inc(hi_ready, 1)

            act.wait_ge(lam_dots, 1)
            nc.scalar.activation(lam_exp, lam_dot, ACT.Exp).then_inc(lam_exps, 1)
            for s in range(2):
                upper(0, s, None)

            with act.Fori(0, DEPTH) as l:
                use0 = l * (PANELS_L // 2)
                ev = l * EVENTS

                act.wait_ge(h_ready, l + 1)
                squares_of(l * 2, range(KD))
                norm(l * 2)
                def tap_products(j):
                    i = j - 2
                    if not 0 <= i < GROUPS1:
                        return
                    if i == 0:
                        act.wait_ge(glu_used, l * GLUS + 2)
                    else:
                        act.wait_ge(taps_added, l * GROUPS1 + i)
                    for m in range(GROUP):
                        tap = EARLY + GROUP * i + m
                        last = nc.scalar.activation(tap_prod[:, m, :], z[:, 0, tap:tap + T1], ACT.Copy,
                                                    scale=lay_conv[:, 4 * tap:4 * tap + 1])
                    last.then_inc(taps_ready, 1)

                for p in range(2):
                    for j in range(4):
                        act.wait_ge(products_done, ev + (EV_GLU + 8 * p + j + 1))
                        nc.scalar.activation(glu_gate[:, j, :], ps[:, j, 0:HALF], ACT.Sigmoid,
                                             bias=lay[:, VEC["gate_bias"] + 2 * p + j // 2:][:, 0:1]
                                             ).then_inc(gate_act, 1)
                    tap_products(2 * p)
                    upper(use0 + (p + 1), 0, ev + (EV_GLU + 8 * p + 4))
                    tap_products(2 * p + 1)
                    upper(use0 + (p + 1), 1, ev + (EV_GLU + 8 * p + 8))
                f = 0
                for j in range(2):
                    for t in range(NT1):
                        n = tok_tile(t)[1]
                        act.wait_ge(products_done, ev + (EV_V + f + 1))
                        nc.scalar.copy(v_tok[0:n, t, PW * j:PW * (j + 1)], ps[0:n, f % 6, 0:PW]).then_inc(qkv_copied, 1)
                        f += 1
                    tap_products(4 + j)
                    upper(use0 + 3, j, ev + (EV_V + f))
                for j in range(4):
                    for oc in range(2):
                        for half in range(2):
                            act.wait_ge(products_done, ev + (EV_V + f + 1))
                            nc.scalar.copy(qk_raw[:, 2 * j + oc, HALF * half:HALF * (half + 1)],
                                           ps[:, f % 6, 0:HALF]).then_inc(qkv_copied, 1)
                            f += 1
                    tap_products(6 + j)
                    upper(use0 + (4 + j // 2), j % 2, ev + (EV_V + f))
                def exponentials(u):
                    t = u % NT1
                    n = tok_tile(t)[1]
                    keys = min(P * (t + 1), T1)
                    act.wait_ge(max_ready, l * TILES1 + (u + 1))
                    if u >= 2:
                        act.wait_ge(diff_ready, l * TILES1 + (u - 1))
                    s = scores_of(t)
                    for c in range(2):
                        last = nc.scalar.activation(probs4[0:n, u % 2, c, 0:keys], s[:, c, :], ACT.Exp,
                                                    bias=neg_top[0:n, u % 2, c:c + 1], scale=0.125,
                                                    accum_out=mass[0:n, u % 2, c:c + 1])
                    last.then_inc(exp_done, 1)

                act.wait_ge(ln_sum, l + 1)
                nc.scalar.activation(rms[:, 20:20 + NT1], ps[:, 6, 0:NT1], ACT.Copy, scale=1.0 / 512).then_inc(ln_mean, 1)
                act.wait_ge(ln_mean_rows, l + 1)
                nc.scalar.copy(mean_sb, mean_rows).then_inc(ln_mean_copied, 1)
                exponentials(0)
                for u in range(TILES1):
                    hd, t = u // NT1, u % NT1
                    p0, n = tok_tile(t)
                    if u + 1 < TILES1:
                        exponentials(u + 1)
                    act.wait_ge(diff_turned, l * TILES1 + (u + 1))
                    if u >= 2:
                        act.wait_ge(pv_done, l * TILES1 + (u - 1))
                    w = n * len(key_blocks(t))
                    at = 512 * (4 + t % 2)
                    turned = line[:, at:at + P * len(key_blocks(t))].rearrange("p (b n) -> p b n", n=P)
                    nc.scalar.copy(diff_t[:, u % 2, 0:w].rearrange("p (b n) -> p b n", n=n),
                                   turned[:, :, 0:n]).then_inc(diff_t_ready, 1)
                    act.wait_ge(pv_done, l * TILES1 + (u + 1))
                    if u == LN_AT:
                        act.wait_ge(ln_stat, l + 1)
                        nc.scalar.activation(rms[:, 20:20 + NT1], ps[:, 6, 256:256 + NT1], ACT.Sqrt, bias=eps5,
                                             scale=1.0 / 512).then_inc(ln_rms, 1)
                    nc.scalar.copy(o_raw[:, hd, p0:p0 + n], ps[:, 6 + t % 2, 0:n]).then_inc(o_copied, 1)
                act.drain()
                for hd in range(HEADS1):
                    if hd >= 2:
                        act.wait_ge(sub_stat, l * 4 + (hd - 1))
                    nc.scalar.activation(sq[:, hd % 2, 0:T1], o_raw[:, hd, :], ACT.Square).then_inc(sub_sq, 1)
                act.wait_ge(sub_stat, l * 4 + 4)
                nc.scalar.activation(rms[:, 0:4 * NT1], ps[:, 6, 0:4 * NT1], ACT.Sqrt, bias=eps5,
                                     scale=1.0 / P).then_inc(sub_rms, 1)
                for c in range(4):
                    act.wait_ge(ln_t, l * 4 + (c + 1))
                    nc.scalar.activation(conv[:, c * T1:(c + 1) * T1], conv[:, c * T1:(c + 1) * T1], ACT.Silu,
                                         bias=lay[:, VEC["ln_b"] + c:][:, 0:1],
                                         scale=lay[:, VEC["ln_g"] + c:][:, 0:1]).then_inc(ln_silu, 1)
                for j in range(4):
                    upper(use0 + (6 + j // 2), j % 2, ev + (EV_OUT + 4 * j + 4))
                    squares_of(l * 2 + 1, (2 * j, 2 * j + 1), l * ADDS)
                norm(l * 2 + 1)
                use, glu_at = 7, 8
                for part, n in enumerate(FC):
                    with act.Fori(0, n // 2) as i:
                        e = ev + EV_FF[part] + i * 8
                        for j in range(4):
                            act.wait_ge(products_done, e + (j + 1))
                            nc.scalar.activation(glu_gate[:, j, :], ps[:, j, 0:HALF], ACT.Silu).then_inc(gate_act, 1)
                        for s in range(2):
                            upper(use0 + use + i + 1, s, e + (4 * s + 4))
                    use += n // 2
                    with act.Fori(0, 4) as b:
                        e = ev + EV_DOWN[part] + b * 5
                        for s in range(2):
                            upper(use0 + use + b + 1, s, e + (4 * s + 1))
                    use += 4
            def follow(pn, event):
                n = N0 + pn + 2
                upper(n // 2, n % 2, E0 + event)

            def square(c, src, ready):
                nc.scalar.activation(sq[:, c % 2, 0:SEQ], src, ACT.Square).then_inc(ready, 1)

            def norm2(idx, src, eps, split):
                for c in range(KD):
                    src_ready, value = src(c)
                    act.wait_ge(*src_ready)
                    nc.scalar.activation(sq8[:, c, 0:SEQ], value, ACT.Square).then_inc(sq_ready, 1)
                act.wait_ge(sums_done, idx + 1)
                nc.scalar.activation(rms[:, 0:NT2], ps[:, 6, 0:NT2], ACT.Sqrt, bias=eps, scale=1.0 / D
                                     ).then_inc(rms_ready, 1)
                if split is not None:
                    for c in range(KD):
                        act.wait_ge(t_ready, split * KD + (c + 1))
                        nc.scalar.copy(hx(hn_hi, c, 0, SEQ), t2[:, c % 2, :]).then_inc(hi_ready, 1)

            norm2(M0, lambda c: ((h_ready, X0), h[:, c, N_META:T1]), eps5, None)
            act.wait_ge(tables_in, n_tables[0])
            nc.scalar.copy(ws_hi, w_small.rearrange(flat)).then_inc(ws_hi_ready, 1)
            norm2(M0 + 1, lambda c: ((x2_ready, c + 1), x2[:, c, :]), eps6, M0)
            act.wait_ge(small_done, 1)
            small = ps[:, 5, 0:NT2 * 64].rearrange("p (t n) -> p t n", t=NT2)
            nc.scalar.activation(gates, small[:, :, 16:64], ACT.Sigmoid)
            nc.scalar.activation(beta, small[:, :, 0:DN_HEADS], ACT.Sigmoid).then_inc(small_act, 1)
            nc.scalar.activation(a_exp[:, 0, :], head_rows[:, 0, :], ACT.Exp)
            act.wait_ge(a_abs_ready, 1)
            nc.scalar.activation(a_ln.rearrange(flat), a_abs.rearrange(flat), ACT.Exp, scale=-1.0)
            act.drain()
            nc.scalar.activation(a_ln.rearrange(flat), a_ln.rearrange(flat), ACT.Ln, bias=ones[:, 0:1]).then_inc(a_ln_ready, 1)
            with act.Fori(0, PN_Z // 2) as i:
                def swish(f):
                    act.wait_ge(dconv_done, i * 4 + (f + 3))
                    nc.scalar.activation(qkv[:, ds(i * 4 + f, 1), :].rearrange(flat), taps_sum[:, f % 2, :], ACT.Silu
                                         ).then_inc(silu_done, 1)

                for f in range(4):
                    act.wait_ge(products_done, i * 4 + (E0 + f + 1))
                    act.wait_ge(dconv_done, i * 4 + (f + 1))
                    nc.scalar.copy(taps[:, f % 2, 3:], ps[:, f, :]).then_inc(qkv_copied, 1)
                    if f % 2:
                        upper(i + (N0 + 2) // 2, f // 2, i * 4 + (E0 + f + 1))
                    if f:
                        swish(f - 1)
                swish(3)
            act.drain()
            for c in range(16):
                if c >= 2:
                    act.wait_ge(l2_stat, c - 1)
                square(c, qkv[:, c, :], l2_sq)
            act.wait_ge(gc_done, 1)
            nc.scalar.copy(g_cum.rearrange(flat), ps[:, 5, 0:32]).then_inc(gc_copied, 1)
            act.wait_ge(l2_stat, 16)
            nc.scalar.activation(l2_rms.rearrange(flat), ps[:, 6, 0:64], ACT.Sqrt, bias=eps6).then_inc(l2_rms_ready, 1)
            act.drain()
            nc.scalar.activation(g_exp.rearrange(flat), g_cum.rearrange(flat), ACT.Exp)
            act.wait_ge(g_rest_ready, 1)
            nc.scalar.activation(ke_exp.rearrange(flat), g_rest.rearrange(flat), ACT.Exp).then_inc(decays_ready, 1)
            with act.Fori(0, 2) as hg:
                def values(t):
                    nc.scalar.activation(dv_t, qkv[:, ds(hg * HG + 16, HG), tile(t)], ACT.Copy).then_inc(dv_ready, 1)

                def decays(t):
                    act.wait_ge(dec_ready, hg * NT2 + (t + 1))
                    nc.scalar.activation(decay, decay, ACT.Exp)
                    nc.scalar.activation(g_rows[t % 2].rearrange(flat), ps[:, 0, :], ACT.Exp).then_inc(dexp_done, 1)

                values(0)
                decays(0)
                for t in range(NT2):
                    it = hg * NT2 + t
                    act.wait_ge(dw_done, it + 1)
                    nc.scalar.mul(dw_t, by_head(0), -1.0).then_inc(dw_ready, 1)
                    if t + 1 < NT2:
                        values(t + 1)
                    for ch in range(2):
                        r = slice(CHUNK * ch, CHUNK * (ch + 1))
                        act.wait_ge(vn_done, it * 2 + (ch + 1))
                        nc.scalar.copy(dvn[r, :, :], by_head(4 + ch)[r, :, :]).then_inc(vn_ready, 1)
                    if t + 1 < NT2:
                        decays(t + 1)
            act.wait_ge(do_copied, 2 * NT2 + 1)
            for c in range(DN_HEADS):
                if c >= 2:
                    act.wait_ge(odn_stat, c - 1)
                square(c, qkv[:, 16 + c, :], odn_sq)
            act.wait_ge(odn_stat, DN_HEADS)
            nc.scalar.activation(rms, ps[:, 5, 0:32], ACT.Sqrt, bias=eps6, scale=1.0 / P).then_inc(odn_rms, 1)
            for c in range(DN_HEADS):
                act.wait_ge(products_done, E0 + EV_Z + c + 1)
                if c >= 2:
                    act.wait_ge(odn_ready, c - 1)
                nc.scalar.activation(z_act[:, c % 2, :], ps[:, c % 4, :], ACT.Silu).then_inc(z_copied, 1)
                if c % 2:
                    follow(PN_Z + c // 2, EV_Z + c + 1)
            f = 0
            items = 0

            def raw_head(dst, bank):
                nonlocal items
                nc.scalar.copy(dst, ps[:, bank, :])
                if items >= 2:
                    act.wait_ge(n_stat, items - 1)
                square(items, ps[:, bank, :], n_sq)
                act.drain().then_inc(nsa_copied, 1)
                items += 1

            def to_compress(bank, oc):
                for i in range(2):
                    src = ps[HD * i:HD * (i + 1), bank, :]
                    nc.scalar.copy(kcmp[0:HD, 2 * oc + i, :], src)
                    nc.scalar.copy(kcmp[HD:P, 2 * oc + i, 0:SEQ - 1], src[:, 1:SEQ])
                act.drain().then_inc(nsa_copied, 1)

            act.wait_ge(odn_ready, DN_HEADS)
            for pn in range(PN_NQ, PN_VS):
                for oc in range(2):
                    act.wait_ge(products_done, E0 + EV_NQ + f + 1)
                    if pn < PN_KC:
                        raw_head(nq[:, f, :], f % 4)
                    elif pn == PN_KC:
                        to_compress(f % 4, oc)
                    else:
                        raw_head(k_raw[:, f - 10, :], f % 4)
                    f += 1
                follow(pn, EV_NQ + f)
            for j, dst in enumerate((vs, vw)):
                for t in range(NT2):
                    act.wait_ge(products_done, E0 + EV_NQ + f + 1)
                    nc.scalar.copy(dst[:, t, :], ps[:, f % 4, 0:PW]).then_inc(nsa_copied, 1)
                    f += 1
                    if j == 0 and t == 2:
                        act.wait_ge(n_stat, 12)
                        nc.scalar.activation(n_rms[:, 0:96], ps[:, 6, 0:96], ACT.Sqrt, bias=eps6, scale=1.0 / HD
                                             ).then_inc(n_rms_ready, 1)
                follow(PN_VS + j, EV_NQ + f)

            def gelu(n):
                act.wait_ge(hidden_done, n)
                nc.scalar.copy(pos_sum, ps[:, 7, 256:257])
                act.drain()
                nc.scalar.activation(c_gelu[:, 0:GROUPS * N_CMP], ps[:, 7, 0:GROUPS * N_CMP], ACT.Gelu_apprx_tanh,
                                     bias=pos_sum)
                act.drain().then_inc(gelu_ready, 1)

            act.wait_ge(n_scaled, 12)
            act.wait_ge(c_pad_ready, 1)
            gelu(1)
            act.wait_ge(products_done, E0 + EV_VC + 1)
            act.wait_ge(hidden_done, 1)
            to_compress(f % 4, 0)
            f += 1
            act.wait_ge(kc_done, 1)
            nc.scalar.copy(kc_raw, ps[:, 7, P:2 * P])
            nc.scalar.activation(
                sq[:, 0, 0:P], ps[:, 7, P:2 * P], ACT.Square)
            act.drain().then_inc(kc_sq, 1)
            act.wait_ge(products_done, E0 + EV_VC + 2)
            to_compress(f % 4, 1)
            f += 1
            follow(PN_VC, EV_VC + 2)
            act.wait_ge(kc_stat, 1)
            nc.scalar.activation(n_rms[:, 96:97], ps[:, 6, 96:97], ACT.Sqrt, bias=eps6, scale=1.0 / HD).then_inc(kc_rms, 1)
            gelu(2)
            act.wait_ge(vc_done, 1)
            nc.scalar.copy(vc, ps[:, 4, 0:PW].rearrange("p (g d) -> p g d", g=GROUPS)).then_inc(vc_ready, 1)
            act.wait_ge(n_scaled, 12)
            with act.Fori(0, GROUPS) as g:
                def exponentials(t, part):
                    slot = t % 2
                    branches = ((0, p_slc[slot], P * (t + 1)), (1, p_win[slot], P * min(t + 1, 3)), (2, p_cmp[slot], N_CMP))
                    act.wait_ge(tops_ready, g * (2 * NT2) + (2 * t + part + 1))
                    for i, p, w in branches[0:1] if part == 0 else branches[1:]:
                        for r in range(REP):
                            nc.scalar.activation(p[:, r, 0:w], p[:, r, 0:w], ACT.Exp, bias=s_neg[:, i, r:r + 1],
                                                 accum_out=s_mass[:, i, r:r + 1])
                    act.drain().then_inc(exps_done, 1)

                def copies(t, part):
                    n, bank = sum(BLOCKS[:t]), 4
                    for i in range(0, t + 1) if part == 0 else range(t + 1, BLOCKS[t]):
                        act.wait_ge(p_turned, g * BLOCKS_G + (n + i + 1))
                        act.wait_ge(pv2_done, g * BLOCKS_G + max(1, n + i))
                        bank = 4 + (n + i) % 2
                        if i < BLOCKS[t] - 1:
                            nc.scalar.copy(p_t[:, (n + i) % 2, :], ps[:, bank, :]).then_inc(p_t_ready, 1)
                        else:
                            for r in range(REP):
                                rows = slice(32 * r, 32 * r + 32)
                                nc.scalar.copy(pc_t[rows, tile(r)], ps[rows, bank, 0:P])
                            act.drain().then_inc(p_t_ready, 1)

                for part in range(2):
                    exponentials(0, part)
                for t in range(NT2):
                    for part in range(2):
                        copies(t, part)
                        if t + 1 < NT2:
                            exponentials(t + 1, part)
            act.wait_ge(att_copied, GROUPS * NT2)

            def split_out(src):
                for c in range(KD):
                    nc.scalar.copy(o_hi[:, c, :], src(c)).then_inc(o_hi_ready, 1)

            split_out(lambda c: qkv[:, 16 + c, :])
            for m, (pn, ev) in enumerate(((PN_MDN, EV_MDN), (PN_MNS, EV_MNS))):
                for j in range(4):
                    b = 4 * (j % 2)
                    for oc in range(2):
                        act.wait_ge(products_done, E0 + ev + 4 * j + oc + 1)
                        if 4 * m + j >= 1:
                            act.wait_ge(merged_part, 2 * (4 * m + j) + oc - 1)
                        nc.scalar.activation(sig[:, oc, :], ps[:, b + oc, :], ACT.Sigmoid).then_inc(sig_ready, 1)
                    follow(pn + 2 * j, ev + 4 * j + 2)
                    follow(pn + 2 * j + 1, ev + 4 * j + 4)
                if m == 0:
                    split_out(lambda c: nq[:, c, :])
            for c in range(KD):
                act.wait_ge(merged_part, KD + c + 1)
                nc.scalar.copy(hx(hn_hi, c, 0, SEQ), merged[:, c, :]).then_inc(merged_hi, 1)
            for j in range(4):
                follow(PN_WO + j, EV_WO + 2 * j + 2)
            norm2(M0 + 2, lambda c: ((x2_added, c + 1), x2[:, c, :]), eps6, M0 + 1)
            for part in range(2):
                with act.Fori(0, 4) as i:
                    for f in range(4):
                        e = i * 4 + (E0 + EV_UP[part] + f + 1)
                        act.wait_ge(products_done, e)
                        act.wait_ge(relu_sq_ready, i * 4 + (16 * part + f + 3))
                        nc.scalar.activation(relu[:, f % 2, :], ps[:, f, :], ACT.Relu).then_inc(relu_ready, 1)
                        if f % 2:
                            upper(i + (N0 + PN_UP[part] + 2) // 2, f // 2, e)
                if part == 0:
                    with act.Fori(0, 4) as i:
                        for s in range(2):
                            upper(i + (N0 + PN_DN[0] + 2) // 2, s, i * 2 + (E0 + EV_DN[0] + s + 1))
                else:
                    with act.Fori(0, 3) as i:
                        for s in range(2):
                            upper(i + (N0 + PN_DN[1] + 2) // 2, s, i * 2 + (E0 + EV_DN[1] + s + 1))
            for c in range(KD):
                act.wait_ge(y_turned, c + 1)
                nc.scalar.copy(y_tok[:, :, P * c:P * (c + 1)], ps[:, c, :].rearrange("p (t n) -> p t n", t=NT2)
                               ).then_inc(y_copied, 1)

        @block.vector
        def _(dve):
            def add_squares(idx, first, end):
                for c in range(first + 1, end):
                    dve.wait_ge(sq_ready, idx * KD + (c + 1))
                    last = nc.vector.tensor_tensor(sq8[:, first, 0:T1], sq8[:, first, 0:T1], sq8[:, c, 0:T1], ALU.add)
                    if c < end - 1:
                        dve.drain()
                last.then_inc(sq_dve, 1)

            def norm(idx, src, gain, dst=None):
                dve.wait_ge(rms_ready, idx + 1)
                nc.vector.reciprocal(rstd[:, 0:NT1], rms[:, 0:NT1]).then_inc(rstd_ready, 1)
                dve.wait_ge(rows_ready, idx + 1)
                for c in range(KD):
                    if c >= 2:
                        dve.wait_ge(hn_ready, idx * KD + (c - 1))
                    nc.vector.scalar_tensor_tensor(t_chunk[:, c % 2, :], src(c), gain(c), mean_rows,
                                                   ALU.mult, ALU.mult).then_inc(t_ready, 1)

            nc.vector.memset(ones, 1.0)
            nc.vector.memset(sq, 0.0)
            nc.vector.memset(diff, 0.0)
            for x in (hn_hi, hn_lo):
                nc.vector.memset(x[:, KD * T1:].bitcast(F32), 0.0)
            dve.wait_ge(setup_in, n_setup[0])
            for l in range(DEPTH):
                for i in range(2):
                    nc.vector.tensor_tensor_reduce(out=lam_prod[:, 2 * l + i, :], in0=lam_rows[:, 2 * i, 64 * l:64 * l + 64],
                                                   in1=lam_rows[:, 2 * i + 1, 64 * l:64 * l + 64], scale=1.0, scalar=0.0,
                                                   op0=ALU.mult, op1=ALU.add, accum_out=lam_dot[:, 2 * l + i:2 * l + i + 1])
            dve.drain().then_inc(lam_dots, 1)
            for c in range(KD):
                dve.wait_ge(x_turned, c + 1)
                nc.vector.tensor_copy(h[:, c, N_META:T1], ps[:, c % 4, :]).then_inc(h_copied, 1)
            dve.wait_ge(x_turned, KD + 1)
            nc.vector.tensor_copy(h[:, :, 0:N_META],
                                  ps[:, 4, 0:N_META * KD].rearrange("p (c n) -> p c n", c=KD))
            dve.wait_ge(cols_turned, 1)
            nc.vector.tensor_copy(vec_cols, ps[:, 5, 0:103])
            nc.vector.tensor_copy(conv_cols, ps[:, 6, 0:DEPTH * TAPS * 4])
            nc.vector.tensor_copy(dn_cols, ps[:, 7, 0:P])
            dve.wait_ge(lam_exps, 1)
            e = lam_exp.rearrange("p (l i) -> p l i", i=2)
            nc.vector.tensor_tensor(neg_lam, e[:, :, 1], e[:, :, 0], ALU.subtract)
            dve.drain()
            nc.vector.tensor_tensor(neg_lam, neg_lam, lam_init, ALU.subtract)
            nc.vector.memset(sq8[:, :, T1:], 0.0)
            dve.drain().then_inc(h_ready, 1)

            with dve.Fori(0, DEPTH) as l:
                ev = l * EVENTS
                nc.vector.tensor_copy(lay, vec_cols[:, ds(l * 37, 37)])
                nc.vector.tensor_copy(lay_conv, conv_cols[:, ds(l * (TAPS * 4), TAPS * 4)])
                nc.vector.tensor_copy(lay_neg_lam, neg_lam[:, ds(l, 1)])
                nc.vector.tensor_copy(weight2[:, 0:1], lam_rest[:, ds(l, 1)])
                dve.drain()
                nc.vector.tensor_tensor(sub_gain, lay[:, VEC["sub"]:VEC["sub"] + 1], weight2[:, 0:1], ALU.mult)
                nc.vector.memset(z[:, :, 0:TAPS - 1], 0.0)
                nc.vector.memset(conv[:, 4 * T1:], 0.0)
                dve.drain()

                def chunk(c):
                    return h[:, c, :]

                add_squares(l * 2, KD // 2, KD)
                norm(l * 2, chunk, lambda c: lay[:, VEC["norm1"] + c:][:, 0:1])
                for p in range(2):
                    for j in range(4):
                        c, half = 2 * p + j // 2, j % 2
                        dve.wait_ge(products_done, ev + (EV_GLU + 8 * p + 4 + j + 1))
                        dve.wait_ge(gate_act, l * GLUS + (4 * p + j + 1))
                        at = TAPS - 1 + HALF * half
                        nc.vector.scalar_tensor_tensor(z[:, c, at:at + HALF], ps[:, 4 + j, 0:HALF],
                                                       lay[:, VEC["a_bias"] + c:][:, 0:1], glu_gate[:, j, :],
                                                       ALU.add, ALU.mult).then_inc(glu_used, 1)
                    if p == 0:
                        acc = conv[:, 0:T1]
                        dve.drain()
                        nc.vector.tensor_scalar(acc, z[:, 0, 0:T1], lay_conv[:, 0:1], lay[:, VEC["conv_b"]:][:, 0:1],
                                                ALU.mult, ALU.add)
                        for j in range(1, EARLY):
                            dve.drain()
                            nc.vector.scalar_tensor_tensor(acc, z[:, 0, j:j + T1], lay_conv[:, 4 * j:4 * j + 1], acc,
                                                           ALU.mult, ALU.add)
                dve.drain()
                for c in range(1, 4):
                    if c > 1:
                        dve.drain()
                    nc.vector.tensor_scalar(conv_acc, z[:, c, 0:T1], lay_conv[:, c:c + 1],
                                            lay[:, VEC["conv_b"] + c:][:, 0:1], ALU.mult, ALU.add)
                    for j in range(1, TAPS):
                        dve.drain()
                        last = nc.vector.scalar_tensor_tensor(
                            conv_acc if j < TAPS - 1 else conv[:, c * T1:(c + 1) * T1], z[:, c, j:j + T1],
                            lay_conv[:, 4 * j + c:4 * j + c + 1], conv_acc, ALU.mult, ALU.add)
                    last.then_inc(conv_done, 1)
                for m in range(KD):
                    c, b = m // 2 + 4 * (m % 2), 2 * (m % 3)
                    dve.wait_ge(rot_done, l * KD + (m + 1))
                    nc.vector.tensor_tensor(rope_b[:, m % 2, :].rearrange("p (b n) -> p b n", b=2), ps[:, b:b + 2, 0:HALF],
                                            sin.rearrange("p (b n) -> p b n", b=2), ALU.mult)
                    dve.drain()
                    dve.wait_ge(rope_a_ready, l * KD + (m + 1))
                    nc.vector.tensor_tensor(qk_raw[:, c, :], rope_a[:, m % 2, :], rope_b[:, m % 2, :], ALU.add
                                            ).then_inc(rope_done, 1)

                def maxima(u):
                    t = u % NT1
                    n = tok_tile(t)[1]
                    keys = min(P * (t + 1), T1)
                    s = scores_of(t)
                    dve.wait_ge(scored, l * TILES1 + (u + 1))
                    own = s[:, :, P * t:keys]
                    nc.vector.tensor_tensor(own, own, causal[0:n, 0:n].unsqueeze(1).to_broadcast([n, 2, n]), ALU.add)
                    dve.drain()
                    nc.vector.reduce_max(top[0:n, u % 2, :], s, AX.X)
                    dve.drain()
                    nc.vector.tensor_scalar(neg_top[0:n, u % 2, :], top[0:n, u % 2, :], -0.125, None,
                                            ALU.mult).then_inc(max_ready, 1)

                def difference(u):
                    t = u % NT1
                    n = tok_tile(t)[1]
                    keys = min(P * (t + 1), T1)
                    dve.wait_ge(exp_done, l * TILES1 + (u + 1))
                    nc.vector.reciprocal(weight[0:n, u % 2, :], mass[0:n, u % 2, :])
                    dve.drain()
                    nc.vector.tensor_tensor(weight2[0:n, u % 2:u % 2 + 1], weight[0:n, u % 2, 1:2],
                                            lay_neg_lam[0:n, :], ALU.mult)
                    dve.drain()
                    p2 = probs4[0:n, u % 2, 1, 0:keys]
                    nc.vector.tensor_scalar(p2, p2, weight2[0:n, u % 2:u % 2 + 1], None, ALU.mult)
                    dve.drain()
                    if u >= 2:
                        dve.wait_ge(diff_turned, l * TILES1 + (u - 1))
                    nc.vector.scalar_tensor_tensor(diff[0:n, u % 2, 0:keys], probs4[0:n, u % 2, 0, 0:keys],
                                                   weight[0:n, u % 2, 0:1], p2, ALU.mult, ALU.add
                                                   ).then_inc(diff_ready, 1)

                maxima(0)
                for u in range(TILES1):
                    if u + 1 < TILES1:
                        maxima(u + 1)
                    difference(u)
                    if u == LN_AT + 2:
                        dve.wait_ge(ln_rms, l + 1)
                        nc.vector.reciprocal(rstd[:, 20:20 + NT1], rms[:, 20:20 + NT1]).then_inc(ln_rstd, 1)
                dve.wait_ge(ln_rows, l + 1)
                for c in range(4):
                    x = conv[:, c * T1:(c + 1) * T1]
                    nc.vector.tensor_tensor(x, x, mean_rows, ALU.mult).then_inc(ln_t, 1)
                dve.wait_ge(sub_rms, l + 1)
                nc.vector.reciprocal(rstd[:, 0:4 * NT1], rms[:, 0:4 * NT1]).then_inc(sub_rstd, 1)
                for hd in range(HEADS1):
                    dve.wait_ge(sub_rows, l * 4 + (hd + 1))
                    if hd >= 2:
                        dve.wait_ge(mix_ready, l * KD + (hd - 1))
                    nc.vector.scalar_tensor_tensor(t_chunk[:, hd % 2, :], o_raw[:, hd, :], sub_gain,
                                                   line[:, 1024 * (hd % 2):1024 * (hd % 2) + T1],
                                                   ALU.mult, ALU.mult).then_inc(sub_t, 1)
                    dve.drain()
                    nc.vector.tensor_copy(hn(hn_hi, hd, 0, T1), t_chunk[:, hd % 2, :]).then_inc(mix_hi, 1)
                for c in range(4):
                    dve.wait_ge(ln_silu, l * 4 + (c + 1))
                    nc.vector.tensor_copy(hn(hn_hi, 4 + c, 0, T1), conv[:, c * T1:(c + 1) * T1]).then_inc(mix_hi, 1)
                nc.vector.memset(sq8[:, :, T1:], 0.0)
                for f in range(16):
                    dve.wait_ge(products_done, ev + (EV_OUT + f + 1))
                    x = h[:, f // 2, HALF * (f % 2):HALF * (f % 2 + 1)]
                    nc.vector.tensor_tensor(x, x, ps[:, f % 6, 0:HALF], ALU.add).then_inc(h_added, 1)
                    if f % 2 and 3 <= f < 13:
                        c = f // 2
                        dve.drain()
                        dve.wait_ge(sq_ready, (l * 2 + 1) * KD + (c + 1))
                        last = nc.vector.tensor_tensor(sq8[:, 0, 0:T1], sq8[:, 0, 0:T1], sq8[:, c, 0:T1], ALU.add)
                        if c == 5:
                            last.then_inc(sq_dve, 1)
                norm(l * 2 + 1, chunk, lambda c: lay[:, VEC["norm2"] + c:][:, 0:1])
                glu_at, ff_at = 8, 0
                for part, n in enumerate(FC):
                    with dve.Fori(0, n // 2) as i:
                        e = ev + EV_FF[part] + i * 8
                        for j in range(4):
                            oc, half = j // 2, j % 2
                            dve.wait_ge(products_done, e + (4 + j + 1))
                            dve.wait_ge(gate_act, l * GLUS + i * 4 + (glu_at + j + 1))
                            dve.wait_ge(ff_ready, l * FFS + i * 4 + (ff_at + j + 1))
                            nc.vector.tensor_tensor(glu_val[:, j, :], ps[:, 4 + j, 0:HALF], glu_gate[:, j, :],
                                                    ALU.mult).then_inc(glu_used, 1)
                            dve.drain()
                            nc.vector.tensor_copy(
                                ff_hi[:, ds(i * 2 + oc, 1), HALF * half:HALF * (half + 1)].rearrange(flat),
                                glu_val[:, j, :]).then_inc(ffv_hi, 1)
                    glu_at += 2 * n
                    ff_at += 2 * n
                    with dve.Fori(0, 2) as bb:
                        for b in range(2):
                            for j in range(4):
                                dve.wait_ge(products_done, ev + EV_DOWN[part] + bb * 10 + (5 * b + 1 + j + 1))
                                x = h[:, ds(bb * 4 + (2 * b + j // 2), 1), HALF * (j % 2):HALF * (j % 2 + 1)].rearrange(flat)
                                nc.vector.tensor_tensor(x, x, ps[:, 4 * b + j, 0:HALF], ALU.add).then_inc(h_added, 1)
                nc.vector.memset(sq8[:, :, T1:], 0.0)
                dve.drain().then_inc(h_ready, 1)
            def inverse_rms(idx):
                for c in range(KD // 2 + 1, KD):
                    dve.wait_ge(sq_ready, idx * KD + c + 1)
                    a = sq8[:, KD // 2, 0:SEQ]
                    last = nc.vector.tensor_tensor(a, a, sq8[:, c, 0:SEQ], ALU.add)
                    if c < KD - 1:
                        dve.drain()
                last.then_inc(sq_dve, 1)
                dve.wait_ge(rms_ready, idx + 1)
                nc.vector.reciprocal(rstd[:, 0:NT2], rms[:, 0:NT2]).then_inc(rstd_ready, 1)
                dve.wait_ge(rows_ready, idx + 1)

            def norm2(idx, split, gain):
                inverse_rms(idx)
                for c in range(KD):
                    if c >= 2:
                        dve.wait_ge(hn_ready, split * KD + (c - 1))
                    nc.vector.scalar_tensor_tensor(t2[:, c % 2, :], x2[:, c, :], col(gain + c), ps[:, 4, :],
                                                   ALU.mult, ALU.mult).then_inc(t_ready, 1)

            inverse_rms(M0)
            for c in range(KD):
                nc.vector.scalar_tensor_tensor(x2[:, c, :], h[:, c, N_META:T1], col(FINAL + c), ps[:, 4, :],
                                               ALU.mult, ALU.mult).then_inc(x2_ready, 1)
            dve.drain()
            norm2(M0 + 1, M0, NORM_MIX)
            dve.wait_ge(small_act, 1)
            small = ps[:, 5, 0:NT2 * 64].rearrange("p (t n) -> p t n", t=NT2)
            nc.vector.tensor_tensor(a_dt, small[:, :, DN_HEADS:2 * DN_HEADS], wide(head_rows[:, 1, :], [P, NT2, DN_HEADS], 1),
                                    ALU.add)
            dve.drain()
            flat_a = a_dt.rearrange(flat)
            nc.vector.scalar_tensor_tensor(a_abs.rearrange(flat), flat_a, -1.0, flat_a, ALU.mult, ALU.max
                                           ).then_inc(a_abs_ready, 1)
            dve.wait_ge(hn_ready, (M0 + 1) * KD)
            nc.vector.memset(taps[:, :, 0:3], 0.0).then_inc(dconv_done, 2)
            dve.wait_ge(a_ln_ready, 1)
            nc.vector.scalar_tensor_tensor(a_sp.rearrange(flat), flat_a, 0.0, a_ln.rearrange(flat), ALU.max, ALU.add)
            dve.drain()
            nc.vector.scalar_tensor_tensor(g_log, a_sp, -1.0, wide(a_exp[:, 0, :], [P, NT2, DN_HEADS], 1),
                                           ALU.mult, ALU.mult).then_inc(g_ready, 1)
            nc.vector.memset(slope4, 0.0).then_inc(silu_done, 2)
            with dve.Fori(0, PN_Z // 2) as i:
                dve.drain()
                nc.vector.tensor_copy(tap_w, dn_cols[:, 0:96].rearrange("p (j c) -> p j c", j=4)[:, :, ds(i * 4, 4)])
                for f in range(4):
                    dve.drain()
                    dve.wait_ge(qkv_copied, i * 4 + (Q0 + f + 1))
                    dve.wait_ge(silu_done, i * 4 + (f + 1))
                    acc = taps_sum[:, f % 2, :]
                    nc.vector.tensor_scalar(acc, taps[:, f % 2, 0:SEQ], tap_w[:, 0, f:f + 1], None, ALU.mult)
                    for j in range(1, 4):
                        dve.drain()
                        last = nc.vector.scalar_tensor_tensor(acc, taps[:, f % 2, j:j + SEQ], tap_w[:, j, f:f + 1], acc,
                                                              ALU.mult, ALU.add)
                    last.then_inc(dconv_done, 1)
            dve.wait_ge(gc_copied, 1)
            nc.vector.tensor_tensor(g_rest.rearrange(flat), ps[:, 5, 32:64], g_cum.rearrange(flat), ALU.subtract
                                    ).then_inc(g_rest_ready, 1)
            dve.wait_ge(l2_rms_ready, 1)
            nc.vector.reciprocal(l2_inv, l2_rms)
            dve.wait_ge(decays_ready, 1)
            dve.drain()
            for hg in range(2):
                heads = slice(HG * hg, HG * (hg + 1))
                dst = col_tab[:, NT2 * hg:NT2 * (hg + 1), :, :]
                nc.vector.tensor_scalar(dst[:, :, 0, :], l2_inv[:, heads, :].rearrange("p h t -> p t h"), P ** -0.5, None,
                                        ALU.mult)
                nc.vector.tensor_copy(dst[:, :, 1, :], l2_inv[:, DN_HEADS + HG * hg:DN_HEADS + HG * (hg + 1), :]
                                      .rearrange("p h t -> p t h"))
                nc.vector.tensor_copy(dst[:, :, 2, :], beta[:, :, heads])
                nc.vector.tensor_copy(dst[:, :, 3, :], g_cum[:, :, heads])
                nc.vector.tensor_tensor(dst[:, :, 4, :], beta[:, :, heads], g_exp[:, :, heads], ALU.mult)
                nc.vector.tensor_copy(dst[:, :, 5, :], ke_exp[:, :, heads])
            nc.vector.memset(slope4, 0.0).then_inc(do_copied, 1)
            with dve.Fori(0, 2) as hg:
                def columns_of(t):
                    nc.vector.tensor_copy(cur, col_tab[:, ds(hg * NT2 + t, 1), :, :].rearrange("p a k h -> p (a k) h")
                                          ).then_inc(cur_ready, 1)

                def normed(t):
                    for i, (dst, at, bank) in enumerate(((dk_t, DN_HEADS, 1), (dq_t, 0, 2))):
                        dve.wait_ge(drows_done, hg * (4 * NT2) + (4 * t + i + 1))
                        nc.vector.tensor_tensor(dst, qkv[:, ds(hg * HG + at, HG), tile(t)], by_head(bank), ALU.mult)

                def scaled(t):
                    dve.drain()
                    dve.wait_ge(drows_done, hg * (4 * NT2) + (4 * t + 3))
                    nc.vector.tensor_tensor(dkb_t, dk_t, by_head(3), ALU.mult).then_inc(dk_ready, 1)
                    dve.wait_ge(drows_done, hg * (4 * NT2) + (4 * t + 4))
                    for hh in range(HG):
                        last = nc.vector.scalar_tensor_tensor(decay[:, hh, :], ps[:, 0, tile(hh)], cur[:, 3, hh:hh + 1],
                                                              decay_mask, ALU.subtract, ALU.add)
                    last.then_inc(dec_ready, 1)

                dve.drain()
                nc.vector.memset(state, 0.0)
                columns_of(0)
                normed(0)
                scaled(0)
                for t in range(NT2):
                    it = hg * NT2 + t
                    dve.drain()
                    dve.wait_ge(dexp_done, it + 1)
                    dve.wait_ge(dkk_done, it + 1)
                    nc.vector.tensor_tensor(da_t, by_head(6), decay, ALU.mult).then_inc(da_ready, 1)
                    eye = wide(ident, [P, 2, P], 1)
                    aside = [(dqk_t, by_head(7), decay), (dkbg, by_head(4), wide(cur[:, 4, :], [P, HG, P], 2)),
                             (dke, by_head(4), wide(cur[:, 5, :], [P, HG, P], 2)),
                             (dvb, by_head(5), wide(cur[:, 2, :], [P, HG, P], 2))]
                    for n in range(LEVELS):
                        mask = wide(levels[:, P * n:P * (n + 1)], [P, 2, P], 1)
                        for pair in range(2):
                            heads = slice(2 * pair, 2 * pair + 2)
                            dve.wait_ge(p1_done, it * (2 * LEVELS) + (2 * n + 1 + pair))
                            nc.vector.tensor_tensor(dp[:, heads, :], by_head(pair)[:, 0:2, :], mask, ALU.mult
                                                    ).then_inc(dp_ready, 1)
                        if n == 0:
                            dve.drain()
                            nc.vector.tensor_tensor(dx, wide(ident, [P, HG, P], 1), dp, ALU.subtract)
                        elif n <= len(aside):
                            dst, a, b = aside[n - 1]
                            nc.vector.tensor_tensor(dst, a, b, ALU.mult)
                        for pair in range(2):
                            heads = slice(2 * pair, 2 * pair + 2)
                            dve.wait_ge(delta_done, it * (2 * LEVELS) + (2 * n + 1 + pair))
                            if 0 < n < LEVELS - 1:
                                nc.vector.tensor_tensor(dx[:, heads, :], dx[:, heads, :], by_head(2 + pair)[:, 0:2, :],
                                                        ALU.subtract)
                            nc.vector.tensor_tensor(dx_t[:, heads, :], dx_t[:, heads, :] if n else eye,
                                                    by_head(2 + pair)[:, 2:4, :], ALU.subtract).then_inc(dx_ready, 1)
                        dve.drain()
                    if t + 1 < NT2:
                        columns_of(t + 1)
                        dve.wait_ge(dqd_ready, it + 1)
                        normed(t + 1)
                    for ch in range(2):
                        dve.drain()
                        dve.wait_ge(s_done, it * 2 + (ch + 1))
                        for hh in range(HG):
                            c = CHUNK * (ch + 1) - 1
                            last = nc.vector.scalar_tensor_tensor(state[:, hh, :], state[:, hh, :],
                                                                  g_rows[t % 2][:, hh, c:c + 1],
                                                                  ps[:, 7, tile(hh)], ALU.mult, ALU.add)
                        last.then_inc(state_ready, 1)
                        if ch == 0 and t + 1 < NT2:
                            scaled(t + 1)
                    nc.vector.tensor_copy(qkv[:, ds(hg * HG + 16, HG), tile(t)], by_head(6)).then_inc(do_copied, 1)
            dve.wait_ge(odn_rms, 1)
            nc.vector.reciprocal(rstd, rms).then_inc(odn_rstd, 1)
            for c in range(DN_HEADS):
                o = qkv[:, 16 + c, :]
                dve.wait_ge(odn_rows, c + 1)
                nc.vector.scalar_tensor_tensor(o, o, col(DN_OUT), ps[:, 6 + c % 2, :], ALU.mult, ALU.mult
                                               ).then_inc(odn_normed, 1)
                dve.drain()
                dve.wait_ge(z_copied, c + 1)
                nc.vector.tensor_tensor(o, o, z_act[:, c % 2, :], ALU.mult).then_inc(odn_ready, 1)
            nc.vector.tensor_scalar(q_gain, col(QN), HD ** -0.5, None, ALU.mult)
            dve.wait_ge(n_rms_ready, 1)
            nc.vector.reciprocal(n_rstd[:, 0:96], n_rms[:, 0:96]).then_inc(n_rstd_ready, 1)
            dve.drain()
            for m in range(12):
                dve.wait_ge(n_rows, m + 1)
                rows = ps[:, 4 + m % 2, :]
                if m < KD:
                    last = nc.vector.scalar_tensor_tensor(nq[:, m, :], nq[:, m, :], q_gain, rows, ALU.mult, ALU.mult)
                else:
                    dst, gain = ((ks2, KS_N), (kw2, KW_N))[(m - KD) // 2]
                    for i in range(2):
                        own = slice(HD * i, HD * (i + 1))
                        for half in range(2):
                            last = nc.vector.scalar_tensor_tensor(
                                dst[HD * half:HD * (half + 1), (m - KD) % 2 * 2 + i, :], k_raw[own, m - KD, :],
                                col(gain)[own, :], rows[own, :], ALU.mult, ALU.mult)
                last.then_inc(n_scaled, 1)
            dve.drain()
            nc.vector.memset(c_gelu[:, GROUPS * N_CMP:], 0.0).then_inc(c_pad_ready, 1)
            dve.wait_ge(kc_rms, 1)
            nc.vector.reciprocal(n_rstd[:, 96:97], n_rms[:, 96:97]).then_inc(kc_rstd, 1)
            dve.wait_ge(kc_rows, 1)
            nc.vector.scalar_tensor_tensor(kc2, kc_raw, col(KC_N), ps[:, 5, 0:P], ALU.mult, ALU.mult).then_inc(kc_ready, 1)
            dve.drain()
            dve.wait_ge(vc_ready, 1)
            nc.vector.memset(pc_t, 0.0)
            nc.vector.memset(p_cmp[0][:, :, N_CMP:], 0.0)
            dve.wait_ge(w_split, N0 + PN_MDN + 4)
            nc.vector.memset(p_cmp[1][:, :, N_CMP:], 0.0).then_inc(pv2_done, 1)
            with dve.Fori(0, GROUPS) as g:
                dve.drain()
                nc.vector.tensor_copy(slope4, neg_slope[:, ds(g * REP, REP)])
                dve.drain()

                def parts(t):
                    slot = t % 2
                    return ((p_slc[slot], P * (t + 1)), (p_win[slot], P * min(t + 1, 3)), (p_cmp[slot], N_CMP))

                def maxima(t):
                    (slc, w_slc), (win, w_win), (cmp, _) = parts(t)
                    for r in range(REP):
                        dve.wait_ge(slc_scored, g * (REP * NT2) + (REP * t + r + 1))
                        nc.vector.scalar_tensor_tensor(slc[:, r, 0:w_slc], dist[:, SEQ - w_slc:], slope4[:, r:r + 1],
                                                       ps[:, r, 0:w_slc], ALU.mult, ALU.add).then_inc(slc_read, 1)
                    dve.drain()
                    nc.vector.reduce_max(s_top[:, 0, :], slc[:, :, 0:w_slc], AX.X)
                    dve.drain()
                    nc.vector.tensor_scalar(s_neg[:, 0, :], s_top[:, 0, :], -1.0, None, ALU.mult).then_inc(tops_ready, 1)
                    for r in range(REP):
                        dve.wait_ge(win_scored, g * (REP * NT2) + (REP * t + r + 1))
                        nc.vector.scalar_tensor_tensor(win[:, r, 0:w_win], dist_win[:, SEQ - P - w_win:], slope4[:, r:r + 1],
                                                       ps[:, r, 0:w_win], ALU.mult, ALU.add)
                        nc.vector.scalar_tensor_tensor(cmp[:, r, 0:N_CMP], dist_cmp[:, N_CMP * t:N_CMP * (t + 1)],
                                                       slope4[:, r:r + 1], ps[:, r, SEQ - P:SEQ - P + N_CMP],
                                                       ALU.mult, ALU.add)
                    dve.drain()
                    nc.vector.reduce_max(s_top[:, 1, :], win[:, :, 0:w_win], AX.X)
                    nc.vector.reduce_max(s_top[:, 2, :], cmp[:, :, 0:N_CMP], AX.X)
                    dve.drain()
                    nc.vector.tensor_scalar(s_neg[:, 1:3, :], s_top[:, 1:3, :], -1.0, None, ALU.mult).then_inc(tops_ready, 1)

                def weigh(t):
                    for part, ids in enumerate(((0,), (1, 2))):
                        own = slice(ids[0], ids[-1] + 1)
                        dve.wait_ge(exps_done, g * (2 * NT2) + (2 * t + part + 1))
                        nc.vector.reciprocal(s_weight[:, own, :], s_mass[:, own, :])
                        dve.drain()
                        g3 = gates[:, t, ds(g * (3 * REP), 3 * REP)].rearrange("p (r i) -> p i r", i=3)
                        for i in ids:
                            nc.vector.tensor_tensor(s_weight[:, i, :], s_weight[:, i, :], g3[:, (1, 2, 0)[i], :], ALU.mult)
                        dve.drain()
                        if t == 0 and part == 1:
                            nc.vector.tensor_scalar(s_weight[:, 2, :], s_weight[:, 2, :], valid[:, 0:1], None, ALU.mult)
                            dve.drain()
                        for i in ids:
                            p, w = parts(t)[i]
                            if i == 2:
                                nc.vector.tensor_tensor(p[:, :, 0:w], p[:, :, 0:w], wide(s_weight[:, i, :], [P, REP, w], 2),
                                                        ALU.mult)
                            else:
                                for r in range(REP):
                                    nc.vector.tensor_scalar(p[:, r, 0:w], p[:, r, 0:w], s_weight[:, i, r:r + 1], None, ALU.mult)
                        dve.drain().then_inc(p_ready, 1)

                maxima(0)
                for t in range(NT2):
                    weigh(t)
                    if t + 1 < NT2:
                        maxima(t + 1)
                    dve.wait_ge(pv2_done, g * BLOCKS_G + (sum(BLOCKS[:t + 1]) + 1))
                    o = ps[0:HD, 6, :].rearrange("p (a b n) -> p a b n", b=2, n=P)
                    for b in range(2):
                        nc.vector.tensor_scalar(nq[HD * b:HD * (b + 1), ds(g * 2, 2), tile(t)], o[:, :, b, :], 1.0, None,
                                                ALU.mult)
                    dve.drain().then_inc(att_copied, 1)
            for m in range(2):
                for j in range(4):
                    for oc in range(2):
                        n = 8 * m + 2 * j + oc
                        dve.wait_ge(products_done, E0 + EV_MDN + 16 * m + 4 * j + 2 + oc + 1)
                        dve.wait_ge(sig_ready, n + 1)
                        proj = ps[:, 4 * (j % 2) + 2 + oc, :]
                        dst = merged[:, 2 * j + oc, :]
                        if m == 0:
                            nc.vector.tensor_tensor(dst, sig[:, oc, :], proj, ALU.mult).then_inc(merged_part, 1)
                        else:
                            nc.vector.tensor_tensor(sig[:, oc, :], sig[:, oc, :], proj, ALU.mult)
                            dve.drain()
                            nc.vector.tensor_tensor(dst, dst, sig[:, oc, :], ALU.add).then_inc(merged_part, 1)
                dve.drain()
            for f in range(KD):
                dve.wait_ge(products_done, E0 + EV_WO + f + 1)
                nc.vector.tensor_tensor(x2[:, f, :], x2[:, f, :], ps[:, f, :], ALU.add).then_inc(x2_added, 1)
            dve.drain()
            norm2(M0 + 2, M0 + 1, NORM_MLP)
            nc.vector.memset(slope4, 0.0).then_inc(relu_sq_ready, 4)
            for part in range(2):
                with dve.Fori(0, 4) as i:
                    for f in range(4):
                        dve.wait_ge(relu_ready, i * 4 + (16 * part + f + 1))
                        dve.wait_ge(f_ready, i * 4 + (16 * part + f + 1))
                        if part:
                            dve.wait_ge(products_done, E0 + EV_DN[0] + 8)
                        u = relu_sq[:, f % 2, :]
                        nc.vector.scalar_tensor_tensor(u, ps[:, f, :], 0.0, relu[:, f % 2, :], ALU.max, ALU.mult
                                                       ).then_inc(relu_sq_ready, 1)
                        dve.drain()
                        nc.vector.tensor_copy(f_hi[:, ds(i * 4 + f, 1), :].rearrange(flat), u).then_inc(f_hi_ready, 1)
                dve.wait_ge(products_done, E0 + EV_DN[part] + 8)
                for c in range(KD):
                    nc.vector.tensor_tensor(x2[:, c, :], x2[:, c, :], ps[:, c, :], ALU.add).then_inc(x2_added, 1)
                dve.drain()

        @block.gpsimd
        def _(pool):
            def lower(n, slot):
                pool.wait_ge(w_hi, n + 1)
                nc.gpsimd.tensor_tensor(wlo[:, slot, :], wraw[:, slot, :], whi[:, slot, :].bitcast(F32),
                                        ALU.subtract).then_inc(w_split, 1)

            def add_squares(idx, n):
                for c in range(1, KD // 2):
                    pool.wait_ge(sq_ready, idx * KD + (c + 1))
                    last = nc.gpsimd.tensor_tensor(sq8[:, 0, 0:n], sq8[:, 0, 0:n], sq8[:, c, 0:n], ALU.add)
                    if c < KD // 2 - 1:
                        pool.drain()
                last.then_inc(sq_pool, 1)

            def norm(idx):
                for c in range(KD):
                    pool.wait_ge(hi_ready, idx * KD + (c + 1))
                    nc.gpsimd.tensor_tensor(hn(hn_lo, c, 0, T1), t_chunk[:, c % 2, :],
                                            hn(hn_hi, c, 0, T1).bitcast(F32), ALU.subtract).then_inc(hn_ready, 1)

            nc.gpsimd.memset(top, 0.0).then_inc(w_split, 2)
            nc.gpsimd.memset(neg_top, 0.0).then_inc(ff_ready, 4)
            for s in range(2):
                lower(s, s)
            with pool.Fori(0, DEPTH) as l:
                first = l * PANELS_L
                add_squares(l * 2, T1)
                norm(l * 2)
                acc = conv[:, 0:T1]
                for j in range(10):
                    if j == 2:
                        pool.wait_ge(glu_used, l * GLUS + 5)
                    lower(first + (j + 2), j % 2)
                    if 2 <= j < 2 + GROUPS1:
                        pool.wait_ge(taps_ready, l * GROUPS1 + (j - 1))
                        for i in range(GROUP):
                            last = nc.gpsimd.tensor_tensor(acc, acc, tap_prod[:, i, :], ALU.add)
                            if i < GROUP - 1:
                                pool.drain()
                        last.then_inc(taps_added, 1)
                pool.wait_ge(qkv_copied, l * 26 + 26)
                for m in range(KD):
                    if m >= 2:
                        pool.wait_ge(rope_done, l * KD + (m - 1))
                    nc.gpsimd.tensor_tensor(rope_a[:, m % 2, :], qk_raw[:, m // 2 + 4 * (m % 2), :], cos, ALU.mult
                                            ).then_inc(rope_a_ready, 1)
                pool.wait_ge(ln_mean_copied, l + 1)
                chunks = [conv[:, c * T1:(c + 1) * T1] for c in range(4)]
                for x in chunks:
                    nc.gpsimd.tensor_tensor(x, x, mean_sb, ALU.subtract)
                pool.drain()
                total, part = sq[:, 0, 0:T1], sq[:, 1, 0:T1]
                nc.gpsimd.tensor_tensor(total, chunks[0], chunks[0], ALU.mult)
                for x in chunks[1:]:
                    nc.gpsimd.tensor_tensor(part, x, x, ALU.mult)
                    pool.drain()
                    last = nc.gpsimd.tensor_tensor(total, total, part, ALU.add)
                    pool.drain()
                last.then_inc(ln_sq, 1)
                for c in range(4):
                    pool.wait_ge(mix_hi, l * KD + (c + 1))
                    nc.gpsimd.tensor_tensor(hn(hn_lo, c, 0, T1), t_chunk[:, c % 2, :],
                                            hn(hn_hi, c, 0, T1).bitcast(F32), ALU.subtract).then_inc(mix_ready, 1)
                for c in range(4):
                    pool.wait_ge(mix_hi, l * KD + (4 + c + 1))
                    nc.gpsimd.tensor_tensor(hn(hn_lo, 4 + c, 0, T1), conv[:, c * T1:(c + 1) * T1],
                                            hn(hn_hi, 4 + c, 0, T1).bitcast(F32), ALU.subtract).then_inc(mix_ready, 1)
                for j in range(10, 14):
                    lower(first + (j + 2), j % 2)
                norm(l * 2 + 1)
                at, ff_at = 14, 0
                for part, n in enumerate(FC):
                    with pool.Fori(0, n // 2) as i:
                        lower(first + i * 2 + (at + 2), 0)
                        for j in range(4):
                            oc, half = j // 2, j % 2
                            pool.wait_ge(ffv_hi, l * FFS + i * 4 + (ff_at + j + 1))
                            a = HALF * half
                            nc.gpsimd.tensor_tensor(
                                ff_lo[:, ds(i * 2 + oc, 1), a:a + HALF].rearrange(flat), glu_val[:, j, :],
                                ff_hi[:, ds(i * 2 + oc, 1), a:a + HALF].rearrange(flat).bitcast(F32),
                                ALU.subtract).then_inc(ff_ready, 1)
                        lower(first + i * 2 + (at + 3), 1)
                    at += n
                    ff_at += 2 * n
                    with pool.Fori(0, 4) as b:
                        for s in range(2):
                            lower(first + b * 2 + (at + 2 + s), s)
                    at += 8
            def norm2(split):
                for c in range(KD):
                    pool.wait_ge(hi_ready, split * KD + (c + 1))
                    nc.gpsimd.tensor_tensor(hx(hn_lo, c, 0, SEQ), t2[:, c % 2, :], hx(hn_hi, c, 0, SEQ).bitcast(F32),
                                            ALU.subtract).then_inc(hn_ready, 1)

            add_squares(M0, SEQ)
            pool.wait_ge(ws_hi_ready, 1)
            nc.gpsimd.tensor_tensor(ws_lo, w_small.rearrange(flat), ws_hi.bitcast(F32), ALU.subtract).then_inc(ws_ready, 1)
            add_squares(M0 + 1, SEQ)
            norm2(M0)
            with pool.Fori(0, PN_Z // 2) as i:
                for s in range(2):
                    lower(i * 2 + (N0 + 2 + s), s)
            with pool.Fori(0, 2) as hg:
                for t in range(NT2):
                    pool.wait_ge(dexp_done, hg * NT2 + (t + 1))
                    pool.wait_ge(do_copied, hg * NT2 + (t + 1))
                    nc.gpsimd.tensor_tensor(dqd_t, dq_t, g_rows[t % 2], ALU.mult).then_inc(dqd_ready, 1)
            for pn in range(PN_Z, PN_NQ):
                lower(N0 + pn + 2, pn % 2)
            for pn in range(PN_NQ, PN_MDN):
                lower(N0 + pn + 2, pn % 2)
            pool.wait_ge(vc_ready, 1)
            pool.wait_ge(kc_ready, 1)
            with pool.Fori(0, GROUPS) as g:
                nc.gpsimd.tensor_copy(q_grp, nq[:, ds(g * 2, 2), :])
                for i, k in enumerate((ks2, kw2)):
                    nc.gpsimd.tensor_copy(k_grp[:, i, :], k[:, ds(g, 1), :].rearrange(flat))
                nc.gpsimd.tensor_copy(kc_grp, kc2[:, ds(g * N_CMP, N_CMP)])
                pool.drain().then_inc(kg_ready, 1)
                pool.wait_ge(pv2_done, g * BLOCKS_G + 1)
                for i, v in enumerate((vs, vw)):
                    nc.gpsimd.tensor_copy(v_grp[:, i, :, :], v[:, :, ds(g * HD, HD)])
                nc.gpsimd.tensor_copy(vc_grp, vc[:, ds(g, 1), :].rearrange(flat))
                pool.drain().then_inc(vg_ready, 1)
                pool.wait_ge(win_scored, g * (REP * NT2) + REP * NT2)
            def split_out(src, first):
                for c in range(KD):
                    pool.wait_ge(o_hi_ready, first + c + 1)
                    nc.gpsimd.tensor_tensor(o_lo[:, c, :], src(c), o_hi[:, c, :].bitcast(F32), ALU.subtract
                                            ).then_inc(o_ready, 1)

            split_out(lambda c: qkv[:, 16 + c, :], 0)
            for m, pn in enumerate((PN_MDN, PN_MNS)):
                for j in range(8):
                    lower(N0 + pn + j + 2, j % 2)
                if m == 0:
                    split_out(lambda c: nq[:, c, :], KD)
            for c in range(KD):
                pool.wait_ge(merged_hi, c + 1)
                nc.gpsimd.tensor_tensor(hx(hn_lo, c, 0, SEQ), merged[:, c, :], hx(hn_hi, c, 0, SEQ).bitcast(F32),
                                        ALU.subtract).then_inc(merged_ready, 1)
            for j in range(4):
                lower(N0 + PN_WO + j + 2, j % 2)
            add_squares(M0 + 2, SEQ)
            norm2(M0 + 1)
            nc.gpsimd.memset(top, 0.0).then_inc(f_ready, 2)
            for part in range(2):
                with pool.Fori(0, 4) as i:
                    for f in range(4):
                        pool.wait_ge(f_hi_ready, i * 4 + (16 * part + f + 1))
                        nc.gpsimd.tensor_tensor(f_lo[:, ds(i * 4 + f, 1), :].rearrange(flat), relu_sq[:, f % 2, :],
                                                f_hi[:, ds(i * 4 + f, 1), :].rearrange(flat).bitcast(F32), ALU.subtract
                                                ).then_inc(f_ready, 1)
                        if f % 2:
                            lower(i * 2 + (N0 + PN_UP[part] + 2 + f // 2), f // 2)
                with pool.Fori(0, 4 - part) as i:
                    for s in range(2):
                        lower(i * 2 + (N0 + PN_DN[part] + 2 + s), s)


_INS = ["x", "meta_tokens", "norm1_g", "w_in", "b_glu", "conv_w", "conv_b", "conv_ln_g", "conv_ln_b", "lam_q1",
        "lam_k1", "lam_q2", "lam_k2", "subln_g", "w_out", "norm2_g", "w_gate_up", "w_down", "final_g", "norm_mix_2",
        "w_in_2", "dn_conv_2", "dn_a_log_2", "dn_dt_bias_2", "dn_out_norm_2", "nsa_q_norm_2", "nsa_k_norm_cmp_2",
        "nsa_k_norm_slc_2", "nsa_k_norm_win_2", "cmp_pos_k_2", "cmp_w1_k_2", "cmp_w2_k_2", "cmp_pos_v_2",
        "cmp_w1_v_2", "cmp_w2_v_2", "w_proj_dn_2", "w_proj_nsa_2", "w_out_2", "norm_mlp_2", "w_up_2", "w_down_2"]


def kernel(**inputs):
    import concourse.bacc as bacc
    from concourse.bass_utils import run_bass_kernel_spmd

    nc = bacc.Bacc("TRN2", target_bir_lowering=False, num_devices=1)
    arrays = {f"in_{n}": np.ascontiguousarray(inputs[n]) for n in _INS}
    arrays["table1"] = packed(first_constants())
    arrays["table2"] = packed(second_constants())
    aps = {n: nc.dram_tensor(n, a.shape, mybir.dt.from_np(a.dtype), kind="ExternalInput").ap()
           for n, a in arrays.items()}
    out = nc.dram_tensor("out", (1, SEQ, D), F32, kind="ExternalOutput").ap()
    hybrid_blocks(nc, {n: aps[f"in_{n}"] for n in _INS}, aps["table1"], aps["table2"], out)
    r = run_bass_kernel_spmd(nc, [arrays], core_ids=[0])
    return r.results[0]["out"]
```
